# Optimizing a Trainium2 kernel written in Bass

```python
import math
import jax, jax.numpy as jnp
from jax import lax
import numpy as np

D_MODEL = 1024
BATCH = 1
SEQ = 1024
DEPTH = 1
DEC_BATCH = 8
DEC_SEQ = 1
PAST_LEN = 8192
PAGE_SIZE = 128

N_MEM = 256
POOL_WIDTH = D_MODEL // 2
POOL_WINDOWS = (2, 4, 8, 16)
N_POOL_GROUPS = len(POOL_WINDOWS)
POOL_GROUP = POOL_WIDTH // N_POOL_GROUPS
POOL_BUF = max(POOL_WINDOWS) - 1
MLSTM_HEADS = 4
MLSTM_WIDTH = D_MODEL
MLSTM_DH = MLSTM_WIDTH // MLSTM_HEADS
MLSTM_CHUNK = 64
XATTN_HEADS = 4
XATTN_WIDTH = D_MODEL // 2
XATTN_DH = XATTN_WIDTH // XATTN_HEADS
N_BRANCH = 3
D_FF = 4 * D_MODEL
N_IN = POOL_WIDTH + 4 * MLSTM_WIDTH + 2 * MLSTM_HEADS + XATTN_WIDTH + N_BRANCH * D_MODEL
EPS = 1e-6
NEG_INF = -1e30

kernel_name = 'hybrid_pool_mlstm_memxattn_decode_step'

def rmsnorm(x, g):
    xf = x.astype(jnp.float32)
    y = xf * lax.rsqrt(jnp.mean(xf * xf, axis=-1, keepdims=True) + EPS)
    return (y * g.astype(jnp.float32)).astype(x.dtype)

def pool_mix(u, buf, pos0, w_pool, pool_scale):
    B, T, P = u.shape
    z = jnp.concatenate([buf.astype(jnp.float32), u.astype(jnp.float32)], axis=1)
    cs = jnp.concatenate([jnp.zeros((B, 1, P), jnp.float32), jnp.cumsum(z, axis=1)], axis=1)
    t = jnp.arange(T)
    means = []
    for g, w in enumerate(POOL_WINDOWS):
        sl = slice(g * POOL_GROUP, (g + 1) * POOL_GROUP)
        hi = cs[:, POOL_BUF + 1:POOL_BUF + 1 + T, sl]
        lo = cs[:, POOL_BUF + 1 - w:POOL_BUF + 1 - w + T, sl]
        cnt = jnp.minimum(w, pos0 + t + 1).astype(jnp.float32)
        means.append((hi - lo) / cnt[None, :, None])
    d = (jnp.concatenate(means, axis=-1) - u.astype(jnp.float32)).astype(u.dtype)
    d = d.reshape(B, T, N_POOL_GROUPS, POOL_GROUP)
    y = jnp.einsum('btgc,gcd->btgd', d, w_pool).reshape(B, T, P) * pool_scale
    new_buf = z[:, -POOL_BUF:].astype(buf.dtype)
    return y, new_buf

def mlstm_chunkwise(q, k, v, ig, lf, C0, n0, m0):
    B, T, H, Dh = q.shape
    L = MLSTM_CHUNK if T % MLSTM_CHUNK == 0 else T
    nc = T // L

    def chunks(a):
        return jnp.moveaxis(a.reshape((B, nc, L) + a.shape[2:]), 1, 0)

    causal = jnp.tril(jnp.ones((L, L), dtype=bool))

    def step(carry, inp):
        C, n, m = carry
        qc, kc, vc, ic, fc = inp
        b = jnp.cumsum(fc, axis=1).transpose(0, 2, 1)
        ic = ic.transpose(0, 2, 1)
        logw = b[..., :, None] - b[..., None, :] + ic[..., None, :]
        logw = jnp.where(causal, logw, NEG_INF)
        log_inter = b + m[..., None]
        m_t = jnp.maximum(log_inter, jnp.max(logw, axis=-1))
        w_intra = jnp.exp(logw - m_t[..., None])
        w_inter = jnp.exp(log_inter - m_t)
        s = jnp.einsum('blhd,bshd->bhls', qc, kc) * w_intra
        num = jnp.einsum('bhls,bshd->bhld', s, vc) + w_inter[..., None] * jnp.einsum('bhvk,blhk->bhlv', C, qc)
        den = jnp.sum(s, axis=-1) + w_inter * jnp.einsum('bhk,blhk->bhl', n, qc)
        h = num / jnp.maximum(jnp.abs(den), jnp.exp(-m_t))[..., None]
        m_new = m_t[..., -1]
        decay = jnp.exp(b[..., -1] + m - m_new)
        w_end = jnp.exp(b[..., -1:] - b + ic - m_new[..., None])
        C_new = decay[..., None, None] * C + jnp.einsum('bhs,bshv,bshk->bhvk', w_end, vc, kc)
        n_new = decay[..., None] * n + jnp.einsum('bhs,bshk->bhk', w_end, kc)
        return (C_new, n_new, m_new), h.transpose(0, 2, 1, 3)

    xs = (chunks(q), chunks(k), chunks(v), chunks(ig), chunks(lf))
    (C, n, m), hs = lax.scan(step, (C0, n0, m0), xs)
    h = jnp.moveaxis(hs, 0, 1).reshape(B, T, H, Dh)
    return h, C, n, m

def memory_kv(mem, g_mem, w_mem_kv):
    B, M, _ = mem.shape
    kv = rmsnorm(mem, g_mem) @ w_mem_kv
    k = kv[..., :XATTN_WIDTH].reshape(B, M, XATTN_HEADS, XATTN_DH)
    v = kv[..., XATTN_WIDTH:].reshape(B, M, XATTN_HEADS, XATTN_DH)
    return k, v

def memory_attention(qx, mk, mv):
    s = jnp.einsum('bthd,bmhd->bhtm', qx, mk).astype(jnp.float32) * (XATTN_DH ** -0.5)
    p = jax.nn.softmax(s, axis=-1).astype(mv.dtype)
    return jnp.einsum('bhtm,bmhd->bthd', p, mv)

def layer_forward(x, pool_buf, C0, n0, m0, mk, mv, pos0, g_pre_mix, w_in, b_if, w_pool, pool_scale,
                  w_br_pool, w_br_mlstm, w_br_xattn, w_out, g_post_mix, g_pre_mlp, w_ff1, w_ff2, g_post_mlp):
    B, T, _ = x.shape
    h = rmsnorm(x, g_pre_mix)
    proj = h @ w_in
    o0 = POOL_WIDTH
    o1 = o0 + 4 * MLSTM_WIDTH
    o2 = o1 + 2 * MLSTM_HEADS
    o3 = o2 + XATTN_WIDTH
    u = proj[..., :o0]
    qkvo = proj[..., o0:o1].reshape(B, T, 4, MLSTM_HEADS, MLSTM_DH)
    gif = proj[..., o1:o2].astype(jnp.float32) + b_if.astype(jnp.float32)
    xq = proj[..., o2:o3].reshape(B, T, XATTN_HEADS, XATTN_DH)
    gates = jax.nn.sigmoid(proj[..., o3:].reshape(B, T, N_BRANCH, D_MODEL))

    y_pool, new_buf = pool_mix(u, pool_buf, pos0, w_pool, pool_scale)

    q = qkvo[:, :, 0].astype(jnp.float32)
    k = qkvo[:, :, 1].astype(jnp.float32) * (MLSTM_DH ** -0.5)
    v = qkvo[:, :, 2].astype(jnp.float32)
    o_gate = jax.nn.sigmoid(qkvo[:, :, 3].astype(jnp.float32))
    ig = gif[..., :MLSTM_HEADS]
    lf = jax.nn.log_sigmoid(gif[..., MLSTM_HEADS:])
    hm, C, n, m = mlstm_chunkwise(q, k, v, ig, lf, C0.astype(jnp.float32), n0.astype(jnp.float32),
                                  m0.astype(jnp.float32))
    y_mlstm = (o_gate * hm).reshape(B, T, MLSTM_WIDTH).astype(x.dtype)

    y_x = memory_attention(xq, mk, mv).reshape(B, T, XATTN_WIDTH)

    merged = (gates[:, :, 0] * (y_pool @ w_br_pool) + gates[:, :, 1] * (y_mlstm @ w_br_mlstm)
              + gates[:, :, 2] * (y_x @ w_br_xattn))
    x = x + rmsnorm(merged @ w_out, g_post_mix)

    h2 = rmsnorm(x, g_pre_mlp)
    f = jnp.square(jax.nn.relu(h2 @ w_ff1)) @ w_ff2
    x = x + rmsnorm(f, g_post_mlp)
    return x, new_buf, C.astype(C0.dtype), n.astype(n0.dtype), m.astype(m0.dtype)

def setup_inputs(seed: int = 0) -> dict:
    key = jax.random.key(seed)
    ks = jax.random.split(key, 32)
    f32 = jnp.float32

    def nrm(k, shape, scale):
        return jax.random.normal(k, shape, f32) * scale

    def gain(k, shape):
        return 1.0 + 0.05 * jax.random.normal(k, shape, f32)

    ig_bias = nrm(ks[14], (DEPTH, MLSTM_HEADS), 0.1)
    fg_bias = 3.0 + jnp.linspace(0.0, 3.0, MLSTM_HEADS, dtype=f32)[None, :] + nrm(ks[15], (DEPTH, MLSTM_HEADS), 0.1)
    return {
        'x_prompt': nrm(ks[0], (BATCH, SEQ, D_MODEL), 1.0),
        'x_sample': nrm(ks[1], (DEC_BATCH, DEC_SEQ, D_MODEL), 1.0),
        'mem_prompt': nrm(ks[2], (BATCH, N_MEM, D_MODEL), 1.0),
        'state_pool_buf': nrm(ks[3], (DEPTH, DEC_BATCH, POOL_BUF, POOL_WIDTH), 1.0),
        'state_mlstm_C': nrm(ks[4], (DEPTH, DEC_BATCH, MLSTM_HEADS, MLSTM_DH, MLSTM_DH), 0.1),
        'state_mlstm_n': nrm(ks[5], (DEPTH, DEC_BATCH, MLSTM_HEADS, MLSTM_DH), 0.1),
        'state_mlstm_m': nrm(ks[6], (DEPTH, DEC_BATCH, MLSTM_HEADS), 0.5),
        'cache_mem_k': nrm(ks[7], (DEPTH, DEC_BATCH, N_MEM, XATTN_HEADS, XATTN_DH), 1.0),
        'cache_mem_v': nrm(ks[8], (DEPTH, DEC_BATCH, N_MEM, XATTN_HEADS, XATTN_DH), 1.0),
        'g_pre_mix': gain(ks[9], (DEPTH, D_MODEL)),
        'w_in': nrm(ks[10], (DEPTH, D_MODEL, N_IN), D_MODEL ** -0.5),
        'b_if': jnp.concatenate([ig_bias, fg_bias], axis=-1),
        'w_pool': nrm(ks[11], (DEPTH, N_POOL_GROUPS, POOL_GROUP, POOL_GROUP), POOL_GROUP ** -0.5),
        'pool_scale': gain(ks[12], (DEPTH, POOL_WIDTH)),
        'g_mem': gain(ks[13], (DEPTH, D_MODEL)),
        'w_mem_kv': nrm(ks[16], (DEPTH, D_MODEL, 2 * XATTN_WIDTH), D_MODEL ** -0.5),
        'w_br_pool': nrm(ks[17], (DEPTH, POOL_WIDTH, D_MODEL), POOL_WIDTH ** -0.5),
        'w_br_mlstm': nrm(ks[18], (DEPTH, MLSTM_WIDTH, D_MODEL), MLSTM_WIDTH ** -0.5),
        'w_br_xattn': nrm(ks[19], (DEPTH, XATTN_WIDTH, D_MODEL), XATTN_WIDTH ** -0.5),
        'w_out': nrm(ks[20], (DEPTH, D_MODEL, D_MODEL), D_MODEL ** -0.5),
        'g_post_mix': gain(ks[21], (DEPTH, D_MODEL)),
        'g_pre_mlp': gain(ks[22], (DEPTH, D_MODEL)),
        'w_ff1': nrm(ks[23], (DEPTH, D_MODEL, D_FF), D_MODEL ** -0.5),
        'w_ff2': nrm(ks[24], (DEPTH, D_FF, D_MODEL), D_FF ** -0.5),
        'g_post_mlp': gain(ks[25], (DEPTH, D_MODEL)),
    }

def reference(x_prompt, x_sample, mem_prompt, state_pool_buf, state_mlstm_C, state_mlstm_n, state_mlstm_m,
              cache_mem_k, cache_mem_v, g_pre_mix, w_in, b_if, w_pool, pool_scale, g_mem, w_mem_kv,
              w_br_pool, w_br_mlstm, w_br_xattn, w_out, g_post_mix, g_pre_mlp, w_ff1, w_ff2, g_post_mlp):
    xp = x_prompt
    xs = x_sample
    sdt = state_mlstm_C.dtype
    buf_p_l, C_p_l, n_p_l, m_p_l, mk_p_l, mv_p_l = [], [], [], [], [], []
    buf_s_l, C_s_l, n_s_l, m_s_l = [], [], [], []
    for l in range(DEPTH):
        w = (g_pre_mix[l], w_in[l], b_if[l], w_pool[l], pool_scale[l], w_br_pool[l], w_br_mlstm[l],
             w_br_xattn[l], w_out[l], g_post_mix[l], g_pre_mlp[l], w_ff1[l], w_ff2[l], g_post_mlp[l])
        mk_p, mv_p = memory_kv(mem_prompt, g_mem[l], w_mem_kv[l])
        zbuf = jnp.zeros((BATCH, POOL_BUF, POOL_WIDTH), xp.dtype)
        zC = jnp.zeros((BATCH, MLSTM_HEADS, MLSTM_DH, MLSTM_DH), sdt)
        zn = jnp.zeros((BATCH, MLSTM_HEADS, MLSTM_DH), sdt)
        zm = jnp.zeros((BATCH, MLSTM_HEADS), sdt)
        xp, bp, Cp, npv, mp = layer_forward(xp, zbuf, zC, zn, zm, mk_p, mv_p, 0, *w)
        buf_p_l.append(bp); C_p_l.append(Cp); n_p_l.append(npv); m_p_l.append(mp)
        mk_p_l.append(mk_p); mv_p_l.append(mv_p)
        xs, bs, Cs, nsv, ms = layer_forward(xs, state_pool_buf[l], state_mlstm_C[l], state_mlstm_n[l],
                                            state_mlstm_m[l], cache_mem_k[l], cache_mem_v[l], PAST_LEN, *w)
        buf_s_l.append(bs); C_s_l.append(Cs); n_s_l.append(nsv); m_s_l.append(ms)
    return (xp, xs,
            jnp.stack(buf_p_l), jnp.stack(C_p_l), jnp.stack(n_p_l), jnp.stack(m_p_l),
            jnp.stack(mk_p_l), jnp.stack(mv_p_l),
            jnp.stack(buf_s_l), jnp.stack(C_s_l), jnp.stack(n_s_l), jnp.stack(m_s_l))


_drawn_inputs = setup_inputs


def setup_inputs(seed=0):
    import zlib

    import numpy as np

    out = dict(_drawn_inputs(seed))
    spreads = {}
    factors = {}
    for name, (base, spread) in spreads.items():
        noise = np.random.default_rng([zlib.crc32(name.encode()), seed]).standard_normal(out[name].shape)
        drawn = base * np.exp(spread * noise) if base else spread * noise
        out[name] = __import__('jax').numpy.asarray(drawn.astype(out[name].dtype))
    for name, factor in factors.items():
        out[name] = (out[name] * factor).astype(out[name].dtype)
    return out
```

```python
import concourse.bass as bass
from concourse import mybir
from contextlib import ExitStack

F32 = mybir.dt.float32
F32R = mybir.dt.float32r
BF16 = mybir.dt.bfloat16
ACT = mybir.ActivationFunctionType
ALU = mybir.AluOpType
AX = mybir.AxisListType

P = 128
D = 1024
T = 1024
ND = 8
N = T + ND
NG = 3
G = N // NG
KD = D // P
HEADS = 4
L = 128
NC = T // L
MEM = 256
FILL = 32
EPS = 1e-6
MASKED = -1e30
K_SCALE = 1.0 / 16.0
X_SCALE = float(128) ** -0.5

SLAB_GATE = 8
SLAB_HEAD = 9
SLABS_PER_HEAD = 18
SLAB_MERGE = SLAB_HEAD + HEADS * SLABS_PER_HEAD
SLAB_OUT = SLAB_MERGE + 8
SLAB_FF = SLAB_OUT + 8
SLABS = SLAB_FF + 64

UNIT_HEAD = 1
UNITS_PER_HEAD = 24
UNIT_POOL = UNIT_HEAD + HEADS * UNITS_PER_HEAD
UNIT_MERGE = UNIT_POOL + 4
UNIT_OUT = UNIT_MERGE + 16
UNIT_FF = UNIT_OUT + 8
UNIT_FF_LOOP = UNIT_FF + 4
UNITS_PER_FF_STEP = 24
UNIT_FF_TAIL = UNIT_FF_LOOP + 3 * UNITS_PER_FF_STEP
V_PRE, V_MEM, V_POST, V_MLP, V_FF, V_POOL = 0, 8, 16, 24, 32, 40
B_, WI_, WE_, EM_ = range(4)


def hybrid_layer(nc, w_stream, xT, memT, vecs, b_if, w_pool, poolbuf, stC, stn, stm, ckT, cv,
                 o_y, o_pool, o_C, o_m, o_kv, o_pool_s, o_C_s, o_n_s,
                 d_side, d_x1, d_qk, d_v):
    with ExitStack() as ctx:
        def sb(name, shape, dt=F32):
            return ctx.enter_context(nc.sbuf_tensor(name, shape, dt))

        def overlap(*groups):
            sizes = []
            made = []
            for group in groups:
                with ExitStack() as own:
                    made.append([own.enter_context(nc.sbuf_tensor(n, s, d)) for n, s, d in group])
                size = 0
                for _, s, d in group:
                    b = 2 if d == BF16 else 4
                    for e in s[1:]:
                        b *= e
                    size += -(-b // 32) * 32
                sizes.append(size)
            ctx.enter_context(nc.sbuf_tensor(f"room_{groups[0][0][0]}", [P, max(sizes) // 4], F32))
            return made

        (h_hi, h_lo), (u_pad, xq, kv_in, v_in, P_sb, PT_sb, ckt, cvt, xs_t) = overlap(
            [("h_hi", [P, KD, N], F32R), ("h_lo", [P, KD, N], F32R)],
            [("u_pad", [P, 4, 16 + N], F32), ("xq", [P, 4, N], F32), ("kv_in", [P, 4, MEM], F32),
             ("v_in", [P, 2, 512], F32), ("P_sb", [P, 4, MEM], F32), ("PT_sb", [P, 8, P], F32),
             ("ckt", [P, 4, MEM], F32), ("cvt", [P, 2, 512], F32), ("xs_t", [P, 4, P], F32)])
        (acc,), (kvT, v_tok, m_hi, m_lo), (R, gf, gi, lf, bb, mm_, tg, wi_diag, mprev, wsel) = overlap(
            [("acc", [P, KD, N], F32)],
            [("kvT", [P, 8, MEM], F32), ("v_tok", [P, 2, 512], F32),
             ("m_hi", [P, KD, MEM], F32R), ("m_lo", [P, KD, MEM], F32R)],
            [("R", [P, N], F32), ("gf", [4, N], F32), ("gi", [4, N], F32), ("lf", [4, N], F32),
             ("bb", [4, N], F32), ("mm_", [4, N], F32), ("tg", [4, N], F32), ("wi_diag", [4, NC + 2 * ND, 4], F32), ("mprev", [4, NC + 1], F32),
             ("wsel", [4, NC + 2 * ND], F32)])
        ((q_h, k_h, kw_all, v_all, o_h, y_hi, y_lo, side_t, qs, ks, kw, SW, Cn, num,
          dC, qkb, dtmp, ns),
         (x_in, mem_in, rstd0, rstd0b, sq0),
         (yp_hi, yp_lo, yx_hi, yx_lo, gates),
         (_p0, _p1, win_a, win_b, pool_d, inv_count, bufT, wp),
         (f_hi, f_lo, rl, sqv)) = overlap(
            [("q_h", [P, 2, N], F32), ("k_h", [P, 2, N], F32), ("kw_all", [P, NC, 256], F32),
             ("v_all", [P, NC, 257], F32), ("o_h", [P, 2, N], F32), ("y_hi", [P, 2, N], F32R),
             ("y_lo", [P, 2, N], F32R), ("side_t", [P, N], F32), ("qs", [P, 2, L], F32),
             ("ks", [P, 2, L], F32), ("kw", [P, 256], F32), ("SW", [P, L], F32),
             ("Cn", [P, 2, 257], F32), ("num", [P, 257], F32),
             ("dC", [P, 2, 256], F32), ("qkb", [P, 512], F32), ("dtmp", [P, 2, 256], F32), ("ns", [ND, 1024], F32)],
            [("x_in", [P, KD, N], F32), ("mem_in", [P, KD, MEM], F32), ("rstd0", [P, N], F32),
             ("rstd0b", [P, N], F32), ("sq0", [P, 2, N], F32)],
            [("yp_hi", [P, 4, N], F32R), ("yp_lo", [P, 4, N], F32R), ("yx_hi", [P, 4, N], F32R),
             ("yx_lo", [P, 4, N], F32R), ("gates", [P, NG, 3, G], F32)],
            [("_p0", [P, 4, N], F32R), ("_p1", [P, 4, N], F32R), ("win_a", [P, 16 + N], F32),
             ("win_b", [P, 16 + N], F32), ("pool_d", [P, 2, N], F32), ("inv_count", [P, 16], F32),
             ("bufT", [P, 4, ND, 15], F32), ("wp", [P, 4, P], F32)],
            [("f_hi", [P, 2, 4, N], F32R), ("f_lo", [P, 2, 4, N], F32R), ("rl", [P, NG, G], F32),
             ("sqv", [P, NG, G], F32)])
        w_raw = sb("w_raw", [P, 2, 1024])
        w_hi = sb("w_hi", [P, 2, 1024], F32R)
        w_lo = sb("w_lo", [P, 2, 1024], F32R)
        vec = sb("vec", [P, 44])
        bif = sb("bif", [4, 2])
        ident = sb("ident", [P, P])
        ident_b = sb("ident_b", [P, P], BF16)
        mask_b = sb("mask_b", [P, P], BF16)
        ones = sb("ones", [P, P])
        eps = sb("eps", [P, 1])
        A_row = sb("A_row", [4, N])
        A_pick = sb("A_pick", [4, L])
        cols = sb("cols", [P, NC + 1, 4, 4])
        col = sb("col", [P, 5])
        decays = sb("decays", [P, NC, 4])
        dw = sb("dw", [P, 2, ND, 4])
        m_out = sb("m_out", [4, 1 + ND])
        m0 = sb("m0", [4, ND])
        wv = sb("wv", [P, 2, ND])
        qkd = sb("qkd", [ND, 512])
        dcol = sb("dcol", [ND, 8])
        rdiag = sb("rdiag", [ND, ND])
        num_d = sb("num_d", [P, 2, ND])
        yd = sb("yd", [P, 2, ND])
        den = sb("den", [P, 4])
        sm = sb("sm", [P, 16])

        bank = [ctx.enter_context(nc.psum_tensor(f"bank{i}", [P, 512], F32)) for i in range(8)]
        b_S, b_W, b_N, b_I, b_U = bank[3:8]

        def sem(name):
            return ctx.enter_context(nc.semaphore(name))

        s_consts = sem("consts")
        s_masks = sem("masks")
        s_const_loaded = sem("const_loaded")
        s_mem_loaded = sem("mem_loaded")
        s_slab_split = sem("slab_split")
        s_mem_sq = sem("mem_sq")
        s_mem_ssq = sem("mem_ssq")
        s_mem_std = sem("mem_std")
        s_mem_h = sem("mem_h")
        s_mem_hi = sem("mem_hi")
        s_mem_lo = sem("mem_lo")
        s_mem_ready = sem("mem_ready")
        s_mem_taken = sem("mem_taken")
        s_memv_t = sem("memv_t")
        s_memv_taken = sem("memv_taken")
        s_kv_stored = sem("kv_stored")
        s_v_stored = sem("v_stored")
        s_x_sq = sem("x_sq")
        s_x_sq_used = sem("x_sq_used")
        s_x_std = sem("x_std")
        s_x_h = sem("x_h")
        s_x_hi = sem("x_hi")
        s_x_lo = sem("x_lo")
        s_gate_row = sem("gate_row")
        s_gate_act = sem("gate_act")
        s_rows_ready = sem("rows_ready")
        s_table_t = sem("table_t")
        s_bcast_ready = sem("bcast_ready")
        s_vT_ready = sem("vT_ready")
        s_vT_taken = sem("vT_taken")
        s_kT_ready = sem("kT_ready")
        s_kT_taken = sem("kT_taken")
        s_dqk_ready = sem("dqk_ready")
        s_dqk_taken = sem("dqk_taken")
        s_dqk_stored = sem("dqk_stored")
        s_col_set = sem("col_set")
        s_staged = sem("staged")
        s_scores_ready = sem("scores_ready")
        s_logw_ready = sem("logw_ready")
        s_weights_ready = sem("weights_ready")
        s_weighted_ready = sem("weighted_ready")
        s_carried_ready = sem("carried_ready")
        s_update_ready = sem("update_ready")
        s_carried_scaled = sem("carried_scaled")
        s_num_ready = sem("num_ready")
        s_den_max = sem("den_max")
        s_den_inv = sem("den_inv")
        s_hn_ready = sem("hn_ready")
        s_hT_ready = sem("hT_ready")
        s_yv_ready = sem("yv_ready")
        s_yhi_ready = sem("yhi_ready")
        s_ylo_ready = sem("ylo_ready")
        s_C_new = sem("C_new")
        s_dstate_loaded = sem("dstate_loaded")
        s_dstate_used = sem("dstate_used")
        s_dstate_stored = sem("dstate_stored")
        s_dkv_ready = sem("dkv_ready")
        s_side_stored = sem("side_stored")
        s_dwk_ready = sem("dwk_ready")
        s_dn_new = sem("dn_new")
        s_ddot_ready = sem("ddot_ready")
        s_dden_ready = sem("dden_ready")
        s_dinv_ready = sem("dinv_ready")
        s_dinv_diag = sem("dinv_diag")
        s_dinv_all = sem("dinv_all")
        s_dy_gated = sem("dy_gated")
        s_dy_scaled = sem("dy_scaled")
        s_dy_hi = sem("dy_hi")
        s_dy_ready = sem("dy_ready")
        s_C_stored = sem("C_stored")
        s_wv_ready = sem("wv_ready")
        s_n_stored = sem("n_stored")
        s_dve_step = sem("dve_step")
        s_dstate_new = sem("dstate_new")
        s_side_loaded = sem("side_loaded")
        s_pool_state_ready = sem("pool_state_ready")
        s_pool_d_ready = sem("pool_d_ready")
        s_pool_in_loaded = sem("pool_in_loaded")
        s_pool_hi = sem("pool_hi")
        s_pool_lo = sem("pool_lo")
        s_pool_stored = sem("pool_stored")
        s_kv_loaded = sem("kv_loaded")
        s_xs_staged = sem("xs_staged")
        s_xscores_ready = sem("xscores_ready")
        s_xmax_ready = sem("xmax_ready")
        s_xbias_ready = sem("xbias_ready")
        s_xexp_ready = sem("xexp_ready")
        s_xinv_ready = sem("xinv_ready")
        s_xprob_ready = sem("xprob_ready")
        s_xprobT_ready = sem("xprobT_ready")
        s_xprobT_taken = sem("xprobT_taken")
        s_xo_ready = sem("xo_ready")
        s_xo_hi = sem("xo_hi")
        s_xo_lo = sem("xo_lo")
        s_ck_loaded = sem("ck_loaded")
        s_cv_loaded = sem("cv_loaded")
        s_dscores_taken = sem("dscores_taken")
        s_dscoresT_ready = sem("dscoresT_ready")
        s_dbias_ready = sem("dbias_ready")
        s_dexp_ready = sem("dexp_ready")
        s_dprob_ready = sem("dprob_ready")
        s_dprobT_ready = sem("dprobT_ready")
        s_dprobT_taken = sem("dprobT_taken")
        s_dattn_hi = sem("dattn_hi")
        s_dattn_lo = sem("dattn_lo")
        s_dkeys_used = sem("dkeys_used")
        s_dvalues_used = sem("dvalues_used")
        s_g_sig = sem("g_sig")
        s_acc_gated = sem("acc_gated")
        s_pool_added = sem("pool_added")
        s_merged = sem("merged")
        s_merged_hi = sem("merged_hi")
        s_merged_lo = sem("merged_lo")
        s_z_evac = sem("z_evac")
        s_z_acc = sem("z_acc")
        s_z_ssq = sem("z_ssq")
        s_z_std = sem("z_std")
        s_x2_loaded = sem("x2_loaded")
        s_z_scaled = sem("z_scaled")
        s_x1_ready = sem("x1_ready")
        s_x1_sq = sem("x1_sq")
        s_x1_ssq = sem("x1_ssq")
        s_x1_std = sem("x1_std")
        s_x1_stored = sem("x1_stored")
        s_h2_ready = sem("h2_ready")
        s_h2_hi = sem("h2_hi")
        s_h2_lo = sem("h2_lo")
        s_relu_squared = sem("relu_squared")
        s_f_hi = sem("f_hi")
        s_f_lo = sem("f_lo")
        s_f_added = sem("f_added")
        s_f_squared = sem("f_squared")
        s_f_ssq = sem("f_ssq")
        s_f_std = sem("f_std")
        s_x3_loaded = sem("x3_loaded")
        s_y_scaled = sem("y_scaled")
        s_y_ready = sem("y_ready")
        s_y_stored = sem("y_stored")
        s_hi_made = sem("hi_made")
        s_x_loaded = [sem(f"x_loaded{i}") for i in range(2)]
        s_slab_loaded = [sem(f"slab_loaded{i}") for i in range(2)]
        s_g_loaded = [sem(f"g_loaded{i}") for i in range(3)]
        s_group_ready = [sem(f"group_ready{i}") for i in range(3)]
        s_group_free = [sem(f"group_free{i}") for i in range(3)]
        block = ctx.enter_context(nc.Block())
        tok = [slice(g * G, (g + 1) * G) for g in range(NG)]

        def sq_ring(i):
            return sq0[:, i // 2, (i % 2) * G:(i % 2 + 1) * G]

        @block.sync
        def _(sp):
            def slab(n, slot, split):
                if split is not None:
                    sp.wait_ge(s_slab_split, split)
                src = w_stream[n] if isinstance(n, int) else w_stream[bass.ds(n, 1)].rearrange("a p c -> (a p) c")
                sp.dma_start(w_raw[:, slot, :], src).then_inc(s_slab_loaded[slot], 16)

            sp.dma_start(mem_in[:, :, :], memT).then_inc(s_mem_loaded, 16)
            slab(0, 0, None)
            slab(1, 1, None)
            sp.dma_start(vec[:, :], vecs).then_inc(s_const_loaded, 16)
            sp.dma_start(bif[:, :], b_if).then_inc(s_const_loaded, 16)
            sp.dma_start(m0[:, :], stm).then_inc(s_const_loaded, 16)
            sp.dma_start(ns[:, :], stn).then_inc(s_const_loaded, 16)
            for i in range(2):
                sp.dma_start(x_in[:, 4 * i:4 * i + 4, :], xT[:, 4 * i:4 * i + 4, :]).then_inc(s_x_loaded[i], 16)
            for n in range(2, SLAB_HEAD + 2):
                slab(n, n % 2, n - 1)
            with sp.Fori(0, HEADS) as h:
                for j in range(2, 10):
                    slab(SLAB_HEAD + SLABS_PER_HEAD * h + j, (SLAB_HEAD + j) % 2,
                         SLAB_HEAD + SLABS_PER_HEAD * h + j - 1)
                with sp.Fori(0, NC // 2) as c2:
                    for e in range(2):
                        c = 2 * c2 + e
                        sp.wait_ge(s_dqk_stored, 16 * (h + 1))
                        sp.dma_start(dC[:, :, :], stC[bass.ds(h, 1), bass.ds(c, 1)].rearrange("a b p k c -> (a b p) k c"))\
                            .then_inc(s_dstate_loaded, 16)
                        sp.dma_start(qkb[:, :], d_qk[bass.ds(h, 1), bass.ds(c, 1)].rearrange("a b n -> (a b) n")
                                     .to_broadcast([P, 512])).then_inc(s_dstate_loaded, 16)
                        sp.wait_ge(s_dstate_used, NC * h + c + 1)
                        sp.dma_start(o_C_s[bass.ds(h, 1), bass.ds(c, 1)].rearrange("a b p k c -> (a b p) k c"), dC[:, :, :])\
                            .then_inc(s_dstate_stored, 16)
                        sp.wait_ge(s_dstate_stored, 16 * (NC * h + c + 1))
                        n = SLAB_HEAD + SLABS_PER_HEAD * h + 10 + c
                        slab(n, (SLAB_HEAD + e) % 2, n - 1)
                for j in range(2):
                    n = SLAB_HEAD + SLABS_PER_HEAD * (h + 1) + j
                    slab(n, (SLAB_HEAD + j) % 2, n - 1)
            sp.wait_ge(s_side_stored, 16 * FILL)
            sp.wait_ge(s_group_ready[2], UNIT_POOL)
            for k in range(4):
                sp.dma_start(u_pad[:, k, 16:16 + N], d_side[k]).then_inc(s_side_loaded, 16)
            for k in range(4):
                sp.dma_start(xq[:, k, :], d_side[4 + k]).then_inc(s_side_loaded, 16)
            sp.dma_start(bufT[:, :, :, :], poolbuf).then_inc(s_pool_in_loaded, 16)
            sp.dma_start(wp[:, :, :], w_pool).then_inc(s_pool_in_loaded, 16)
            sp.dma_start(kv_in[:, :, :], o_kv[:, 0:4, :]).then_inc(s_kv_loaded, 16)
            sp.dma_start(v_in[:, :, :], d_v).then_inc(s_kv_loaded, 16)
            sp.dma_start(ckt[:, :, :], ckT[0]).then_inc(s_ck_loaded, 16)
            sp.dma_start(cvt[:, :, :], cv[0]).then_inc(s_cv_loaded, 16)
            with sp.Fori(1, ND) as b:
                sp.wait_ge(s_dkeys_used, b)
                sp.dma_start(ckt[:, :, :], ckT[bass.ds(b, 1)].rearrange("a p k c -> (a p) k c")).then_inc(s_ck_loaded, 16)
            with sp.Fori(1, ND) as b:
                sp.wait_ge(s_dvalues_used, b)
                sp.dma_start(cvt[:, :, :], cv[bass.ds(b, 1)].rearrange("a p k c -> (a p) k c")).then_inc(s_cv_loaded, 16)
            sp.wait_ge(s_n_stored, 32)
            for j in range(8):
                for g in range(NG):
                    if j == 0:
                        if g == 0:
                            sp.wait_ge(s_xo_lo, NC)
                    else:
                        sp.wait_ge(s_merged, NG * (j - 1) + g + 1)
                    sp.dma_start(gates[:, g, :, :], d_side[8:32, :, tok[g]].rearrange("(b j) p t -> j p b t", j=8)[j])\
                        .then_inc(s_g_loaded[g], 16)
                n = SLAB_MERGE + 2 + j
                slab(n, n % 2, n - 1)
            sp.wait_ge(s_merged_lo, 24)
            sp.wait_ge(s_group_ready[2], UNIT_OUT)
            sp.dma_start(x_in[:, :, :], xT).then_inc(s_x2_loaded, 16)
            with sp.Fori(SLAB_MERGE + 10, SLABS - 1, 2) as n:
                slab(n, (SLAB_MERGE + 10) % 2, n - 1)
                slab(n + 1, (SLAB_MERGE + 11) % 2, n)
            sp.wait_ge(s_f_added, 24 * 8)
            sp.wait_ge(s_x1_stored, 16)
            sp.dma_start(x_in[:, :, :], d_x1).then_inc(s_x3_loaded, 16)
            for k in range(KD):
                sp.wait_ge(s_y_ready, k + 1)
                sp.dma_start(o_y[:, k, :], x_in[:, k, :]).then_inc(s_y_stored, 16)
            sp.wait_ge(s_y_stored, 16 * KD)

        @block.gpsimd
        def _(pool):
            for tile_, value in ((ident, 0.0), (ident_b, 0.0), (mask_b, 0.0), (ones, 1.0), (eps, EPS)):
                pool.memset(tile_[:, :], value).then_inc(s_consts, 1)
            pool.wait_ge(s_consts, 5)
            for tile_ in (ident, ident_b):
                pool.affine_select(out=tile_[:, :], in_=tile_[:, :], compare_op=ALU.not_equal, fill=1.0, base=0,
                                   pattern=[[-1, P]], channel_multiplier=1).then_inc(s_masks, 1)
            pool.affine_select(out=mask_b[:, :], in_=mask_b[:, :], compare_op=ALU.is_ge, fill=MASKED, base=0,
                               pattern=[[1, P]], channel_multiplier=-1).then_inc(s_masks, 1)

            def split(n, slot, used=None):
                pool.wait_ge(s_slab_loaded[slot], 16 * (n // 2 + 1) if isinstance(n, int) else 8 * (n - slot) + 16)
                if used is not None:
                    pool.wait_ge(*used)
                pool.tensor_tensor(w_hi[:, slot, :], w_raw[:, slot, :], ones[:, 0:1].to_broadcast([P, 1024]), ALU.mult).then_inc(s_hi_made, 1)
                pool.wait_ge(s_hi_made, n + 1)
                pool.tensor_tensor(w_lo[:, slot, :], w_raw[:, slot, :], w_hi[:, slot, :].bitcast(F32), ALU.subtract)\
                    .then_inc(s_slab_split, 1)

            for n in range(SLAB_HEAD + 2):
                if n < 2:
                    split(n, n % 2)
                elif n < SLAB_HEAD + 1:
                    split(n, n % 2, (s_mem_ready, n - 1))
                else:
                    split(n, n % 2, (s_group_ready[2], 1))
            with pool.Fori(0, HEADS) as h:
                for j in range(2, SLABS_PER_HEAD + 2):
                    d = j - 2
                    units = d + 1 if d < 16 else 20 + 4 * (d - 16)
                    split(SLAB_HEAD + SLABS_PER_HEAD * h + j, (SLAB_HEAD + j) % 2,
                          (s_group_ready[2], UNIT_HEAD + UNITS_PER_HEAD * h + units))
            for j in range(2, 20):
                d = j - 2
                units = UNIT_MERGE + 2 * (d + 1) if d < 8 else UNIT_OUT + d - 7
                n = SLAB_MERGE + j
                split(n, n % 2, (s_group_ready[2], units))
            done = [0, 1] + [1, 2, 3, 4] + [6, 8, 10, 12] + [13, 14, 15, 16] + [18, 20]
            done[0] = -1
            done[1] = 0
            with pool.Fori(0, 3) as i:
                for j in range(16):
                    split(SLAB_FF + 4 + 16 * i + j, (SLAB_FF + j) % 2,
                          (s_group_ready[2], UNIT_FF_LOOP + UNITS_PER_FF_STEP * i + done[j]))
            tail = [-1, 0, 1, 2, 3, 4, 6, 8, 10, 12, 14, 16]
            for j in range(12):
                n = SLAB_FF + 52 + j
                split(n, n % 2, (s_group_ready[2], UNIT_FF_TAIL + tail[j]))

        @block.tensor
        def _(pe):
            def product(out, blocks, passes3=True):
                n = 3 * len(blocks) if passes3 else len(blocks)
                i = 0
                for b in blocks:
                    for st, mv in (((b[0], b[2]), (b[1], b[2]), (b[0], b[3])) if passes3 else (b,)):
                        last = pe.matmul(out, st, mv, start=i == 0, stop=i == n - 1)
                        i += 1
                return last

            def group(g, t, blocks, passes3=True):
                if not (isinstance(t, int) and t == 0):
                    pe.wait_ge(s_group_free[g], t)
                product(bank[g][:, 0:G], blocks, passes3).then_inc(s_group_ready[g], 1)

            def w_blocks(slot, count, width, col0):
                return [(w_hi[:, slot, k * width + col0:k * width + col0 + P],
                         w_lo[:, slot, k * width + col0:k * width + col0 + P]) for k in range(count)]

            def h_group(slot, g, t):
                group(g, t, [(a, b, h_hi[:, k, tok[g]], h_lo[:, k, tok[g]])
                             for k, (a, b) in enumerate(w_blocks(slot, KD, P, 0))])

            def h_unit(n, slot, t):
                pe.wait_ge(s_slab_split, n + 1)
                for g in range(NG):
                    h_group(slot, g, t)

            def mean_square(out_banks, sq, used):
                for k in range(KD):
                    pe.wait_ge(sq, k + 1)
                    for g in range(NG):
                        last = pe.matmul(out_banks[g][:, 0:G], ones[:, :], sq0[:, k % 2, tok[g]], start=k == 0, stop=k == 7)
                    last.then_inc(used, 1)

            pe.wait_ge(s_consts, 5)
            pe.wait_ge(s_masks, 3)
            pe.wait_ge(s_mem_sq, 1)
            for k in range(KD):
                last = pe.matmul(b_U[:, 0:MEM], ones[:, :], kvT[:, k, :], start=k == 0, stop=k == 7)
            last.then_inc(s_mem_ssq, 1)
            mean_square((b_S, b_W, b_N), s_x_sq, s_x_sq_used)
            pe.wait_ge(s_mem_lo, 1)
            for n in range(8):
                pe.wait_ge(s_slab_split, n + 1)
                if n >= 2:
                    pe.wait_ge(s_mem_taken, n - 1)
                product((b_I, b_U)[n % 2][:, 0:MEM], [(a, b, m_hi[:, k, :], m_lo[:, k, :])
                        for k, (a, b) in enumerate(w_blocks(n % 2, KD, P, 0))]).then_inc(s_mem_ready, 1)
            pe.wait_ge(s_mem_taken, 8)
            for m in range(2):
                for j in range(4):
                    last = pe.transpose((b_I, b_U)[m][:, j * P:(j + 1) * P], kvT[:, 4 + j, m * P:(m + 1) * P], ident[:, :])
                last.then_inc(s_memv_t, 1)
            pe.wait_ge(s_slab_split, SLAB_GATE + 1)
            for g in range(NG):
                pe.wait_ge(s_x_lo, KD * (g + 1))
                h_group(SLAB_GATE % 2, g, 0)

            def gate_tables():
                pe.wait_ge(s_rows_ready, 1)
                for c in range(NC + 1):
                    w = L if c < NC else ND
                    b = (b_S, b_W, b_N)[c // 4]
                    last = pe.transpose(b[0:w, (c % 4) * P:(c % 4 + 1) * P], R[:, c * L:c * L + w], ident[:, :])
                    if c in (3, 7, 8):
                        last.then_inc(s_table_t, 1)
                pe.matmul(b_U[:, 0:96], ones[0:4, :], wi_diag[:, :, :].rearrange("p c h -> p (c h)"),
                          start=True, stop=True).then_inc(s_bcast_ready, 1)

            gate_tables()
            b_tr = (b_S, b_W, b_N, b_I)
            with pe.Fori(0, HEADS) as h:
                n0 = SLAB_HEAD + SLABS_PER_HEAD * h
                t0 = UNIT_HEAD + UNITS_PER_HEAD * h
                sl = [(SLAB_HEAD + j) % 2 for j in range(SLABS_PER_HEAD)]

                def transposes(src, ready, taken):
                    for r in range(4):
                        for c in (2 * r, 2 * r + 1):
                            for k in range(2):
                                last = pe.transpose(b_tr[r][:, (c % 2) * 256 + k * P:(c % 2) * 256 + (k + 1) * P],
                                                    src[:, k, c * L:(c + 1) * L], ident[:, :])
                        last.then_inc(ready, 1)

                for j in range(3):
                    h_unit(n0 + j, sl[j], t0 + j)
                for g in range(NG):
                    pe.wait_ge(s_group_free[g], t0 + 2)
                transposes(o_h, s_vT_ready, None)
                for j in range(3, 7):
                    h_unit(n0 + j, sl[j], t0 + j)
                for g in range(NG):
                    pe.wait_ge(s_group_free[g], t0 + 6)
                pe.wait_ge(s_vT_taken, 4 * h + 4)
                transposes(k_h, s_kT_ready, None)
                for i, src in enumerate((q_h, k_h)):
                    for k in range(2):
                        last = pe.transpose(b_U[0:ND, (2 * i + k) * P:(2 * i + k + 1) * P], src[:, k, T:N], ident[:, :])
                last.then_inc(s_dqk_ready, 1)
                h_unit(n0 + 7, sl[7], t0 + 7)
                with pe.Fori(0, NC // 2) as c2:
                    for e in range(2):
                        c = 2 * c2 + e
                        i1 = NC * h + c + 1
                        t = t0 + 8 + c
                        n = n0 + 8 + c
                        slot = (SLAB_HEAD + e) % 2
                        pe.wait_ge(s_staged, i1)
                        for k in range(2):
                            last = pe.matmul(b_S[:, 0:L], ks[:, k, :], qs[:, k, :], start=k == 0, stop=k == 1)
                        last.then_inc(s_scores_ready, 1)
                        pe.matmul(b_W[:, 0:L], ident_b[:, :], mask_b[:, :], start=True, stop=False)
                        pe.matmul(b_W[:, 0:L], ones[0:4, :], A_pick[:, :], start=False, stop=True).then_inc(s_logw_ready, 1)
                        pe.wait_ge(s_slab_split, n + 1)
                        h_group(slot, 0, t)
                        pe.wait_ge(s_weighted_ready, i1)
                        vc = v_all[:, bass.ds(c, 1), :].rearrange("p a n -> p (a n)")
                        pe.matmul(b_N[:, 0:257], SW[:, :], vc, start=True, stop=True)
                        for k in range(2):
                            pe.matmul(b_N[:, 260 + k:261 + k], kw[:, k * P:(k + 1) * P], ones[:, 0:1], start=True, stop=True)
                        for k in range(2):
                            last = pe.matmul(b_I[:, 0:257], qs[:, k, :], Cn[:, k, :], start=k == 0, stop=k == 1)
                        last.then_inc(s_carried_ready, 1)
                        for k in range(2):
                            last = pe.matmul(b_U[:, k * 256:(k + 1) * 256], kw[:, k * P:(k + 1) * P],
                                             v_all[:, bass.ds(c, 1), 0:256].rearrange("p a n -> p (a n)"), start=True, stop=True)
                        last.then_inc(s_update_ready, 1)
                        h_group(slot, 1, t)
                        pe.wait_ge(s_hn_ready, i1)
                        for k in range(2):
                            last = pe.transpose(b_S[:, P + k * P:P + (k + 1) * P], num[:, k * P:(k + 1) * P], ident[:, :])
                        last.then_inc(s_hT_ready, 1)
                        h_group(slot, 2, t)
                pe.wait_ge(s_dinv_diag, h + 1)
                pe.wait_ge(s_dy_gated, h + 1)
                pe.matmul(b_U[:, 0:ND], ones[0:ND, :], rdiag[:, :], start=True, stop=True).then_inc(s_dinv_all, 1)
                pe.wait_ge(s_ylo_ready, NC * h + NC)
                for j in range(8):
                    sj = 16 + j // 4
                    if j % 4 == 0:
                        pe.wait_ge(s_slab_split, n0 + sj + 1)
                    for g in range(NG):
                        if j == 0 and g == 2:
                            pe.wait_ge(s_dy_ready, h + 1)
                        group(g, t0 + 16 + j, [(a, b, y_hi[:, k, tok[g]], y_lo[:, k, tok[g]])
                                               for k, (a, b) in enumerate(w_blocks(sl[sj], 2, 512, (j % 4) * P))])

            pe.wait_ge(s_pool_in_loaded, 32)
            for w in range(4):
                pe.wait_ge(s_pool_d_ready, w + 1)
                for g in range(NG):
                    group(g, UNIT_POOL + w, [(wp[:, w, :], pool_d[:, w % 2, tok[g]])], False)
            pe.wait_ge(s_side_loaded, 16 * 8)
            with pe.Fori(0, ND) as b:
                pe.wait_ge(s_ck_loaded, 16 * (b + 1))
                for m in range(2):
                    for hh in range(4):
                        last = pe.matmul(b_N[:, bass.ds(m * 32 + hh * 8 + b, 1)], ckt[:, hh, m * P:(m + 1) * P],
                                         xq[:, hh, bass.ds(T + b, 1)], start=True, stop=True)
                last.then_inc(s_dkeys_used, 1)
            pe.wait_ge(s_dscores_taken, 1)
            for m in range(2):
                last = pe.transpose(b_U[0:32, m * P:(m + 1) * P], P_sb[:, 0, m * 32:(m + 1) * 32], ident[:, :])
            last.then_inc(s_dscoresT_ready, 1)
            pe.wait_ge(s_dprob_ready, 1)
            for m in range(2):
                last = pe.transpose(b_N[:, m * 32:(m + 1) * 32], P_sb[0:32, 1, m * P:(m + 1) * P], ident[0:32, 0:32])
            last.then_inc(s_dprobT_ready, 1)
            pe.wait_ge(s_dprobT_taken, 1)
            with pe.Fori(0, ND) as b:
                pe.wait_ge(s_cv_loaded, 16 * (b + 1))
                for hh in range(4):
                    for m in range(2):
                        last = pe.matmul(b_I[:, bass.ds(hh * 8 + b, 1)], cvt[:, m, hh * P:(hh + 1) * P],
                                         P_sb[:, 2, bass.ds(m * 32 + hh * 8 + b, 1)], start=m == 0, stop=m == 1)
                last.then_inc(s_dvalues_used, 1)
            pe.wait_ge(s_kv_loaded, 32)
            with pe.Fori(0, NC) as c:
                pe.wait_ge(s_xs_staged, c + 1)
                for hh in range(4):
                    last = pe.matmul((b_S, b_W)[hh // 2][:, (hh % 2) * MEM:(hh % 2 + 1) * MEM], xs_t[:, hh, :], kv_in[:, hh, :],
                                     start=True, stop=True)
                last.then_inc(s_xscores_ready, 1)
                pe.wait_ge(s_xprob_ready, c + 1)
                for i in range(8):
                    last = pe.transpose((b_N, b_I)[i // 4][:, (i % 4) * P:(i % 4 + 1) * P],
                                        P_sb[:, i // 2, (i % 2) * P:(i % 2 + 1) * P], ident[:, :])
                last.then_inc(s_xprobT_ready, 1)
                pe.wait_ge(s_xprobT_taken, 2 * (c + 1))
                for hh in range(4):
                    for m in range(2):
                        last = pe.matmul(b_U[:, hh * P:(hh + 1) * P], v_in[:, m, hh * P:(hh + 1) * P], PT_sb[:, 2 * hh + m, :],
                                         start=m == 0, stop=m == 1)
                last.then_inc(s_xo_ready, 1)
            pe.wait_ge(s_xo_lo, NC)
            pe.wait_ge(s_dattn_lo, 1)
            pe.wait_ge(s_pool_lo, 1)
            with pe.Fori(0, 8, 2) as j2:
                for e in range(2):
                    pe.wait_ge(s_slab_split, SLAB_MERGE + j2 + e + 1)
                    wb = w_blocks((SLAB_MERGE + e) % 2, 8, P, 0)
                    for i, (hi, lo) in enumerate(((yp_hi, yp_lo), (yx_hi, yx_lo))):
                        for g in range(NG):
                            group(g, UNIT_MERGE + 2 * j2 + 2 * e + i,
                                  [(*wb[4 * i + k], hi[:, k, tok[g]], lo[:, k, tok[g]]) for k in range(4)])
            pe.wait_ge(s_merged_lo, 24)
            with pe.Fori(0, 8, 2) as j2:
                for e in range(2):
                    h_unit(SLAB_OUT + j2 + e, (SLAB_OUT + e) % 2, UNIT_OUT + j2 + e)
            for g in range(NG):
                pe.wait_ge(s_z_acc, NG * 8 + g + 1)
                pe.matmul((b_S, b_W, b_N)[g][:, 0:G], ones[:, :], rstd0b[:, tok[g]], start=True, stop=True).then_inc(s_z_ssq, 1)
            for g in range(NG):
                for k in range(KD):
                    pe.wait_ge(s_x1_sq, g * KD + k + 1)
                    last = pe.matmul((b_I, b_U, b_S)[g][:, 0:G], ones[:, :], sq_ring(k % 4), start=k == 0, stop=k == 7)
                    last.then_inc(s_x1_ssq, 1)
            def ff1(n, slots, t, first=False):
                for j in range(4):
                    pe.wait_ge(s_slab_split, n + j + 1)
                    for g in range(NG):
                        if first and j == 0:
                            pe.wait_ge(s_h2_lo, KD * (g + 1))
                        h_group(slots[j], g, t + j)

            def ff2(n, slots, t, half, blocks_done):
                pe.wait_ge(s_f_lo, blocks_done)
                for j in range(8):
                    if j % 2 == 0:
                        pe.wait_ge(s_slab_split, n + j // 2 + 1)
                    for g in range(NG):
                        group(g, t + j, [(a, b, f_hi[:, half, k, tok[g]], f_lo[:, half, k, tok[g]])
                                         for k, (a, b) in enumerate(w_blocks(slots[j // 2], 4, 256, (j % 2) * P))])

            def par(n0_):
                return [(n0_ + j) % 2 for j in range(4)]

            ff1(SLAB_FF, par(SLAB_FF), UNIT_FF, True)
            with pe.Fori(0, 3) as i:
                n0 = SLAB_FF + 4 + 16 * i
                t0 = UNIT_FF_LOOP + UNITS_PER_FF_STEP * i
                p = par(SLAB_FF)
                ff1(n0, p, t0)
                ff2(n0 + 4, p, t0 + 4, 0, 24 * i + 12)
                ff1(n0 + 8, p, t0 + 12)
                ff2(n0 + 12, p, t0 + 16, 1, 24 * i + 24)
            n0, t0, p = SLAB_FF + 52, UNIT_FF_TAIL, par(SLAB_FF)
            ff1(n0, p, t0)
            ff2(n0 + 4, p, t0 + 4, 0, 84)
            ff2(n0 + 8, p, t0 + 12, 1, 96)
            for g in range(NG):
                for k in range(KD):
                    pe.wait_ge(s_f_squared, g * KD + k + 1)
                    last = pe.matmul((b_S, b_W, b_N)[g][:, 0:G], ones[:, :], sq_ring(k % 4), start=k == 0, stop=k == 7)
                    last.then_inc(s_f_ssq, 1)

        @block.scalar
        def _(act):
            def take(g, t, out, func=ACT.Copy, scale=1.0):
                act.wait_ge(s_group_ready[g], t + 1)
                act.activation(out, bank[g][:, 0:G], func, scale=scale).then_inc(s_group_free[g], 1)

            act.wait_ge(s_mem_loaded, 16)
            act.activation(kvT[:, :, :], mem_in[:, :, :], ACT.Square).then_inc(s_mem_sq, 1)
            for k in range(KD):
                act.wait_ge(s_x_loaded[k // 4], 16)
                if k >= 2:
                    act.wait_ge(s_x_sq_used, k - 1)
                act.activation(sq0[:, k % 2, :], x_in[:, k, :], ACT.Square).then_inc(s_x_sq, 1)
                if k == 1:
                    act.wait_ge(s_consts, 5)
                    act.wait_ge(s_mem_ssq, 1)
                    act.activation(kvT[:, 0, :], b_U[:, 0:MEM], ACT.Sqrt, scale=1.0 / D, bias=eps[:, 0:1]).then_inc(s_mem_std, 1)
            act.wait_ge(s_x_sq_used, KD)
            for g in range(NG):
                act.activation(rstd0b[:, tok[g]], (b_S, b_W, b_N)[g][:, 0:G], ACT.Sqrt, scale=1.0 / D, bias=eps[:, 0:1]).then_inc(s_x_std, 1)
            act.wait_ge(s_mem_h, 1)
            act.activation(m_hi[:, :, :], mem_in[:, :, :], ACT.Copy).then_inc(s_mem_hi, 1)
            for g in range(NG):
                for k in range(KD):
                    act.wait_ge(s_x_h, g * KD + k + 1)
                    act.activation(h_hi[:, k, tok[g]], x_in[:, k, tok[g]], ACT.Copy).then_inc(s_x_hi, 1)
            for n in range(8):
                act.wait_ge(s_mem_ready, n + 1)
                act.activation(kvT[:, n, :], (b_I, b_U)[n % 2][:, 0:MEM], ACT.Copy).then_inc(s_mem_taken, 1)
            act.wait_ge(s_mem_taken, 8)
            act.dma_start(o_kv, kvT[:, :, :]).then_inc(s_kv_stored, 16)
            for m in range(2):
                act.wait_ge(s_memv_t, m + 1)
                act.activation(v_tok[:, m, :], (b_I, b_U)[m][:, :], ACT.Copy).then_inc(s_memv_taken, 1)
            act.wait_ge(s_memv_taken, 2)
            act.dma_start(d_v, v_tok[:, :, :]).then_inc(s_v_stored, 16)
            act.wait_ge(s_gate_row, 1)
            act.activation(lf[:, :], tg[:, :], ACT.Exp, scale=-1.0).then_inc(s_gate_act, 1)
            act.wait_ge(s_gate_act, 1)
            act.activation(tg[:, :], lf[:, :], ACT.Ln, bias=ones[0:4, 0:1]).then_inc(s_gate_act, 1)
            act.wait_ge(s_gate_row, 2)
            act.activation(R[32:36, :], tg[:, :], ACT.Exp)
            act.activation(R[64:68, :], lf[:, :], ACT.Exp)
            act.activation(R[96:100, :], mm_[:, :], ACT.Exp, scale=-1.0).then_inc(s_gate_act, 1)

            with act.Fori(0, HEADS) as h:
                t0 = UNIT_HEAD + UNITS_PER_HEAD * h
                def block_of(dst, k, t, scale=1.0):
                    for g in (0, 2):
                        take(g, t, dst[:, k, tok[g]], scale=scale)
                block_of(o_h, 0, t0)
                block_of(o_h, 1, t0 + 1)
                block_of(q_h, 0, t0 + 2)
                for r in range(4):
                    act.wait_ge(s_vT_ready, 4 * h + r + 1)
                    act.activation(v_all[:, 2 * r:2 * r + 2, 0:256],
                                   (b_S, b_W, b_N, b_I)[r][:, :].rearrange("p (c n) -> p c n", c=2), ACT.Copy)\
                       .then_inc(s_vT_taken, 1)
                block_of(q_h, 1, t0 + 3)
                block_of(k_h, 0, t0 + 4, K_SCALE)
                block_of(k_h, 1, t0 + 5, K_SCALE)
                act.wait_ge(s_wv_ready, h + 1)
                for g in range(NG):
                    take(g, t0 + 6, o_h[:, 0, tok[g]], ACT.Sigmoid)
                for r in range(4):
                    act.wait_ge(s_kT_ready, 4 * h + r + 1)
                    act.activation(kw_all[:, 2 * r:2 * r + 2, :],
                                   (b_S, b_W, b_N, b_I)[r][:, :].rearrange("p (c n) -> p c n", c=2), ACT.Copy)\
                       .then_inc(s_kT_taken, 1)
                act.wait_ge(s_dqk_taken, h + 1)
                act.dma_start(d_qk[bass.ds(h, 1)].rearrange("a b n -> (a b) n"), qkd[:, :]).then_inc(s_dqk_stored, 16)
                for g in range(NG):
                    take(g, t0 + 7, o_h[:, 1, tok[g]], ACT.Sigmoid)
                with act.Fori(0, NC) as c:
                    i1 = NC * h + c + 1
                    t = t0 + 8 + c
                    act.wait_ge(s_logw_ready, i1)
                    act.activation(SW[:, :], b_W[:, 0:L], ACT.Exp, bias=col[:, B_:B_ + 1]).then_inc(s_weights_ready, 1)
                    take(0, t, side_t[:, tok[0]])
                    act.wait_ge(s_carried_ready, i1)
                    act.activation(num[:, :], b_I[:, 0:257], ACT.Copy, scale=col[:, WI_:WI_ + 1]).then_inc(s_carried_scaled, 1)
                    take(1, t, side_t[:, tok[1]])
                    take(2, t, side_t[:, tok[2]])
                    act.wait_ge(s_group_free[2], t + 1)
                    act.dma_start(d_side[bass.ds(NC * h + c, 1)].rearrange("a p n -> (a p) n"), side_t[:, :])\
                       .then_inc(s_side_stored, 16)
                    act.wait_ge(s_side_stored, 16 * i1)
                act.wait_ge(s_C_new, NC * (h + 1))
                act.dma_start(o_C[bass.ds(h, 1)].rearrange("a p k c -> (a p) k c"), Cn[:, :, :]).then_inc(s_C_stored, 16)
            act.dma_start(o_n_s, ns[:, :]).then_inc(s_n_stored, 16)
            act.dma_start(o_m, m_out[:, :]).then_inc(s_n_stored, 16)
            act.wait_ge(s_side_loaded, 16 * 8)
            act.dma_start(o_pool, u_pad[:, :, 16 + T - 15:16 + T]).then_inc(s_pool_stored, 16)
            for w in range(4):
                for g in range(NG):
                    act.wait_ge(s_group_ready[g], UNIT_POOL + w + 1)
                    act.activation(yp_hi[:, w, tok[g]], bank[g][:, 0:G], ACT.Copy, scale=vec[:, V_POOL + w:V_POOL + w + 1])\
                       .then_inc(s_pool_hi, 1)
            act.wait_ge(s_pool_state_ready, 1)
            act.dma_start(o_pool_s, win_a[:, 0:480]).then_inc(s_pool_stored, 16)
            act.wait_ge(s_dbias_ready, 1)
            act.activation(P_sb[0:32, 1, :], b_U[0:32, 0:MEM], ACT.Exp, bias=sm[0:32, 9:10], scale=X_SCALE,
                           accum_out=sm[0:32, 10:11]).then_inc(s_dexp_ready, 1)
            act.wait_ge(s_pool_stored, 32)
            act.wait_ge(s_dvalues_used, ND)
            act.activation(yx_hi[:, :, T:N], b_I[:, 0:32].rearrange("p (h b) -> p h b", h=4), ACT.Copy).then_inc(s_dattn_hi, 1)
            with act.Fori(0, NC) as c:
                act.wait_ge(s_xbias_ready, c + 1)
                for hh in range(4):
                    act.activation(P_sb[:, hh, :], (b_S, b_W)[hh // 2][:, (hh % 2) * MEM:(hh % 2 + 1) * MEM], ACT.Exp,
                                   bias=sm[:, 4 + hh:5 + hh], scale=X_SCALE, accum_out=sm[:, 8 + hh:9 + hh]).then_inc(s_xexp_ready, 1)
                act.wait_ge(s_xprobT_ready, c + 1)
                act.activation(PT_sb[:, 0:4, :], b_N[:, :].rearrange("p (i t) -> p i t", i=4), ACT.Copy).then_inc(s_xprobT_taken, 1)
            with act.Fori(0, 8) as j:
                for g in range(NG):
                    act.wait_ge(s_g_loaded[g], 16 * (j + 1))
                    act.activation(gates[:, g, :, :], gates[:, g, :, :], ACT.Sigmoid).then_inc(s_g_sig, 1)
                for g in range(NG):
                    act.wait_ge(s_merged, NG * j + g + 1)
                    act.activation(h_hi[:, bass.ds(j, 1), tok[g]].rearrange("p a t -> p (a t)"),
                                   acc[:, bass.ds(j, 1), tok[g]].rearrange("p a t -> p (a t)"), ACT.Copy).then_inc(s_merged_hi, 1)
            with act.Fori(0, 8) as j:
                for g in range(NG):
                    act.wait_ge(s_group_ready[g], UNIT_OUT + j + 1)
                    act.activation(acc[:, bass.ds(j, 1), tok[g]].rearrange("p a t -> p (a t)"), bank[g][:, 0:G], ACT.Copy)\
                       .then_inc(s_z_evac, 1)
                    act.wait_ge(s_z_acc, NG * j + g + 1)
                    act.activation(gates[:, g, 0, :], bank[g][:, 0:G], ACT.Square).then_inc(s_group_free[g], 1)
            for g in range(NG):
                act.wait_ge(s_z_ssq, g + 1)
                act.activation(rstd0b[:, tok[g]], (b_S, b_W, b_N)[g][:, 0:G], ACT.Sqrt, scale=1.0 / D, bias=eps[:, 0:1]).then_inc(s_z_std, 1)
            for g in range(NG):
                for k in range(KD):
                    act.wait_ge(s_x1_ready, g * KD + k + 1)
                    if g * KD + k >= 4:
                        act.wait_ge(s_x1_ssq, g * KD + k - 3)
                    act.activation(sq_ring(k % 4), x_in[:, k, tok[g]], ACT.Square).then_inc(s_x1_sq, 1)
            act.dma_start(d_x1, x_in[:, :, :]).then_inc(s_x1_stored, 16)
            for g in range(NG):
                act.wait_ge(s_x1_ssq, KD * (g + 1))
                act.activation(rstd0b[:, tok[g]], (b_I, b_U, b_S)[g][:, 0:G], ACT.Sqrt, scale=1.0 / D, bias=eps[:, 0:1]).then_inc(s_x1_std, 1)
            for g in range(NG):
                for k in range(KD):
                    act.wait_ge(s_h2_ready, g * KD + k + 1)
                    act.activation(h_hi[:, k, tok[g]], acc[:, k, tok[g]], ACT.Copy).then_inc(s_h2_hi, 1)
            act.wait_ge(s_x1_stored, 16)

            def ff1(t, half, count):
                for j in range(4):
                    for g in range(NG):
                        take(g, t + j, rl[:, g, :], ACT.Relu)
                        act.wait_ge(s_relu_squared, count + NG * j + g + 1)
                        act.activation(f_hi[:, half, j, tok[g]], sqv[:, g, :], ACT.Copy).then_inc(s_f_hi, 1)

            ff1(UNIT_FF, 0, 0)
            with act.Fori(0, 3) as i:
                t0 = UNIT_FF_LOOP + UNITS_PER_FF_STEP * i
                ff1(t0, 1, 24 * i + 12)
                ff1(t0 + 12, 0, 24 * i + 24)
            ff1(UNIT_FF_TAIL, 1, 84)
            act.wait_ge(s_f_added, 24 * 8)
            for g in range(NG):
                for k in range(KD):
                    if g * KD + k >= 4:
                        act.wait_ge(s_f_ssq, g * KD + k - 3)
                    act.activation(sq_ring(k % 4), acc[:, k, tok[g]], ACT.Square).then_inc(s_f_squared, 1)
            for g in range(NG):
                act.wait_ge(s_f_ssq, KD * (g + 1))
                act.activation(rstd0b[:, tok[g]], (b_S, b_W, b_N)[g][:, 0:G], ACT.Sqrt, scale=1.0 / D, bias=eps[:, 0:1]).then_inc(s_f_std, 1)
            for q, n in ((s_kv_stored, 16), (s_v_stored, 16), (s_C_stored, 64), (s_n_stored, 32), (s_pool_stored, 32),
                         (s_side_stored, 16 * FILL)):
                act.wait_ge(q, n)

        @block.vector
        def _(dve):
            chain = [0]

            def step(ins):
                chain[0] += 1
                ins.then_inc(s_dve_step, 1)
                dve.wait_ge(s_dve_step, chain[0])

            def stt(out, in0, scalar, in1, op0, op1):
                return dve.scalar_tensor_tensor(out=out, in0=in0, scalar=scalar, in1=in1, op0=op0, op1=op1)

            def vcol(c):
                return vec[:, c:c + 1]

            dve.wait_ge(s_const_loaded, 64)
            dve.wait_ge(s_mem_std, 1)
            step(dve.reciprocal(kvT[:, 1, :], kvT[:, 0, :]))
            for k in range(KD):
                last = stt(mem_in[:, k, :], mem_in[:, k, :], vcol(V_MEM + k), kvT[:, 1, :], ALU.mult, ALU.mult)
            last.then_inc(s_mem_h, 1)
            dve.wait_ge(s_mem_hi, 1)
            dve.tensor_tensor(m_lo[:, :, :], mem_in[:, :, :], m_hi[:, :, :].bitcast(F32), ALU.subtract).then_inc(s_mem_lo, 1)
            for g in range(NG):
                dve.wait_ge(s_x_std, g + 1)
                step(dve.reciprocal(rstd0[:, tok[g]], rstd0b[:, tok[g]]))
                for k in range(KD):
                    stt(x_in[:, k, tok[g]], x_in[:, k, tok[g]], vcol(V_PRE + k), rstd0[:, tok[g]], ALU.mult, ALU.mult)\
                        .then_inc(s_x_h, 1)
                for k in range(KD):
                    dve.wait_ge(s_x_hi, g * KD + k + 1)
                    dve.tensor_tensor(h_lo[:, k, tok[g]], x_in[:, k, tok[g]], h_hi[:, k, tok[g]].bitcast(F32), ALU.subtract)\
                        .then_inc(s_x_lo, 1)

            dve.wait_ge(s_kv_stored, 16)
            dve.wait_ge(s_v_stored, 16)
            step(dve.memset(R[:, :], 0.0))
            for g in range(NG):
                dve.wait_ge(s_group_ready[g], 1)
                dve.tensor_scalar(gi[:, tok[g]], bank[g][0:4, 0:G], bif[:, 0:1], None, ALU.add)
                dve.tensor_scalar(gf[:, tok[g]], bank[g][32:36, 0:G], bif[:, 1:2], None, ALU.add).then_inc(s_group_free[g], 1)
            dve.wait_ge(s_group_free[2], 1)
            stt(tg[:, :], gf[:, :], -1.0, gf[:, :], ALU.mult, ALU.max).then_inc(s_gate_row, 1)
            dve.wait_ge(s_gate_act, 2)
            step(stt(lf[:, :], gf[:, :], 0.0, tg[:, :], ALU.min, ALU.subtract))
            dve.tensor_tensor_scan(mm_[:, 0:T], lf[:, 0:T], gi[:, 0:T], 0.0, ALU.add, ALU.max)
            dve.memset(gf[:, :], 1.0)
            step(dve.tensor_tensor(tg[:, T:N], lf[:, T:N], m0[:, :], ALU.add))
            dve.tensor_tensor(mm_[:, T:N], tg[:, T:N], gi[:, T:N], ALU.max)
            step(dve.memset(gf[:, 0:T].rearrange("p (c l) -> p c l", l=L)[:, :, 0:1], 0.0))
            dve.tensor_copy(bb[:, T:N], lf[:, T:N])
            step(dve.tensor_tensor_scan(bb[:, 0:T], gf[:, 0:T], lf[:, 0:T], 0.0, ALU.mult, ALU.add))
            dve.memset(mprev[:, 0:1], 0.0)
            dve.tensor_copy(mprev[:, 1:NC + 1], mm_[:, L - 1:T:L])
            dve.tensor_copy(m_out[:, :], mm_[:, T - 1:N])
            dve.tensor_tensor(A_row[:, :], bb[:, :], mm_[:, :], ALU.subtract)
            step(dve.tensor_tensor(R[0:4, :], gi[:, :], bb[:, :], ALU.subtract))

            def chunks(a):
                return a.rearrange("p (c l) -> p c l", l=L)
            dve.tensor_tensor(chunks(tg[:, 0:T]), chunks(A_row[:, 0:T]),
                              mprev[:, 0:NC].unsqueeze(2).to_broadcast([4, NC, L]), ALU.add)
            dve.tensor_tensor(tg[:, T:N], A_row[:, T:N], m0[:, :], ALU.add)
            dve.tensor_tensor(chunks(lf[:, 0:T]), chunks(R[0:4, 0:T]),
                              chunks(A_row[:, 0:T])[:, :, L - 1:L].to_broadcast([4, NC, L]), ALU.add)
            dve.tensor_tensor(lf[:, T:N], R[0:4, T:N], A_row[:, T:N], ALU.add).then_inc(s_gate_row, 1)
            dve.wait_ge(s_gate_act, 3)
            dve.tensor_copy(wsel[:, 0:NC], R[32:36, L - 1:T:L])
            dve.tensor_copy(wsel[:, NC:NC + ND], R[64:68, T:N])
            step(dve.tensor_copy(wsel[:, NC + ND:NC + 2 * ND], R[32:36, T:N]))
            dve.tensor_tensor(wi_diag[:, :, :], wsel[:, :].unsqueeze(2).to_broadcast([4, NC + 2 * ND, 4]),
                              ident[0:4, 0:4].unsqueeze(1).to_broadcast([4, NC + 2 * ND, 4]), ALU.mult)\
               .then_inc(s_rows_ready, 1)
            for i, b in enumerate((b_S, b_W, b_N)):
                dve.wait_ge(s_table_t, i + 1)
                v = b[:, :].rearrange("p (c q r) -> p c q r", c=4, q=4)
                if i < 2:
                    dve.tensor_copy(cols[:, 4 * i:4 * i + 4, :, :], v[:, :, :, 0:4])
                else:
                    dve.tensor_copy(cols[0:ND, NC:NC + 1, :, :], v[0:ND, 0:1, :, 0:4])
            dve.wait_ge(s_bcast_ready, 1)
            dve.tensor_copy(decays[:, :, :], b_U[:, 0:32].rearrange("p (c h) -> p c h", h=4))
            dve.tensor_copy(dw[:, :, :, :], b_U[:, 32:96].rearrange("p (w b h) -> p w b h", w=2, h=4))
            dve.memset(v_all[:, :, 256:257], 1.0)
            step(dve.memset(acc[:, :, :], 0.0))

            with dve.Fori(0, HEADS) as h:
                t0 = UNIT_HEAD + UNITS_PER_HEAD * h
                h1 = h + 1

                def take1(dst, k, t, scale=1.0):
                    dve.wait_ge(s_group_ready[1], t + 1)
                    dve.tensor_scalar(dst[:, k, tok[1]], bank[1][:, 0:G], scale, None, ALU.mult).then_inc(s_group_free[1], 1)
                take1(o_h, 0, t0)
                take1(o_h, 1, t0 + 1)
                take1(q_h, 0, t0 + 2)
                dve.wait_ge(s_group_free[2], t0 + 2)
                dve.tensor_tensor(wv[:, :, :], o_h[:, :, T:N],
                                  dw[:, 0:1, :, bass.ds(h, 1)].rearrange("p w b h -> p (w h) b").to_broadcast([P, 2, ND]),
                                  ALU.mult).then_inc(s_wv_ready, 1)
                take1(q_h, 1, t0 + 3)
                take1(k_h, 0, t0 + 4, K_SCALE)
                take1(k_h, 1, t0 + 5, K_SCALE)
                dve.memset(Cn[:, :, :], 0.0)
                dve.tensor_copy(dcol[:, 0:4], cols[0:ND, NC, :, bass.ds(h, 1)].rearrange("p q h -> p (q h)"))
                dve.wait_ge(s_dqk_ready, h1)
                dve.tensor_copy(qkd[:, :], b_U[0:ND, :]).then_inc(s_dqk_taken, 1)
                n_h = ns[:, bass.ds(256 * h, 256)]
                dve.wait_ge(s_dqk_taken, h1)
                dve.tensor_scalar(dtmp[0:ND, 0, :], qkd[:, 256:512], dcol[:, WE_:WE_ + 1], None, ALU.mult).then_inc(s_dwk_ready, 1)
                dve.wait_ge(s_dwk_ready, h1)
                stt(dtmp[0:ND, 1, :], n_h, dcol[:, WI_:WI_ + 1], dtmp[0:ND, 0, :], ALU.mult, ALU.add).then_inc(s_dn_new, 1)
                dve.wait_ge(s_dn_new, h1)
                dve.tensor_tensor_reduce(out=dtmp[0:ND, 0, :], in0=dtmp[0:ND, 1, :], in1=qkd[:, 0:256], scale=1.0, scalar=0.0,
                                         op0=ALU.mult, op1=ALU.add, accum_out=dcol[:, 4:5]).then_inc(s_ddot_ready, 1)
                dve.tensor_scalar(n_h, dtmp[0:ND, 1, :], 1.0, None, ALU.mult)
                dve.wait_ge(s_ddot_ready, h1)
                dve.tensor_scalar(dcol[:, 7:8], dcol[:, 4:5], dcol[:, EM_:EM_ + 1], None, ALU.max).then_inc(s_dden_ready, 1)
                dve.wait_ge(s_dden_ready, 2 * h1 - 1)
                stt(dcol[:, 5:6], dcol[:, 4:5], -1.0, dcol[:, 7:8], ALU.mult, ALU.max).then_inc(s_dden_ready, 1)
                dve.wait_ge(s_dden_ready, 2 * h1)
                dve.reciprocal(dcol[:, 6:7], dcol[:, 5:6]).then_inc(s_dinv_ready, 1)
                dve.wait_ge(s_kT_taken, 4 * h1)
                dve.wait_ge(s_group_free[2], t0 + 6)
                dve.wait_ge(s_dinv_ready, h1)
                dve.tensor_scalar(rdiag[:, :], ident[0:ND, 0:ND], dcol[:, 6:7], None, ALU.mult).then_inc(s_dinv_diag, 1)

                with dve.Fori(0, NC) as c:
                    i1 = NC * h + c + 1
                    cc = bass.ds(L * c, L)
                    dve.tensor_copy(col[:, 0:4], cols[:, bass.ds(c, 1), :, bass.ds(h, 1)].rearrange("p c q h -> p (c q h)"))
                    dve.tensor_copy(col[:, 4:5], decays[:, bass.ds(c, 1), bass.ds(h, 1)].rearrange("p c h -> p (c h)"))\
                       .then_inc(s_col_set, 1)
                    dve.tensor_scalar(A_pick[:, :], A_row[:, cc], ident[0:4, bass.ds(h, 1)], None, ALU.mult)
                    dve.tensor_copy(qs[:, :, :], q_h[:, :, cc])
                    dve.tensor_copy(ks[:, :, :], k_h[:, :, cc])
                    dve.wait_ge(s_col_set, i1)
                    dve.tensor_scalar(kw[:, :], kw_all[:, bass.ds(c, 1), :].rearrange("p c n -> p (c n)"),
                                      col[:, WE_:WE_ + 1], None, ALU.mult).then_inc(s_staged, 1)
                    dve.wait_ge(s_scores_ready, i1)
                    dve.wait_ge(s_weights_ready, i1)
                    dve.tensor_tensor(SW[:, :], b_S[:, 0:L], SW[:, :], ALU.mult).then_inc(s_weighted_ready, 1)
                    dve.wait_ge(s_dstate_loaded, 32 * i1)
                    for k in range(2):
                        last = dve.tensor_scalar(dtmp[:, k, :], qkb[:, 256:512],
                                                 wv[:, k, bass.ds(c, 1)], None, ALU.mult)
                    last.then_inc(s_dkv_ready, 1)
                    dve.wait_ge(s_dkv_ready, i1)
                    stt(dC[:, :, :], dC[:, :, :],
                        dw[:, 1:2, bass.ds(c, 1), bass.ds(h, 1)].rearrange("p w b h -> p (w b h)"),
                        dtmp[:, :, :], ALU.mult, ALU.add).then_inc(s_dstate_new, 1)
                    dve.wait_ge(s_dstate_new, i1)
                    for k in range(2):
                        last = dve.tensor_tensor_reduce(out=dtmp[:, k, :], in0=dC[:, k, :], in1=qkb[:, 0:256], scale=1.0,
                                                        scalar=0.0, op0=ALU.mult, op1=ALU.add,
                                                        accum_out=den[:, 2 + k:3 + k])
                    last.then_inc(s_dstate_used, 1)
                    dve.wait_ge(s_dstate_used, i1)
                    dve.tensor_scalar(num_d[:, :, bass.ds(c, 1)].rearrange("p k b -> p (k b)"), den[:, 2:4], 1.0, None, ALU.mult)
                    dve.wait_ge(s_update_ready, i1)
                    stt(Cn[:, :, 0:256], Cn[:, :, 0:256], col[:, 4:5], b_U[:, :].rearrange("p (k n) -> p k n", k=2),
                        ALU.mult, ALU.add)
                    stt(Cn[:, :, 256], Cn[:, :, 256], col[:, 4:5], b_N[:, 260:262], ALU.mult, ALU.add).then_inc(s_C_new, 1)
                    dve.wait_ge(s_carried_scaled, i1)
                    dve.tensor_tensor(num[:, :], num[:, :], b_N[:, 0:257], ALU.add).then_inc(s_num_ready, 1)
                    dve.wait_ge(s_num_ready, i1)
                    dve.tensor_scalar(den[:, 0:1], num[:, 256:257], col[:, EM_:EM_ + 1], None, ALU.max).then_inc(s_den_max, 1)
                    dve.wait_ge(s_den_max, 2 * i1 - 1)
                    stt(den[:, 0:1], num[:, 256:257], -1.0, den[:, 0:1], ALU.mult, ALU.max).then_inc(s_den_max, 1)
                    dve.wait_ge(s_den_max, 2 * i1)
                    dve.reciprocal(den[:, 1:2], den[:, 0:1]).then_inc(s_den_inv, 1)
                    dve.wait_ge(s_den_inv, i1)
                    dve.tensor_scalar(num[:, 0:256], num[:, 0:256], den[:, 1:2], None, ALU.mult).then_inc(s_hn_ready, 1)
                    dve.wait_ge(s_hT_ready, i1)
                    dve.tensor_tensor(dtmp[:, :, 0:L], b_S[:, P:P + 256].rearrange("p (k l) -> p k l", k=2), o_h[:, :, cc],
                                      ALU.mult).then_inc(s_yv_ready, 1)
                    dve.wait_ge(s_yv_ready, i1)
                    dve.tensor_scalar(y_hi[:, :, cc], dtmp[:, :, 0:L], 1.0, None, ALU.mult).then_inc(s_yhi_ready, 1)
                    dve.wait_ge(s_yhi_ready, i1)
                    dve.tensor_tensor(y_lo[:, :, cc], dtmp[:, :, 0:L], y_hi[:, :, cc].bitcast(F32), ALU.subtract)\
                       .then_inc(s_ylo_ready, 1)
                dve.tensor_tensor(yd[:, :, :], num_d[:, :, :], o_h[:, :, T:N], ALU.mult).then_inc(s_dy_gated, 1)
                dve.wait_ge(s_dy_gated, h1)
                dve.wait_ge(s_dinv_all, h1)
                for k in range(2):
                    last = dve.tensor_tensor(yd[:, k, :], yd[:, k, :], b_U[:, 0:ND], ALU.mult)
                last.then_inc(s_dy_scaled, 1)
                dve.wait_ge(s_dy_scaled, h1)
                dve.tensor_scalar(y_hi[:, :, T:N], yd[:, :, :], 1.0, None, ALU.mult).then_inc(s_dy_hi, 1)
                dve.wait_ge(s_dy_hi, h1)
                dve.tensor_tensor(y_lo[:, :, T:N], yd[:, :, :], y_hi[:, :, T:N].bitcast(F32), ALU.subtract)\
                   .then_inc(s_dy_ready, 1)
                for j in range(8):
                    for g in range(NG):
                        dve.wait_ge(s_group_ready[g], t0 + 17 + j)
                        dve.tensor_tensor(acc[:, j, tok[g]], acc[:, j, tok[g]], bank[g][:, 0:G], ALU.add)\
                           .then_inc(s_group_free[g], 1)
                dve.wait_ge(s_C_stored, 16 * h1)

            dve.memset(u_pad[:, :, 0:16], 0.0)
            dve.memset(win_a[:, 0:16], 0.0)
            step(dve.memset(win_b[:, 0:16], 0.0))
            for t in range(15):
                dve.memset(inv_count[:, t:t + 1], 1.0 / (t + 1))

            def pool_lo(w):
                for g in range(NG):
                    dve.wait_ge(s_pool_hi, NG * w + g + 1)
                    stt(yp_lo[:, w, tok[g]], bank[g][:, 0:G], vcol(V_POOL + w), yp_hi[:, w, tok[g]].bitcast(F32),
                        ALU.mult, ALU.subtract).then_inc(s_group_free[g], 1)

            dve.wait_ge(s_pool_in_loaded, 32)
            for w in range(4):
                win = 2 << w
                u = u_pad[:, w, :]
                dve.wait_ge(s_side_loaded, 16 * 8)
                src = u
                for i in range(w + 1):
                    dst = (win_a, win_b)[i % 2]
                    step(dve.tensor_tensor(dst[:, 16:], src[:, 16:16 + N], src[:, 16 - (1 << i):16 + N - (1 << i)], ALU.add))
                    src = dst
                d = pool_d[:, w % 2, :]
                if w >= 2:
                    dve.wait_ge(s_group_ready[2], UNIT_POOL + w - 1)
                dve.tensor_reduce(sm[:, 0:ND], bufT[:, w, :, 15 - (win - 1):15], axis=AX.X, op=ALU.add)
                step(stt(d, src[:, 16:], 1.0 / win, u[:, 16:], ALU.mult, ALU.subtract))
                dve.tensor_tensor(sm[:, 0:ND], sm[:, 0:ND], u[:, 16 + T:], ALU.add)
                step(dve.tensor_tensor(d[:, 0:win - 1], src[:, 16:16 + win - 1], inv_count[:, 0:win - 1], ALU.mult))
                dve.tensor_tensor(d[:, 0:win - 1], d[:, 0:win - 1], u[:, 16:16 + win - 1], ALU.subtract)
                stt(d[:, T:N], sm[:, 0:ND], 1.0 / win, u[:, 16 + T:], ALU.mult, ALU.subtract).then_inc(s_pool_d_ready, 1)
                if w:
                    pool_lo(w - 1)
            po = win_a[:, 0:480].rearrange("p (k b j) -> p k b j", k=4, b=ND)
            for k in range(4):
                dve.tensor_copy(po[:, k, :, 0:14], bufT[:, k, :, 1:15])
            dve.tensor_copy(po[:, :, :, 14], u_pad[:, :, 16 + T:16 + N]).then_inc(s_pool_state_ready, 1)
            pool_lo(3)
            dve.wait_ge(s_group_free[2], UNIT_MERGE)
            dve.memset(sm[:, 15:16], 0.0).then_inc(s_pool_lo, 1)
            dve.wait_ge(s_dkeys_used, ND)
            dve.tensor_copy(P_sb[:, 0, 0:64], b_N[:, 0:64]).then_inc(s_dscores_taken, 1)
            dve.wait_ge(s_dscoresT_ready, 1)
            step(dve.tensor_reduce(sm[0:32, 8:9], b_U[0:32, 0:MEM], axis=AX.X, op=ALU.max))
            dve.tensor_scalar(sm[0:32, 9:10], sm[0:32, 8:9], -X_SCALE, None, ALU.mult).then_inc(s_dbias_ready, 1)
            dve.wait_ge(s_dexp_ready, 1)
            step(dve.reciprocal(sm[0:32, 11:12], sm[0:32, 10:11]))
            dve.tensor_scalar(P_sb[0:32, 1, :], P_sb[0:32, 1, :], sm[0:32, 11:12], None, ALU.mult).then_inc(s_dprob_ready, 1)
            dve.wait_ge(s_dprobT_ready, 1)
            dve.tensor_copy(P_sb[:, 2, 0:64], b_N[:, 0:64]).then_inc(s_dprobT_taken, 1)
            dve.wait_ge(s_dattn_hi, 1)
            dve.tensor_tensor(yx_lo[:, :, T:N], b_I[:, 0:32].rearrange("p (h b) -> p h b", h=4),
                              yx_hi[:, :, T:N].bitcast(F32), ALU.subtract).then_inc(s_dattn_lo, 1)
            with dve.Fori(0, NC) as c:
                cc = bass.ds(L * c, L)
                c1 = c + 1
                dve.tensor_copy(xs_t[:, :, :], xq[:, :, cc]).then_inc(s_xs_staged, 1)
                dve.wait_ge(s_xscores_ready, c1)
                for i in range(2):
                    last = dve.tensor_reduce(sm[:, 2 * i:2 * i + 2], (b_S, b_W)[i][:, :].rearrange("p (h m) -> p h m", h=2),
                                             axis=AX.X, op=ALU.max)
                last.then_inc(s_xmax_ready, 1)
                dve.wait_ge(s_xmax_ready, c1)
                dve.tensor_scalar(sm[:, 4:8], sm[:, 0:4], -X_SCALE, None, ALU.mult).then_inc(s_xbias_ready, 1)
                dve.wait_ge(s_xexp_ready, 4 * c1)
                dve.reciprocal(sm[:, 12:16], sm[:, 8:12]).then_inc(s_xinv_ready, 1)
                dve.wait_ge(s_xinv_ready, c1)
                for hh in range(4):
                    last = dve.tensor_scalar(P_sb[:, hh, :], P_sb[:, hh, :], sm[:, 12 + hh:13 + hh], None, ALU.mult)
                last.then_inc(s_xprob_ready, 1)
                dve.wait_ge(s_xprobT_ready, c1)
                dve.tensor_copy(PT_sb[:, 4:8, :], b_I[:, :].rearrange("p (i t) -> p i t", i=4)).then_inc(s_xprobT_taken, 1)
                dve.wait_ge(s_xo_ready, c1)
                o = b_U[:, :].rearrange("p (h t) -> p h t", h=4)
                dve.tensor_scalar(yx_hi[:, :, cc], o, 1.0, None, ALU.mult).then_inc(s_xo_hi, 1)
                dve.wait_ge(s_xo_hi, c1)
                dve.tensor_tensor(yx_lo[:, :, cc], o, yx_hi[:, :, cc].bitcast(F32), ALU.subtract).then_inc(s_xo_lo, 1)
            with dve.Fori(0, 8) as j:
                def a(g):
                    return acc[:, bass.ds(j, 1), tok[g]].rearrange("p a t -> p (a t)")
                i3 = NG * j
                for g in range(NG):
                    dve.wait_ge(s_g_sig, i3 + g + 1)
                    dve.tensor_tensor(a(g), a(g), gates[:, g, 1, :], ALU.mult).then_inc(s_acc_gated, 1)
                    dve.wait_ge(s_group_ready[g], UNIT_MERGE + 2 * j + 1)
                    dve.tensor_tensor(gates[:, g, 0, :], bank[g][:, 0:G], gates[:, g, 0, :], ALU.mult).then_inc(s_group_free[g], 1)
                for g in range(NG):
                    dve.wait_ge(s_acc_gated, i3 + g + 1)
                    dve.wait_ge(s_group_free[g], UNIT_MERGE + 2 * j + 1)
                    dve.tensor_tensor(a(g), a(g), gates[:, g, 0, :], ALU.add).then_inc(s_pool_added, 1)
                    dve.wait_ge(s_group_ready[g], UNIT_MERGE + 2 * j + 2)
                    dve.tensor_tensor(gates[:, g, 2, :], bank[g][:, 0:G], gates[:, g, 2, :], ALU.mult).then_inc(s_group_free[g], 1)
                    dve.wait_ge(s_group_free[g], UNIT_MERGE + 2 * j + 2)
                    dve.wait_ge(s_pool_added, i3 + g + 1)
                    dve.tensor_tensor(a(g), a(g), gates[:, g, 2, :], ALU.add).then_inc(s_merged, 1)
                for g in range(NG):
                    dve.wait_ge(s_merged_hi, i3 + g + 1)
                    hj = h_hi[:, bass.ds(j, 1), tok[g]].rearrange("p a t -> p (a t)")
                    lj = h_lo[:, bass.ds(j, 1), tok[g]].rearrange("p a t -> p (a t)")
                    dve.tensor_tensor(lj, a(g), hj.bitcast(F32), ALU.subtract).then_inc(s_merged_lo, 1)
            dve.wait_ge(s_group_ready[2], UNIT_OUT)
            for g in range(NG):
                dve.memset(rstd0b[:, tok[g]], 0.0).then_inc(s_z_acc, 1)
            with dve.Fori(0, 8) as j:
                for g in range(NG):
                    dve.wait_ge(s_group_free[g], UNIT_OUT + j + 1)
                    dve.wait_ge(s_z_acc, NG * j + g + 1)
                    dve.tensor_tensor(rstd0b[:, tok[g]], rstd0b[:, tok[g]], gates[:, g, 0, :], ALU.add).then_inc(s_z_acc, 1)
            for g in range(NG):
                dve.wait_ge(s_z_std, g + 1)
                step(dve.reciprocal(rstd0[:, tok[g]], rstd0b[:, tok[g]]))
                for k in range(KD):
                    dve.wait_ge(s_x2_loaded, 16)
                    stt(acc[:, k, tok[g]], acc[:, k, tok[g]], vcol(V_POST + k), rstd0[:, tok[g]], ALU.mult, ALU.mult)\
                        .then_inc(s_z_scaled, 1)
                for k in range(KD):
                    dve.wait_ge(s_z_scaled, g * KD + k + 1)
                    dve.tensor_tensor(x_in[:, k, tok[g]], x_in[:, k, tok[g]], acc[:, k, tok[g]], ALU.add).then_inc(s_x1_ready, 1)
            for g in range(NG):
                dve.wait_ge(s_x1_std, g + 1)
                step(dve.reciprocal(rstd0[:, tok[g]], rstd0b[:, tok[g]]))
                for k in range(KD):
                    stt(acc[:, k, tok[g]], x_in[:, k, tok[g]], vcol(V_MLP + k), rstd0[:, tok[g]], ALU.mult, ALU.mult)\
                        .then_inc(s_h2_ready, 1)
                for k in range(KD):
                    dve.wait_ge(s_h2_hi, g * KD + k + 1)
                    dve.tensor_tensor(h_lo[:, k, tok[g]], acc[:, k, tok[g]], h_hi[:, k, tok[g]].bitcast(F32), ALU.subtract)\
                        .then_inc(s_h2_lo, 1)
            dve.wait_ge(s_h2_lo, NG * KD)
            step(dve.memset(acc[:, :, :], 0.0))

            def ff1(t, half, count):
                for j in range(4):
                    for g in range(NG):
                        dve.wait_ge(s_group_free[g], t + j + 1)
                        dve.tensor_tensor(sqv[:, g, :], rl[:, g, :], rl[:, g, :], ALU.mult).then_inc(s_relu_squared, 1)
                        dve.wait_ge(s_f_hi, count + NG * j + g + 1)
                        dve.tensor_tensor(f_lo[:, half, j, tok[g]], sqv[:, g, :], f_hi[:, half, j, tok[g]].bitcast(F32),
                                          ALU.subtract).then_inc(s_f_lo, 1)

            def ff2(t):
                for j in range(8):
                    for g in range(NG):
                        dve.wait_ge(s_group_ready[g], t + j + 1)
                        dve.tensor_tensor(acc[:, j, tok[g]], acc[:, j, tok[g]], bank[g][:, 0:G], ALU.add)\
                           .then_inc(s_group_free[g], 1)

            ff1(UNIT_FF, 0, 0)
            with dve.Fori(0, 3) as i:
                t0 = UNIT_FF_LOOP + UNITS_PER_FF_STEP * i
                ff1(t0, 1, 24 * i + 12)
                ff2(t0 + 4)
                ff1(t0 + 12, 0, 24 * i + 24)
                ff2(t0 + 16)
            ff1(UNIT_FF_TAIL, 1, 84)
            ff2(UNIT_FF_TAIL + 4)
            ff2(UNIT_FF_TAIL + 12)
            for g in range(NG):
                dve.wait_ge(s_group_free[g], UNIT_FF_TAIL + 20)
            dve.memset(sm[:, 0:1], 0.0).then_inc(s_f_added, 192)
            for g in range(NG):
                dve.wait_ge(s_f_std, g + 1)
                step(dve.reciprocal(rstd0[:, tok[g]], rstd0b[:, tok[g]]))
            dve.wait_ge(s_x3_loaded, 16)
            for k in range(KD):
                stt(acc[:, k, :], acc[:, k, :], vcol(V_FF + k), rstd0[:, :], ALU.mult, ALU.mult).then_inc(s_y_scaled, 1)
                if k:
                    dve.wait_ge(s_y_scaled, k)
                    dve.tensor_tensor(x_in[:, k - 1, :], x_in[:, k - 1, :], acc[:, k - 1, :], ALU.add).then_inc(s_y_ready, 1)
            dve.wait_ge(s_y_scaled, KD)
            dve.tensor_tensor(x_in[:, KD - 1, :], x_in[:, KD - 1, :], acc[:, KD - 1, :], ALU.add).then_inc(s_y_ready, 1)


def lay_out(inputs):
    import numpy as np

    def feat(a):
        return a.T.reshape(KD, P, a.shape[0]).transpose(1, 0, 2)

    def slab(w):
        return w.reshape(-1, P, w.shape[1]).transpose(1, 0, 2).reshape(P, 1024)

    def vector(v):
        return v.reshape(-1, P).T

    x = np.concatenate([inputs["x_prompt"][0], inputs["x_sample"][:, 0]], axis=0)
    w_in = inputs["w_in"][0]
    q0, k0, v0, o0 = (512 + 1024 * i for i in range(4))
    gif = np.zeros((D, P), np.float32)
    gif[:, 0:4] = w_in[:, 4608:4612]
    gif[:, 32:36] = w_in[:, 4612:4616]
    slabs = [slab(inputs["w_mem_kv"][0][:, P * j:P * (j + 1)]) for j in range(8)] + [slab(gif)]
    side = [P * j for j in range(4)] + [4616 + P * j for j in range(28)]
    for h in range(HEADS):
        for c0 in (v0, q0, k0, o0):
            slabs += [slab(w_in[:, c0 + 256 * h + P * i:c0 + 256 * h + P * (i + 1)]) for i in range(2)]
        slabs += [slab(w_in[:, side[8 * h + c]:side[8 * h + c] + P]) for c in range(8)]
        slabs += [slab(inputs["w_br_mlstm"][0][256 * h:256 * (h + 1), 512 * i:512 * (i + 1)]) for i in range(2)]
    for j in range(8):
        slabs.append(slab(np.concatenate([inputs["w_br_pool"][0][:, P * j:P * (j + 1)],
                                          inputs["w_br_xattn"][0][:, P * j:P * (j + 1)]], axis=0)))
    slabs += [slab(inputs["w_out"][0][:, P * j:P * (j + 1)]) for j in range(8)]

    def ff1(c):
        return [slab(inputs["w_ff1"][0][:, 512 * c + P * j:512 * c + P * (j + 1)]) for j in range(4)]

    def ff2(c):
        return [slab(inputs["w_ff2"][0][512 * c:512 * (c + 1), 256 * j:256 * (j + 1)]) for j in range(4)]
    slabs += ff1(0)
    for c in range(7):
        slabs += ff1(c + 1) + ff2(c)
    slabs += ff2(7)
    return {
        "w_stream": np.stack(slabs),
        "xT": feat(x), "memT": feat(inputs["mem_prompt"][0]),
        "vecs": np.concatenate([vector(inputs[n][0]) for n in ("g_pre_mix", "g_mem", "g_post_mix", "g_pre_mlp",
                                                                "g_post_mlp", "pool_scale")], axis=1),
        "b_if": inputs["b_if"][0].reshape(2, 4).T,
        "w_pool": inputs["w_pool"][0].transpose(1, 0, 2),
        "poolbuf": inputs["state_pool_buf"][0].transpose(2, 0, 1).reshape(4, P, ND, 15).transpose(1, 0, 2, 3),
        "stC": inputs["state_mlstm_C"][0].reshape(ND, 4, 2, P, 256).transpose(1, 0, 3, 2, 4),
        "stn": inputs["state_mlstm_n"][0].reshape(ND, 1024),
        "stm": inputs["state_mlstm_m"][0].T,
        "ckT": inputs["cache_mem_k"][0].transpose(0, 3, 2, 1),
        "cv": inputs["cache_mem_v"][0].reshape(ND, 2, P, 512).transpose(0, 2, 1, 3),
    }


def kernel(**inputs):
    import numpy as np
    import concourse.bacc as bacc
    from concourse.bass_utils import run_bass_kernel_spmd

    nc = bacc.Bacc("TRN2", target_bir_lowering=False, num_devices=1)
    arrays, args = {}, []
    for name, a in lay_out({n: np.asarray(v) for n, v in inputs.items()}).items():
        arrays[name] = np.ascontiguousarray(a)
        args.append(nc.dram_tensor(name, a.shape, F32, kind="ExternalInput").ap())
    outs = {"o_y": (P, KD, N), "o_pool": (P, 4, 15), "o_C": (4, P, 2, 257), "o_m": (4, 1 + ND), "o_kv": (P, 8, MEM),
            "o_pool_s": (P, 480), "o_C_s": (4, ND, P, 2, 256), "o_n_s": (ND, 1024)}
    for name, shape in outs.items():
        args.append(nc.dram_tensor(name, shape, F32, kind="ExternalOutput").ap())
    for name, shape in (("d_side", (FILL, P, N)), ("d_x1", (P, KD, N)), ("d_qk", (4, ND, 512)), ("d_v", (P, 2, 512))):
        args.append(nc.dram_tensor(name, shape, F32, kind="Internal").ap())
    hybrid_layer(nc, *args)
    r = run_bass_kernel_spmd(nc, [arrays], core_ids=[0]).results[0]
    y = r["o_y"].transpose(1, 0, 2).reshape(D, N).T
    pool_p = r["o_pool"].transpose(2, 1, 0).reshape(1, 1, 15, 512)
    C_p = r["o_C"][:, :, :, 0:256].transpose(0, 3, 2, 1).reshape(1, 1, 4, 256, 256)
    n_p = r["o_C"][:, :, :, 256].transpose(0, 2, 1).reshape(1, 1, 4, 256)
    kv = r["o_kv"].transpose(1, 0, 2).reshape(1024, MEM).T
    pool_s = r["o_pool_s"].reshape(P, 4, ND, 15).transpose(2, 3, 1, 0).reshape(1, ND, 15, 512)
    C_s = r["o_C_s"].transpose(1, 0, 3, 2, 4).reshape(1, ND, 4, 256, 256)
    out = (y[0:T].reshape(1, T, D), y[T:].reshape(ND, 1, D), pool_p, C_p, n_p, r["o_m"][:, 0].reshape(1, 1, 4),
           kv[:, 0:512].reshape(1, 1, MEM, 4, P), kv[:, 512:].reshape(1, 1, MEM, 4, P),
           pool_s, C_s, r["o_n_s"].reshape(1, ND, 4, 256), r["o_m"][:, 1:].T.reshape(1, ND, 4))
    return tuple(np.ascontiguousarray(a) for a in out)
```

```python
import concourse.bass as bass
from concourse import mybir
from contextlib import ExitStack

F32 = mybir.dt.float32
F32R = mybir.dt.float32r
BF16 = mybir.dt.bfloat16
ACT = mybir.ActivationFunctionType
ALU = mybir.AluOpType
AX = mybir.AxisListType

P = 128
D = 1024
T = 1024
ND = 8
N = T + ND
NG = 3
G = N // NG
KD = D // P
HEADS = 4
L = 128
NC = T // L
MEM = 256
FILL = 32
EPS = 1e-6
MASKED = -1e30
K_SCALE = 1.0 / 16.0
X_SCALE = float(128) ** -0.5

SLAB_GATE = 8
SLAB_HEAD = 9
SLABS_PER_HEAD = 18
SLAB_MERGE = SLAB_HEAD + HEADS * SLABS_PER_HEAD
SLAB_OUT = SLAB_MERGE + 8
SLAB_FF = SLAB_OUT + 8
SLABS = SLAB_FF + 64

UNIT_HEAD = 1
UNITS_PER_HEAD = 24
UNIT_POOL = UNIT_HEAD + HEADS * UNITS_PER_HEAD
UNIT_MERGE = UNIT_POOL + 4
UNIT_OUT = UNIT_MERGE + 16
UNIT_FF = UNIT_OUT + 8
UNIT_FF_LOOP = UNIT_FF + 4
UNITS_PER_FF_STEP = 24
UNIT_FF_TAIL = UNIT_FF_LOOP + 3 * UNITS_PER_FF_STEP
V_PRE, V_MEM, V_POST, V_MLP, V_FF, V_POOL = 0, 8, 16, 24, 32, 40
B_, WI_, WE_, EM_ = range(4)


def hybrid_layer(nc, w_stream, xT, memT, vecs, b_if, w_pool, poolbuf, stC, stn, stm, ckT, cv,
                 o_y, o_pool, o_C, o_m, o_kv, o_pool_s, o_C_s, o_n_s,
                 d_side, d_x1, d_qk, d_v):
    with ExitStack() as ctx:
        def sb(name, shape, dt=F32):
            return ctx.enter_context(nc.sbuf_tensor(name, shape, dt))

        def overlap(*groups):
            sizes = []
            made = []
            for group in groups:
                with ExitStack() as own:
                    made.append([own.enter_context(nc.sbuf_tensor(n, s, d)) for n, s, d in group])
                size = 0
                for _, s, d in group:
                    b = 2 if d == BF16 else 4
                    for e in s[1:]:
                        b *= e
                    size += -(-b // 32) * 32
                sizes.append(size)
            ctx.enter_context(nc.sbuf_tensor(f"room_{groups[0][0][0]}", [P, max(sizes) // 4], F32))
            return made

        (h_hi, h_lo), (u_pad, xq, kv_in, v_in, P_sb, PT_sb, cache_t, xs_t,
                          dec_scores, dec_exp, dec_probs, dec_out) = overlap(
            [("h_hi", [P, KD, N], F32R), ("h_lo", [P, KD, N], F32R)],
            [("u_pad", [P, 4, 16 + N], F32), ("xq", [P, 4, N], F32), ("kv_in", [P, 4, MEM], F32),
             ("v_in", [P, 2, 512], F32), ("P_sb", [P, 4, MEM], F32), ("PT_sb", [P, 8, P], F32),
             ("cache_t", [P, 2, 4 * MEM], F32), ("xs_t", [P, 4, P], F32), ("dec_scores", [P, 64], F32),
             ("dec_exp", [32, MEM], F32), ("dec_probs", [P, 64], F32),
             ("dec_out", [P, 4, ND], F32)])
        (acc,), (kvT, v_tok, m_hi, m_lo), (R, gf, gi, lf, bb, mm_, tg, wi_diag, mprev, wsel) = overlap(
            [("acc", [P, KD, N], F32)],
            [("kvT", [P, 8, MEM], F32), ("v_tok", [P, 2, 512], F32),
             ("m_hi", [P, KD, MEM], F32R), ("m_lo", [P, KD, MEM], F32R)],
            [("R", [P, N], F32), ("gf", [4, N], F32), ("gi", [4, N], F32), ("lf", [4, N], F32),
             ("bb", [4, N], F32), ("mm_", [4, N], F32), ("tg", [4, N], F32), ("wi_diag", [4, NC + 2 * ND, 4], F32), ("mprev", [4, NC + 1], F32),
             ("wsel", [4, NC + 2 * ND], F32)])
        ((q_h, k_h, kw_all, v_all, o_h, y_hi, y_lo, side_t, qs, ks, kw, SW, Cn, num,
          dC, qkb, dtmp, ns),
         (x_in, mem_in, rstd0, rstd0b, sq0),
         (yp_hi, yp_lo, yx_hi, yx_lo, gates),
         (_p0, _p1, win_a, win_b, pool_d, inv_count, bufT, wp),
         (f_hi, f_lo, rl, sqv)) = overlap(
            [("q_h", [P, 2, N], F32), ("k_h", [P, 2, N], F32), ("kw_all", [P, NC, 256], F32),
             ("v_all", [P, NC, 257], F32), ("o_h", [P, 2, N], F32), ("y_hi", [P, 2, N], F32R),
             ("y_lo", [P, 2, N], F32R), ("side_t", [P, N], F32), ("qs", [P, 2, L], F32),
             ("ks", [P, 2, L], F32), ("kw", [P, 256], F32), ("SW", [P, L], F32),
             ("Cn", [P, 2, 257], F32), ("num", [P, 257], F32),
             ("dC", [P, 2, 256], F32), ("qkb", [P, 512], F32), ("dtmp", [P, 2, 256], F32), ("ns", [ND, 1024], F32)],
            [("x_in", [P, KD, N], F32), ("mem_in", [P, KD, MEM], F32), ("rstd0", [P, N], F32),
             ("rstd0b", [P, N], F32), ("sq0", [P, 2, N], F32)],
            [("yp_hi", [P, 4, N], F32R), ("yp_lo", [P, 4, N], F32R), ("yx_hi", [P, 4, N], F32R),
             ("yx_lo", [P, 4, N], F32R), ("gates", [P, NG, 3, G], F32)],
            [("_p0", [P, 4, N], F32R), ("_p1", [P, 4, N], F32R), ("win_a", [P, 16 + N], F32),
             ("win_b", [P, 16 + N], F32), ("pool_d", [P, 2, N], F32), ("inv_count", [P, 16], F32),
             ("bufT", [P, 4, ND, 15], F32), ("wp", [P, 4, P], F32)],
            [("f_hi", [P, 2, 4, N], F32R), ("f_lo", [P, 2, 4, N], F32R), ("rl", [P, NG, G], F32),
             ("sqv", [P, NG, G], F32)])
        w_raw = sb("w_raw", [P, 2, 1024])
        w_hi = sb("w_hi", [P, 2, 1024], F32R)
        w_lo = sb("w_lo", [P, 2, 1024], F32R)
        vec = sb("vec", [P, 44])
        bif = sb("bif", [4, 2])
        ident = sb("ident", [P, P])
        ident_b = sb("ident_b", [P, P], BF16)
        mask_b = sb("mask_b", [P, P], BF16)
        ones = sb("ones", [P, P])
        eps = sb("eps", [P, 1])
        A_row = sb("A_row", [4, N])
        A_pick = sb("A_pick", [4, L])
        cols = sb("cols", [P, NC + 1, 4, 4])
        col = sb("col", [P, 5])
        decays = sb("decays", [P, NC, 4])
        dw = sb("dw", [P, 2, ND, 4])
        m_out = sb("m_out", [4, 1 + ND])
        m0 = sb("m0", [4, ND])
        wv = sb("wv", [P, 2, ND])
        qkd = sb("qkd", [ND, 512])
        dcol = sb("dcol", [ND, 8])
        rdiag = sb("rdiag", [ND, ND])
        num_d = sb("num_d", [P, 2, ND])
        yd = sb("yd", [P, 2, ND])
        den = sb("den", [P, 4])
        sm = sb("sm", [P, 16])

        bank = [ctx.enter_context(nc.psum_tensor(f"bank{i}", [P, 512], F32)) for i in range(8)]
        b_S, b_W, b_N, b_I, b_U = bank[3:8]

        def sem(name):
            return ctx.enter_context(nc.semaphore(name))

        s_consts = sem("consts")
        s_masks = sem("masks")
        s_const_loaded = sem("const_loaded")
        s_mem_loaded = sem("mem_loaded")
        s_slab_split = sem("slab_split")
        s_mem_sq = sem("mem_sq")
        s_mem_ssq = sem("mem_ssq")
        s_mem_std = sem("mem_std")
        s_mem_h = sem("mem_h")
        s_mem_hi = sem("mem_hi")
        s_mem_lo = sem("mem_lo")
        s_mem_ready = sem("mem_ready")
        s_mem_taken = sem("mem_taken")
        s_memv_t = sem("memv_t")
        s_memv_taken = sem("memv_taken")
        s_kv_stored = sem("kv_stored")
        s_x_sq = sem("x_sq")
        s_x_sq_used = sem("x_sq_used")
        s_x_std = sem("x_std")
        s_x_h = sem("x_h")
        s_x_hi = sem("x_hi")
        s_x_lo = sem("x_lo")
        s_gate_row = sem("gate_row")
        s_gate_act = sem("gate_act")
        s_rows_ready = sem("rows_ready")
        s_table_t = sem("table_t")
        s_bcast_ready = sem("bcast_ready")
        s_vT_ready = sem("vT_ready")
        s_vT_taken = sem("vT_taken")
        s_kT_ready = sem("kT_ready")
        s_kT_taken = sem("kT_taken")
        s_dqk_ready = sem("dqk_ready")
        s_dqk_taken = sem("dqk_taken")
        s_dqk_stored = sem("dqk_stored")
        s_col_set = sem("col_set")
        s_staged = sem("staged")
        s_scores_ready = sem("scores_ready")
        s_logw_ready = sem("logw_ready")
        s_weights_ready = sem("weights_ready")
        s_weighted_ready = sem("weighted_ready")
        s_carried_ready = sem("carried_ready")
        s_update_ready = sem("update_ready")
        s_carried_scaled = sem("carried_scaled")
        s_num_ready = sem("num_ready")
        s_den_max = sem("den_max")
        s_den_inv = sem("den_inv")
        s_hn_ready = sem("hn_ready")
        s_hT_ready = sem("hT_ready")
        s_yv_ready = sem("yv_ready")
        s_yhi_ready = sem("yhi_ready")
        s_ylo_ready = sem("ylo_ready")
        s_C_new = sem("C_new")
        s_dstate_loaded = sem("dstate_loaded")
        s_dstate_used = sem("dstate_used")
        s_dstate_stored = sem("dstate_stored")
        s_dkv_ready = sem("dkv_ready")
        s_spilled = sem("spilled")
        s_dwk_ready = sem("dwk_ready")
        s_dn_new = sem("dn_new")
        s_ddot_ready = sem("ddot_ready")
        s_dden_ready = sem("dden_ready")
        s_dinv_ready = sem("dinv_ready")
        s_dinv_diag = sem("dinv_diag")
        s_dinv_all = sem("dinv_all")
        s_dy_gated = sem("dy_gated")
        s_dy_scaled = sem("dy_scaled")
        s_dy_hi = sem("dy_hi")
        s_dy_ready = sem("dy_ready")
        s_C_stored = sem("C_stored")
        s_wv_ready = sem("wv_ready")
        s_n_stored = sem("n_stored")
        s_dve_step = sem("dve_step")
        s_dstate_new = sem("dstate_new")
        s_u_loaded = sem("u_loaded")
        s_xq_loaded = sem("xq_loaded")
        s_pool_state_ready = sem("pool_state_ready")
        s_pool_d_ready = sem("pool_d_ready")
        s_pool_in_loaded = sem("pool_in_loaded")
        s_pool_hi = sem("pool_hi")
        s_pool_stored = sem("pool_stored")
        s_kv_loaded = sem("kv_loaded")
        s_xs_staged = sem("xs_staged")
        s_xscores_ready = sem("xscores_ready")
        s_xmax_ready = sem("xmax_ready")
        s_xbias_ready = sem("xbias_ready")
        s_xexp_ready = sem("xexp_ready")
        s_xinv_ready = sem("xinv_ready")
        s_xprob_ready = sem("xprob_ready")
        s_xprobT_ready = sem("xprobT_ready")
        s_xprobT_taken = sem("xprobT_taken")
        s_xo_ready = sem("xo_ready")
        s_xo_hi = sem("xo_hi")
        s_xo_lo = sem("xo_lo")
        s_dscores_taken = sem("dscores_taken")
        s_dscoresT_ready = sem("dscoresT_ready")
        s_dexp_ready = sem("dexp_ready")
        s_dprob_ready = sem("dprob_ready")
        s_dprobT_ready = sem("dprobT_ready")
        s_dprobT_taken = sem("dprobT_taken")
        s_dattn_hi = sem("dattn_hi")
        s_dattn_lo = sem("dattn_lo")
        s_dkeys_used = sem("dkeys_used")
        s_dvalues_used = sem("dvalues_used")
        s_dvalues_taken = sem("dvalues_taken")
        s_g_sig = sem("g_sig")
        s_xg_sig = sem("xg_sig")
        s_acc_gated = sem("acc_gated")
        s_pool_added = sem("pool_added")
        s_merged = sem("merged")
        s_merged_hi = sem("merged_hi")
        s_merged_lo = sem("merged_lo")
        s_z_evac = sem("z_evac")
        s_z_acc = sem("z_acc")
        s_z_ssq = sem("z_ssq")
        s_z_std = sem("z_std")
        s_x2_loaded = sem("x2_loaded")
        s_z_scaled = sem("z_scaled")
        s_x1_ready = sem("x1_ready")
        s_x1_sq = sem("x1_sq")
        s_x1_ssq = sem("x1_ssq")
        s_x1_std = sem("x1_std")
        s_x1_stored = sem("x1_stored")
        s_h2_ready = sem("h2_ready")
        s_h2_hi = sem("h2_hi")
        s_h2_lo = sem("h2_lo")
        s_relu_squared = sem("relu_squared")
        s_f_hi = sem("f_hi")
        s_f_lo = sem("f_lo")
        s_f_added = sem("f_added")
        s_f_squared = sem("f_squared")
        s_f_ssq = sem("f_ssq")
        s_f_std = sem("f_std")
        s_x3_loaded = sem("x3_loaded")
        s_y_scaled = sem("y_scaled")
        s_y_ready = sem("y_ready")
        s_y_stored = sem("y_stored")
        s_hi_made = sem("hi_made")
        s_x_loaded = [sem(f"x_loaded{i}") for i in range(2)]
        s_slab_loaded = [sem(f"slab_loaded{i}") for i in range(2)]
        s_g_loaded = [sem(f"g_loaded{i}") for i in range(3)]
        s_xg_loaded = [sem(f"xg_loaded{i}") for i in range(2)]
        s_cache_loaded = [sem(f"cache_loaded{i}") for i in range(2)]
        s_group_ready = [sem(f"group_ready{i}") for i in range(3)]
        s_group_free = [sem(f"group_free{i}") for i in range(3)]
        block = ctx.enter_context(nc.Block())
        tok = [slice(g * G, (g + 1) * G) for g in range(NG)]

        def sq_ring(i):
            return sq0[:, i // 2, (i % 2) * G:(i % 2 + 1) * G]

        @block.sync
        def _(sp):
            def slab(n, slot, split):
                if split is not None:
                    sp.wait_ge(s_slab_split, split)
                src = w_stream[n] if isinstance(n, int) else w_stream[bass.ds(n, 1)].rearrange("a p c -> (a p) c")
                sp.dma_start(w_raw[:, slot, :], src).then_inc(s_slab_loaded[slot], 16)

            sp.dma_start(mem_in[:, :, :], memT).then_inc(s_mem_loaded, 16)
            slab(0, 0, None)
            slab(1, 1, None)
            sp.dma_start(vec[:, :], vecs).then_inc(s_const_loaded, 16)
            sp.dma_start(bif[:, :], b_if).then_inc(s_const_loaded, 16)
            sp.dma_start(m0[:, :], stm).then_inc(s_const_loaded, 16)
            sp.dma_start(ns[:, :], stn).then_inc(s_const_loaded, 16)
            for i in range(2):
                sp.dma_start(x_in[:, 4 * i:4 * i + 4, :], xT[:, 4 * i:4 * i + 4, :]).then_inc(s_x_loaded[i], 16)
            for n in range(2, SLAB_HEAD + 2):
                slab(n, n % 2, n - 1)
            with sp.Fori(0, HEADS) as h:
                for j in range(2, 10):
                    slab(SLAB_HEAD + SLABS_PER_HEAD * h + j, (SLAB_HEAD + j) % 2,
                         SLAB_HEAD + SLABS_PER_HEAD * h + j - 1)
                with sp.Fori(0, NC // 2) as c2:
                    for e in range(2):
                        c = 2 * c2 + e
                        sp.wait_ge(s_dqk_stored, 16 * (h + 1))
                        sp.dma_start(dC[:, :, :], stC[bass.ds(h, 1), bass.ds(c, 1)].rearrange("a b p k c -> (a b p) k c"))\
                            .then_inc(s_dstate_loaded, 16)
                        sp.dma_start(qkb[:, :], d_qk[bass.ds(h, 1), bass.ds(c, 1)].rearrange("a b n -> (a b) n")
                                     .to_broadcast([P, 512])).then_inc(s_dstate_loaded, 16)
                        sp.wait_ge(s_dstate_used, NC * h + c + 1)
                        sp.dma_start(o_C_s[bass.ds(h, 1), bass.ds(c, 1)].rearrange("a b p k c -> (a b p) k c"), dC[:, :, :])\
                            .then_inc(s_dstate_stored, 16)
                        sp.wait_ge(s_dstate_stored, 16 * (NC * h + c + 1))
                        n = SLAB_HEAD + SLABS_PER_HEAD * h + 10 + c
                        slab(n, (SLAB_HEAD + e) % 2, n - 1)
                for j in range(2):
                    n = SLAB_HEAD + SLABS_PER_HEAD * (h + 1) + j
                    slab(n, (SLAB_HEAD + j) % 2, n - 1)
            sp.wait_ge(s_spilled, 16 * (FILL + 1))
            sp.wait_ge(s_group_ready[2], UNIT_HEAD + UNITS_PER_HEAD * (HEADS - 1) + 16)
            for k in range(4):
                sp.dma_start(u_pad[:, k, 16:16 + N], d_side[k]).then_inc(s_u_loaded, 16)
            for k in range(4):
                sp.dma_start(xq[:, k, :], d_side[4 + k]).then_inc(s_xq_loaded, 16)

            def cache(b, slot, values):
                src = (cv if values else ckT)[bass.ds(b, 1)].rearrange("a p k c -> (a p) (k c)")
                sp.dma_start(cache_t[:, slot, :], src).then_inc(s_cache_loaded[slot], 16)
            cache(0, 0, False)
            cache(1, 1, False)
            sp.dma_start(kv_in[:, :, :], o_kv[:, 0:4, :]).then_inc(s_kv_loaded, 16)
            sp.dma_start(v_in[:, :, :], d_v).then_inc(s_kv_loaded, 16)
            sp.wait_ge(s_group_ready[2], UNIT_POOL)
            sp.dma_start(bufT[:, :, :, :], poolbuf).then_inc(s_pool_in_loaded, 16)
            sp.dma_start(wp[:, :, :], w_pool).then_inc(s_pool_in_loaded, 16)
            with sp.Fori(1, ND // 2) as b2:
                for e in range(2):
                    sp.wait_ge(s_dkeys_used, 2 * b2 + e - 1)
                    cache(2 * b2 + e, e, False)
            sp.wait_ge(s_n_stored, 32)
            sp.wait_ge(s_C_stored, 64)

            def pool_gates(j):
                for g in range(NG):
                    if not isinstance(j, int) or j:
                        sp.wait_ge(s_pool_added, NG * (j - 1) + g + 1)
                    sp.dma_start(gates[:, g, 0:2, :], d_side[bass.ds(8 + 3 * j, 2), :, tok[g]].rearrange("b p t -> p b t"))\
                        .then_inc(s_g_loaded[g], 16)

            def attention_gates(j):
                sp.dma_start(gates[:, :, (2, 0)[j % 2], :], d_side[8 + 3 * j + 2].rearrange("p (g t) -> p g t", g=NG))\
                    .then_inc(s_xg_loaded[j % 2], 16)

            def m_slab(i):
                slab(SLAB_MERGE + i, (SLAB_MERGE + i) % 2, SLAB_MERGE + i - 1)
            pool_gates(0)
            for e in range(2):
                sp.wait_ge(s_dkeys_used, ND - 1 + e)
                cache(e, e, True)
            m_slab(2)
            m_slab(3)
            attention_gates(0)
            for c in range(NC):
                if c + 2 < ND:
                    sp.wait_ge(s_dvalues_used, c + 1)
                    cache(c + 2, c % 2, True)
                if c + 1 < NC:
                    pool_gates(c + 1)
                if c % 2:
                    m_slab(4 + c // 2)
            for j in range(1, 8):
                if j == 1:
                    sp.wait_ge(s_pool_added, NG * 8)
                else:
                    sp.wait_ge(s_merged, NG * (j - 1))
                attention_gates(j)
                if j % 2 == 0:
                    m_slab(7 + j // 2)
            m_slab(11)
            sp.wait_ge(s_merged_lo, 24)
            sp.wait_ge(s_group_ready[2], UNIT_OUT)
            sp.dma_start(x_in[:, :, :], xT).then_inc(s_x2_loaded, 16)
            with sp.Fori(SLAB_MERGE + 12, SLABS - 1, 2) as n:
                slab(n, (SLAB_MERGE + 12) % 2, n - 1)
                slab(n + 1, (SLAB_MERGE + 13) % 2, n)
            sp.wait_ge(s_f_added, 24 * 8)
            sp.wait_ge(s_x1_stored, 16)
            sp.dma_start(x_in[:, :, :], d_x1).then_inc(s_x3_loaded, 16)
            for k in range(KD):
                sp.wait_ge(s_y_ready, k + 1)
                sp.dma_start(o_y[:, k, :], x_in[:, k, :]).then_inc(s_y_stored, 16)
            sp.wait_ge(s_y_stored, 16 * KD)

        @block.gpsimd
        def _(pool):
            for tile_, value in ((ident, 0.0), (ident_b, 0.0), (mask_b, 0.0), (ones, 1.0), (eps, EPS)):
                pool.memset(tile_[:, :], value).then_inc(s_consts, 1)
            pool.wait_ge(s_consts, 5)
            for tile_ in (ident, ident_b):
                pool.affine_select(out=tile_[:, :], in_=tile_[:, :], compare_op=ALU.not_equal, fill=1.0, base=0,
                                   pattern=[[-1, P]], channel_multiplier=1).then_inc(s_masks, 1)
            pool.affine_select(out=mask_b[:, :], in_=mask_b[:, :], compare_op=ALU.is_ge, fill=MASKED, base=0,
                               pattern=[[1, P]], channel_multiplier=-1).then_inc(s_masks, 1)

            def split(n, slot, used=None):
                pool.wait_ge(s_slab_loaded[slot], 16 * (n // 2 + 1) if isinstance(n, int) else 8 * (n - slot) + 16)
                if used is not None:
                    pool.wait_ge(*used)
                pool.tensor_tensor(w_hi[:, slot, :], w_raw[:, slot, :], ones[:, 0:1].to_broadcast([P, 1024]), ALU.mult).then_inc(s_hi_made, 1)
                pool.wait_ge(s_hi_made, n + 1)
                pool.tensor_tensor(w_lo[:, slot, :], w_raw[:, slot, :], w_hi[:, slot, :].bitcast(F32), ALU.subtract)\
                    .then_inc(s_slab_split, 1)

            for n in range(SLAB_HEAD + 2):
                if n < 2:
                    split(n, n % 2)
                elif n < SLAB_HEAD + 1:
                    split(n, n % 2, (s_mem_ready, n - 1))
                else:
                    split(n, n % 2, (s_group_ready[2], 1))
            with pool.Fori(0, HEADS) as h:
                for j in range(2, SLABS_PER_HEAD + 2):
                    d = j - 2
                    units = d + 1 if d < 16 else 20 + 4 * (d - 16)
                    split(SLAB_HEAD + SLABS_PER_HEAD * h + j, (SLAB_HEAD + j) % 2,
                          (s_group_ready[2], UNIT_HEAD + UNITS_PER_HEAD * h + units))

            def split_merge(j):
                d = j - 2
                units = UNIT_MERGE + 2 * (d + 1) if d < 8 else UNIT_OUT + d - 7
                split(SLAB_MERGE + j, (SLAB_MERGE + j) % 2, (s_group_ready[2], units))
            pool.wait_ge(s_xq_loaded, 64)
            for c in range(NC):
                pool.wait_ge(s_xbias_ready, c + 1)
                pool.tensor_copy(xs_t[:, :, :], xq[:, :, c * L:(c + 1) * L]).then_inc(s_xs_staged, 1)
                if c >= 2 and c % 2 == 0:
                    split_merge(1 + c // 2)
            for j in range(5, 20):
                split_merge(j)
            done = [0, 1] + [1, 2, 3, 4] + [6, 8, 10, 12] + [13, 14, 15, 16] + [18, 20]
            done[0] = -1
            done[1] = 0
            with pool.Fori(0, 3) as i:
                for j in range(16):
                    split(SLAB_FF + 4 + 16 * i + j, (SLAB_FF + j) % 2,
                          (s_group_ready[2], UNIT_FF_LOOP + UNITS_PER_FF_STEP * i + done[j]))
            tail = [-1, 0, 1, 2, 3, 4, 6, 8, 10, 12, 14, 16]
            for j in range(12):
                n = SLAB_FF + 52 + j
                split(n, n % 2, (s_group_ready[2], UNIT_FF_TAIL + tail[j]))

        @block.tensor
        def _(pe):
            def product(out, blocks, passes3=True):
                n = 3 * len(blocks) if passes3 else len(blocks)
                i = 0
                for b in blocks:
                    for st, mv in (((b[0], b[2]), (b[1], b[2]), (b[0], b[3])) if passes3 else (b,)):
                        last = pe.matmul(out, st, mv, start=i == 0, stop=i == n - 1)
                        i += 1
                return last

            def group(g, t, blocks, passes3=True):
                if not (isinstance(t, int) and t == 0):
                    pe.wait_ge(s_group_free[g], t)
                product(bank[g][:, 0:G], blocks, passes3).then_inc(s_group_ready[g], 1)

            def w_blocks(slot, count, width, col0):
                return [(w_hi[:, slot, k * width + col0:k * width + col0 + P],
                         w_lo[:, slot, k * width + col0:k * width + col0 + P]) for k in range(count)]

            def h_group(slot, g, t):
                group(g, t, [(a, b, h_hi[:, k, tok[g]], h_lo[:, k, tok[g]])
                             for k, (a, b) in enumerate(w_blocks(slot, KD, P, 0))])

            def h_unit(n, slot, t):
                pe.wait_ge(s_slab_split, n + 1)
                for g in range(NG):
                    h_group(slot, g, t)

            def mean_square(out_banks, sq, used):
                for k in range(KD):
                    pe.wait_ge(sq, k + 1)
                    for g in range(NG):
                        last = pe.matmul(out_banks[g][:, 0:G], ones[:, :], sq0[:, k % 2, tok[g]], start=k == 0, stop=k == 7)
                    last.then_inc(used, 1)

            pe.wait_ge(s_consts, 5)
            pe.wait_ge(s_masks, 3)
            pe.wait_ge(s_mem_sq, 1)
            for k in range(KD):
                last = pe.matmul(b_U[:, 0:MEM], ones[:, :], kvT[:, k, :], start=k == 0, stop=k == 7)
            last.then_inc(s_mem_ssq, 1)
            mean_square((b_S, b_W, b_N), s_x_sq, s_x_sq_used)
            pe.wait_ge(s_mem_lo, 1)
            for n in range(8):
                pe.wait_ge(s_slab_split, n + 1)
                if n >= 2:
                    pe.wait_ge(s_mem_taken, n - 1)
                product((b_I, b_U)[n % 2][:, 0:MEM], [(a, b, m_hi[:, k, :], m_lo[:, k, :])
                        for k, (a, b) in enumerate(w_blocks(n % 2, KD, P, 0))]).then_inc(s_mem_ready, 1)
            pe.wait_ge(s_mem_taken, 8)
            for m in range(2):
                for j in range(4):
                    last = pe.transpose((b_I, b_U)[m][:, j * P:(j + 1) * P], kvT[:, 4 + j, m * P:(m + 1) * P], ident[:, :])
                last.then_inc(s_memv_t, 1)
            pe.wait_ge(s_slab_split, SLAB_GATE + 1)
            for g in range(NG):
                pe.wait_ge(s_x_lo, KD * (g + 1))
                h_group(SLAB_GATE % 2, g, 0)

            def gate_tables():
                pe.wait_ge(s_rows_ready, 1)
                for c in range(NC + 1):
                    w = L if c < NC else ND
                    b = (b_S, b_W, b_N)[c // 4]
                    last = pe.transpose(b[0:w, (c % 4) * P:(c % 4 + 1) * P], R[:, c * L:c * L + w], ident[:, :])
                    if c in (3, 7, 8):
                        last.then_inc(s_table_t, 1)
                pe.matmul(b_U[:, 0:96], ones[0:4, :], wi_diag[:, :, :].rearrange("p c h -> p (c h)"),
                          start=True, stop=True).then_inc(s_bcast_ready, 1)

            gate_tables()
            b_tr = (b_S, b_W, b_N, b_I)
            with pe.Fori(0, HEADS) as h:
                n0 = SLAB_HEAD + SLABS_PER_HEAD * h
                t0 = UNIT_HEAD + UNITS_PER_HEAD * h
                sl = [(SLAB_HEAD + j) % 2 for j in range(SLABS_PER_HEAD)]

                def transposes(src, ready, taken):
                    for r in range(4):
                        for c in (2 * r, 2 * r + 1):
                            for k in range(2):
                                last = pe.transpose(b_tr[r][:, (c % 2) * 256 + k * P:(c % 2) * 256 + (k + 1) * P],
                                                    src[:, k, c * L:(c + 1) * L], ident[:, :])
                        last.then_inc(ready, 1)

                for j in range(3):
                    h_unit(n0 + j, sl[j], t0 + j)
                for g in range(NG):
                    pe.wait_ge(s_group_free[g], t0 + 2)
                transposes(o_h, s_vT_ready, None)
                for j in range(3, 7):
                    h_unit(n0 + j, sl[j], t0 + j)
                for g in range(NG):
                    pe.wait_ge(s_group_free[g], t0 + 6)
                pe.wait_ge(s_vT_taken, 4 * h + 4)
                transposes(k_h, s_kT_ready, None)
                for i, src in enumerate((q_h, k_h)):
                    for k in range(2):
                        last = pe.transpose(b_U[0:ND, (2 * i + k) * P:(2 * i + k + 1) * P], src[:, k, T:N], ident[:, :])
                last.then_inc(s_dqk_ready, 1)
                h_unit(n0 + 7, sl[7], t0 + 7)
                with pe.Fori(0, NC // 2) as c2:
                    for e in range(2):
                        c = 2 * c2 + e
                        i1 = NC * h + c + 1
                        t = t0 + 8 + c
                        n = n0 + 8 + c
                        slot = (SLAB_HEAD + e) % 2
                        pe.wait_ge(s_staged, i1)
                        for k in range(2):
                            last = pe.matmul(b_S[:, 0:L], ks[:, k, :], qs[:, k, :], start=k == 0, stop=k == 1)
                        last.then_inc(s_scores_ready, 1)
                        pe.matmul(b_W[:, 0:L], ident_b[:, :], mask_b[:, :], start=True, stop=False)
                        pe.matmul(b_W[:, 0:L], ones[0:4, :], A_pick[:, :], start=False, stop=True).then_inc(s_logw_ready, 1)
                        pe.wait_ge(s_slab_split, n + 1)
                        h_group(slot, 0, t)
                        pe.wait_ge(s_weighted_ready, i1)
                        vc = v_all[:, bass.ds(c, 1), :].rearrange("p a n -> p (a n)")
                        pe.matmul(b_N[:, 0:257], SW[:, :], vc, start=True, stop=True)
                        for k in range(2):
                            pe.matmul(b_N[:, 260 + k:261 + k], kw[:, k * P:(k + 1) * P], ones[:, 0:1], start=True, stop=True)
                        for k in range(2):
                            last = pe.matmul(b_I[:, 0:257], qs[:, k, :], Cn[:, k, :], start=k == 0, stop=k == 1)
                        last.then_inc(s_carried_ready, 1)
                        for k in range(2):
                            last = pe.matmul(b_U[:, k * 256:(k + 1) * 256], kw[:, k * P:(k + 1) * P],
                                             v_all[:, bass.ds(c, 1), 0:256].rearrange("p a n -> p (a n)"), start=True, stop=True)
                        last.then_inc(s_update_ready, 1)
                        h_group(slot, 1, t)
                        pe.wait_ge(s_hn_ready, i1)
                        for k in range(2):
                            last = pe.transpose(b_S[:, P + k * P:P + (k + 1) * P], num[:, k * P:(k + 1) * P], ident[:, :])
                        last.then_inc(s_hT_ready, 1)
                        h_group(slot, 2, t)
                pe.wait_ge(s_dinv_diag, h + 1)
                pe.wait_ge(s_dy_gated, h + 1)
                pe.matmul(b_U[:, 0:ND], ones[0:ND, :], rdiag[:, :], start=True, stop=True).then_inc(s_dinv_all, 1)
                pe.wait_ge(s_ylo_ready, NC * h + NC)
                for j in range(8):
                    sj = 16 + j // 4
                    if j % 4 == 0:
                        pe.wait_ge(s_slab_split, n0 + sj + 1)
                    for g in range(NG):
                        if j == 0 and g == 2:
                            pe.wait_ge(s_dy_ready, h + 1)
                        group(g, t0 + 16 + j, [(a, b, y_hi[:, k, tok[g]], y_lo[:, k, tok[g]])
                                               for k, (a, b) in enumerate(w_blocks(sl[sj], 2, 512, (j % 4) * P))])

            pe.wait_ge(s_pool_in_loaded, 32)
            pe.wait_ge(s_xq_loaded, 64)
            for w in range(4):
                for e in range(2):
                    b = 2 * w + e
                    pe.wait_ge(s_cache_loaded[e], 16 * (w + 1))
                    for m in range(2):
                        for hh in range(4):
                            last = pe.matmul(b_N[:, m * 32 + hh * 8 + b:m * 32 + hh * 8 + b + 1],
                                             cache_t[:, e, hh * MEM + m * P:hh * MEM + (m + 1) * P],
                                             xq[:, hh, T + b:T + b + 1], start=True, stop=True)
                    last.then_inc(s_dkeys_used, 1)
                if w == 3:
                    pe.wait_ge(s_dscores_taken, 1)
                    for m in range(2):
                        last = pe.transpose(b_U[0:32, m * P:(m + 1) * P], dec_scores[:, m * 32:(m + 1) * 32], ident[:, :])
                    last.then_inc(s_dscoresT_ready, 1)
                pe.wait_ge(s_pool_d_ready, w + 1)
                for g in range(NG):
                    group(g, UNIT_POOL + w, [(wp[:, w, :], pool_d[:, w % 2, tok[g]])], False)
            pe.wait_ge(s_dprob_ready, 1)
            for m in range(2):
                last = pe.transpose(b_N[:, m * 32:(m + 1) * 32], dec_exp[:, m * P:(m + 1) * P], ident[0:32, 0:32])
            last.then_inc(s_dprobT_ready, 1)
            pe.wait_ge(s_dprobT_taken, 1)

            def merge_group(i, e, g, branch, hi, lo):
                if g == 0 and e % 2 == 0:
                    pe.wait_ge(s_slab_split, SLAB_MERGE + 4 * branch + 2 * i + e // 2 + 1)
                wb = w_blocks((SLAB_MERGE + e // 2) % 2, 4, 256, (e % 2) * P)
                group(g, UNIT_MERGE + 8 * branch + 4 * i + e,
                      [(*wb[k], hi[:, k, tok[g]], lo[:, k, tok[g]]) for k in range(4)])
            pe.wait_ge(s_kv_loaded, 32)
            with pe.Fori(0, 2) as i:
                for e in range(4):
                    c = 4 * i + e
                    pe.wait_ge(s_xs_staged, c + 1)
                    for hh in range(4):
                        last = pe.matmul((b_S, b_W)[hh // 2][:, (hh % 2) * MEM:(hh % 2 + 1) * MEM], xs_t[:, hh, :], kv_in[:, hh, :],
                                         start=True, stop=True)
                        if hh % 2:
                            last.then_inc(s_xscores_ready, 1)
                    merge_group(i, e, 0, 0, yp_hi, yp_lo)
                    merge_group(i, e, 1, 0, yp_hi, yp_lo)
                    pe.wait_ge(s_xprob_ready, c + 1)
                    for q in range(8):
                        last = pe.transpose((b_N, b_I)[q // 4][:, (q % 4) * P:(q % 4 + 1) * P],
                                            P_sb[:, q // 2, (q % 2) * P:(q % 2 + 1) * P], ident[:, :])
                        if q % 4 == 3:
                            last.then_inc(s_xprobT_ready, 1)
                    pe.wait_ge(s_cache_loaded[e % 2], 64 + 16 * (2 * i + e // 2 + 1))
                    for hh in range(4):
                        for m in range(2):
                            last = pe.matmul(b_S[:, hh:hh + 1], cache_t[:, e % 2, m * 512 + hh * P:m * 512 + (hh + 1) * P],
                                             dec_probs[:, bass.ds(m * 32 + hh * 8 + c, 1)], start=m == 0, stop=m == 1)
                    last.then_inc(s_dvalues_used, 1)
                    merge_group(i, e, 2, 0, yp_hi, yp_lo)
                    pe.wait_ge(s_dvalues_taken, c + 1)
                    for hh in range(4):
                        if hh % 2 == 0:
                            pe.wait_ge(s_xprobT_taken, 2 * c + 1 + hh // 2)
                        for m in range(2):
                            last = pe.matmul(b_U[:, hh * P:(hh + 1) * P], v_in[:, m, hh * P:(hh + 1) * P], PT_sb[:, 2 * hh + m, :],
                                             start=m == 0, stop=m == 1)
                    last.then_inc(s_xo_ready, 1)
            pe.wait_ge(s_xo_lo, NC - 1)
            with pe.Fori(0, 2) as i:
                for e in range(4):
                    for g in range(NG):
                        if e == 0 and g == 2:
                            pe.wait_ge(s_xo_lo, NC)
                            pe.wait_ge(s_dattn_lo, 1)
                        merge_group(i, e, g, 1, yx_hi, yx_lo)
            with pe.Fori(0, 8, 2) as j2:
                for e in range(2):
                    pe.wait_ge(s_slab_split, SLAB_OUT + j2 + e + 1)
                    for g in range(NG):
                        if e == 0:
                            pe.wait_ge(s_merged_lo, 22 + g)
                        h_group((SLAB_OUT + e) % 2, g, UNIT_OUT + j2 + e)
            for g in range(NG):
                pe.wait_ge(s_z_acc, NG * 8 + g + 1)
                pe.matmul((b_S, b_W, b_N)[g][:, 0:G], ones[:, :], rstd0b[:, tok[g]], start=True, stop=True).then_inc(s_z_ssq, 1)
            for g in range(NG):
                for k in range(KD):
                    pe.wait_ge(s_x1_sq, g * KD + k + 1)
                    last = pe.matmul((b_I, b_U, b_S)[g][:, 0:G], ones[:, :], sq_ring(k % 4), start=k == 0, stop=k == 7)
                    last.then_inc(s_x1_ssq, 1)
            def ff1(n, slots, t, first=False):
                for j in range(4):
                    pe.wait_ge(s_slab_split, n + j + 1)
                    for g in range(NG):
                        if first and j == 0:
                            pe.wait_ge(s_h2_lo, KD * (g + 1))
                        h_group(slots[j], g, t + j)

            def ff2(n, slots, t, half, blocks_done):
                pe.wait_ge(s_f_lo, blocks_done)
                for j in range(8):
                    if j % 2 == 0:
                        pe.wait_ge(s_slab_split, n + j // 2 + 1)
                    for g in range(NG):
                        group(g, t + j, [(a, b, f_hi[:, half, k, tok[g]], f_lo[:, half, k, tok[g]])
                                         for k, (a, b) in enumerate(w_blocks(slots[j // 2], 4, 256, (j % 2) * P))])

            def par(n0_):
                return [(n0_ + j) % 2 for j in range(4)]

            ff1(SLAB_FF, par(SLAB_FF), UNIT_FF, True)
            with pe.Fori(0, 3) as i:
                n0 = SLAB_FF + 4 + 16 * i
                t0 = UNIT_FF_LOOP + UNITS_PER_FF_STEP * i
                p = par(SLAB_FF)
                ff1(n0, p, t0)
                ff2(n0 + 4, p, t0 + 4, 0, 24 * i + 12)
                ff1(n0 + 8, p, t0 + 12)
                ff2(n0 + 12, p, t0 + 16, 1, 24 * i + 24)
            n0, t0, p = SLAB_FF + 52, UNIT_FF_TAIL, par(SLAB_FF)
            ff1(n0, p, t0)
            ff2(n0 + 4, p, t0 + 4, 0, 84)
            ff2(n0 + 8, p, t0 + 12, 1, 96)
            for g in range(NG):
                for k in range(KD):
                    pe.wait_ge(s_f_squared, g * KD + k + 1)
                    last = pe.matmul((b_S, b_W, b_N)[g][:, 0:G], ones[:, :], sq_ring(k % 4), start=k == 0, stop=k == 7)
                    last.then_inc(s_f_ssq, 1)

        @block.scalar
        def _(act):
            def take(g, t, out, func=ACT.Copy, scale=1.0):
                act.wait_ge(s_group_ready[g], t + 1)
                act.activation(out, bank[g][:, 0:G], func, scale=scale).then_inc(s_group_free[g], 1)

            act.wait_ge(s_mem_loaded, 16)
            act.activation(kvT[:, :, :], mem_in[:, :, :], ACT.Square).then_inc(s_mem_sq, 1)
            for k in range(KD):
                act.wait_ge(s_x_loaded[k // 4], 16)
                if k >= 2:
                    act.wait_ge(s_x_sq_used, k - 1)
                act.activation(sq0[:, k % 2, :], x_in[:, k, :], ACT.Square).then_inc(s_x_sq, 1)
                if k == 1:
                    act.wait_ge(s_consts, 5)
                    act.wait_ge(s_mem_ssq, 1)
                    act.activation(kvT[:, 0, :], b_U[:, 0:MEM], ACT.Sqrt, scale=1.0 / D, bias=eps[:, 0:1]).then_inc(s_mem_std, 1)
            act.wait_ge(s_x_sq_used, KD)
            for g in range(NG):
                act.activation(rstd0b[:, tok[g]], (b_S, b_W, b_N)[g][:, 0:G], ACT.Sqrt, scale=1.0 / D, bias=eps[:, 0:1]).then_inc(s_x_std, 1)
            act.wait_ge(s_mem_h, 1)
            act.activation(m_hi[:, :, :], mem_in[:, :, :], ACT.Copy).then_inc(s_mem_hi, 1)
            for g in range(NG):
                for k in range(KD):
                    act.wait_ge(s_x_h, g * KD + k + 1)
                    act.activation(h_hi[:, k, tok[g]], x_in[:, k, tok[g]], ACT.Copy).then_inc(s_x_hi, 1)
            for n in range(8):
                act.wait_ge(s_mem_ready, n + 1)
                act.activation(kvT[:, n, :], (b_I, b_U)[n % 2][:, 0:MEM], ACT.Copy).then_inc(s_mem_taken, 1)
            act.wait_ge(s_mem_taken, 8)
            act.dma_start(o_kv, kvT[:, :, :]).then_inc(s_kv_stored, 16)
            for m in range(2):
                act.wait_ge(s_memv_t, m + 1)
                act.activation(v_tok[:, m, :], (b_I, b_U)[m][:, :], ACT.Copy).then_inc(s_memv_taken, 1)
            act.wait_ge(s_memv_taken, 2)
            act.dma_start(d_v, v_tok[:, :, :]).then_inc(s_spilled, 16)
            act.wait_ge(s_gate_row, 1)
            act.activation(lf[:, :], tg[:, :], ACT.Exp, scale=-1.0).then_inc(s_gate_act, 1)
            act.wait_ge(s_gate_act, 1)
            act.activation(tg[:, :], lf[:, :], ACT.Ln, bias=ones[0:4, 0:1]).then_inc(s_gate_act, 1)
            act.wait_ge(s_gate_row, 2)
            act.activation(R[32:36, :], tg[:, :], ACT.Exp)
            act.activation(R[64:68, :], lf[:, :], ACT.Exp)
            act.activation(R[96:100, :], mm_[:, :], ACT.Exp, scale=-1.0).then_inc(s_gate_act, 1)

            with act.Fori(0, HEADS) as h:
                t0 = UNIT_HEAD + UNITS_PER_HEAD * h
                def block_of(dst, k, t, scale=1.0):
                    for g in (0, 2):
                        take(g, t, dst[:, k, tok[g]], scale=scale)
                block_of(o_h, 0, t0)
                block_of(o_h, 1, t0 + 1)
                block_of(q_h, 0, t0 + 2)
                for r in range(4):
                    act.wait_ge(s_vT_ready, 4 * h + r + 1)
                    act.activation(v_all[:, 2 * r:2 * r + 2, 0:256],
                                   (b_S, b_W, b_N, b_I)[r][:, :].rearrange("p (c n) -> p c n", c=2), ACT.Copy)\
                       .then_inc(s_vT_taken, 1)
                block_of(q_h, 1, t0 + 3)
                block_of(k_h, 0, t0 + 4, K_SCALE)
                block_of(k_h, 1, t0 + 5, K_SCALE)
                act.wait_ge(s_wv_ready, h + 1)
                for g in range(NG):
                    take(g, t0 + 6, o_h[:, 0, tok[g]], ACT.Sigmoid)
                for r in range(4):
                    act.wait_ge(s_kT_ready, 4 * h + r + 1)
                    act.activation(kw_all[:, 2 * r:2 * r + 2, :],
                                   (b_S, b_W, b_N, b_I)[r][:, :].rearrange("p (c n) -> p c n", c=2), ACT.Copy)\
                       .then_inc(s_kT_taken, 1)
                act.wait_ge(s_dqk_taken, h + 1)
                act.dma_start(d_qk[bass.ds(h, 1)].rearrange("a b n -> (a b) n"), qkd[:, :]).then_inc(s_dqk_stored, 16)
                for g in range(NG):
                    take(g, t0 + 7, o_h[:, 1, tok[g]], ACT.Sigmoid)
                with act.Fori(0, NC) as c:
                    i1 = NC * h + c + 1
                    t = t0 + 8 + c
                    act.wait_ge(s_logw_ready, i1)
                    act.activation(SW[:, :], b_W[:, 0:L], ACT.Exp, bias=col[:, B_:B_ + 1]).then_inc(s_weights_ready, 1)
                    act.wait_ge(s_spilled, 16 * i1)
                    take(0, t, side_t[:, tok[0]])
                    act.wait_ge(s_carried_ready, i1)
                    act.activation(num[:, :], b_I[:, 0:257], ACT.Copy, scale=col[:, WI_:WI_ + 1]).then_inc(s_carried_scaled, 1)
                    take(1, t, side_t[:, tok[1]])
                    take(2, t, side_t[:, tok[2]])
                    act.wait_ge(s_group_free[2], t + 1)
                    act.dma_start(d_side[bass.ds(NC * h + c, 1)].rearrange("a p n -> (a p) n"), side_t[:, :])\
                       .then_inc(s_spilled, 16)
                act.wait_ge(s_C_new, NC * (h + 1))
                act.dma_start(o_C[bass.ds(h, 1)].rearrange("a p k c -> (a p) k c"), Cn[:, :, :]).then_inc(s_C_stored, 16)
            act.dma_start(o_n_s, ns[:, :]).then_inc(s_n_stored, 16)
            act.dma_start(o_m, m_out[:, :]).then_inc(s_n_stored, 16)
            act.wait_ge(s_u_loaded, 64)
            act.dma_start(o_pool, u_pad[:, :, 16 + T - 15:16 + T]).then_inc(s_pool_stored, 16)
            for w in range(4):
                for g in range(NG):
                    act.wait_ge(s_group_ready[g], UNIT_POOL + w + 1)
                    act.activation(yp_hi[:, w, tok[g]], bank[g][:, 0:G], ACT.Copy, scale=vec[:, V_POOL + w:V_POOL + w + 1])\
                       .then_inc(s_pool_hi, 1)
            act.wait_ge(s_pool_state_ready, 1)
            act.dma_start(o_pool_s, win_a[:, 0:480]).then_inc(s_pool_stored, 16)
            act.wait_ge(s_xbias_ready, 1)
            act.activation(dec_exp[:, :], b_U[0:32, 0:MEM], ACT.Exp, bias=sm[0:32, 9:10], scale=X_SCALE,
                           accum_out=sm[0:32, 10:11]).then_inc(s_dexp_ready, 1)
            act.wait_ge(s_pool_stored, 32)
            with act.Fori(0, NC) as c:
                act.wait_ge(s_xbias_ready, c + 2)
                for hh in range(4):
                    act.activation(P_sb[:, hh, :], (b_S, b_W)[hh // 2][:, (hh % 2) * MEM:(hh % 2 + 1) * MEM], ACT.Exp,
                                   bias=sm[:, 4 + hh:5 + hh], scale=X_SCALE, accum_out=sm[:, 8 + hh:9 + hh]).then_inc(s_xexp_ready, 1)
                for q, b in enumerate((b_N, b_I)):
                    act.wait_ge(s_xprobT_ready, 2 * c + 1 + q)
                    act.activation(PT_sb[:, 4 * q:4 * q + 4, :], b[:, :].rearrange("p (i t) -> p i t", i=4), ACT.Copy)\
                       .then_inc(s_xprobT_taken, 1)
                for g in range(NG):
                    act.wait_ge(s_g_loaded[g], 16 * (c + 1))
                    act.activation(gates[:, g, 0:2, :], gates[:, g, 0:2, :], ACT.Sigmoid).then_inc(s_g_sig, 1)
                act.wait_ge(s_xo_ready, c + 1)
                act.activation(yx_hi[:, :, bass.ds(L * c, L)], b_U[:, :].rearrange("p (h t) -> p h t", h=4), ACT.Copy)\
                   .then_inc(s_xo_hi, 1)
            act.wait_ge(s_dvalues_taken, ND)
            act.activation(yx_hi[:, :, T:N], dec_out[:, :, :], ACT.Copy).then_inc(s_dattn_hi, 1)
            with act.Fori(0, 4) as i:
                for e in range(2):
                    j = 2 * i + e
                    act.wait_ge(s_xg_loaded[e], 16 * (i + 1))
                    act.activation(gates[:, :, (2, 0)[e], :], gates[:, :, (2, 0)[e], :], ACT.Sigmoid).then_inc(s_xg_sig, 1)
                    for g in range(NG):
                        act.wait_ge(s_merged, NG * j + g + 1)
                        act.activation(h_hi[:, bass.ds(j, 1), tok[g]].rearrange("p a t -> p (a t)"),
                                       acc[:, bass.ds(j, 1), tok[g]].rearrange("p a t -> p (a t)"), ACT.Copy).then_inc(s_merged_hi, 1)
            with act.Fori(0, 8) as j:
                for g in range(NG):
                    act.wait_ge(s_group_ready[g], UNIT_OUT + j + 1)
                    act.activation(acc[:, bass.ds(j, 1), tok[g]].rearrange("p a t -> p (a t)"), bank[g][:, 0:G], ACT.Copy)\
                       .then_inc(s_z_evac, 1)
                    act.wait_ge(s_z_acc, NG * j + g + 1)
                    act.activation(gates[:, g, 0, :], bank[g][:, 0:G], ACT.Square).then_inc(s_group_free[g], 1)
            for g in range(NG):
                act.wait_ge(s_z_ssq, g + 1)
                act.activation(rstd0b[:, tok[g]], (b_S, b_W, b_N)[g][:, 0:G], ACT.Sqrt, scale=1.0 / D, bias=eps[:, 0:1]).then_inc(s_z_std, 1)
            for g in range(NG):
                for k in range(KD):
                    act.wait_ge(s_x1_ready, g * KD + k + 1)
                    if g * KD + k >= 4:
                        act.wait_ge(s_x1_ssq, g * KD + k - 3)
                    act.activation(sq_ring(k % 4), x_in[:, k, tok[g]], ACT.Square).then_inc(s_x1_sq, 1)
            act.dma_start(d_x1, x_in[:, :, :]).then_inc(s_x1_stored, 16)
            for g in range(NG):
                act.wait_ge(s_x1_ssq, KD * (g + 1))
                act.activation(rstd0b[:, tok[g]], (b_I, b_U, b_S)[g][:, 0:G], ACT.Sqrt, scale=1.0 / D, bias=eps[:, 0:1]).then_inc(s_x1_std, 1)
            for g in range(NG):
                for k in range(KD):
                    act.wait_ge(s_h2_ready, g * KD + k + 1)
                    act.activation(h_hi[:, k, tok[g]], acc[:, k, tok[g]], ACT.Copy).then_inc(s_h2_hi, 1)
            act.wait_ge(s_x1_stored, 16)

            def ff1(t, half, count):
                for j in range(4):
                    for g in range(NG):
                        take(g, t + j, rl[:, g, :], ACT.Relu)
                        act.wait_ge(s_relu_squared, count + NG * j + g + 1)
                        act.activation(f_hi[:, half, j, tok[g]], sqv[:, g, :], ACT.Copy).then_inc(s_f_hi, 1)

            ff1(UNIT_FF, 0, 0)
            with act.Fori(0, 3) as i:
                t0 = UNIT_FF_LOOP + UNITS_PER_FF_STEP * i
                ff1(t0, 1, 24 * i + 12)
                ff1(t0 + 12, 0, 24 * i + 24)
            ff1(UNIT_FF_TAIL, 1, 84)
            act.wait_ge(s_f_added, 24 * 8)
            for g in range(NG):
                for k in range(KD):
                    if g * KD + k >= 4:
                        act.wait_ge(s_f_ssq, g * KD + k - 3)
                    act.activation(sq_ring(k % 4), acc[:, k, tok[g]], ACT.Square).then_inc(s_f_squared, 1)
            for g in range(NG):
                act.wait_ge(s_f_ssq, KD * (g + 1))
                act.activation(rstd0b[:, tok[g]], (b_S, b_W, b_N)[g][:, 0:G], ACT.Sqrt, scale=1.0 / D, bias=eps[:, 0:1]).then_inc(s_f_std, 1)
            for q, n in ((s_kv_stored, 16), (s_C_stored, 64), (s_n_stored, 32), (s_pool_stored, 32),
                         (s_spilled, 16 * (FILL + 1))):
                act.wait_ge(q, n)

        @block.vector
        def _(dve):
            chain = [0]

            def step(ins):
                chain[0] += 1
                ins.then_inc(s_dve_step, 1)
                dve.wait_ge(s_dve_step, chain[0])

            def stt(out, in0, scalar, in1, op0, op1):
                return dve.scalar_tensor_tensor(out=out, in0=in0, scalar=scalar, in1=in1, op0=op0, op1=op1)

            def vcol(c):
                return vec[:, c:c + 1]

            dve.wait_ge(s_const_loaded, 64)
            dve.wait_ge(s_mem_std, 1)
            step(dve.reciprocal(kvT[:, 1, :], kvT[:, 0, :]))
            for k in range(KD):
                last = stt(mem_in[:, k, :], mem_in[:, k, :], vcol(V_MEM + k), kvT[:, 1, :], ALU.mult, ALU.mult)
            last.then_inc(s_mem_h, 1)
            dve.wait_ge(s_mem_hi, 1)
            dve.tensor_tensor(m_lo[:, :, :], mem_in[:, :, :], m_hi[:, :, :].bitcast(F32), ALU.subtract).then_inc(s_mem_lo, 1)
            for g in range(NG):
                dve.wait_ge(s_x_std, g + 1)
                step(dve.reciprocal(rstd0[:, tok[g]], rstd0b[:, tok[g]]))
                for k in range(KD):
                    stt(x_in[:, k, tok[g]], x_in[:, k, tok[g]], vcol(V_PRE + k), rstd0[:, tok[g]], ALU.mult, ALU.mult)\
                        .then_inc(s_x_h, 1)
                for k in range(KD):
                    dve.wait_ge(s_x_hi, g * KD + k + 1)
                    dve.tensor_tensor(h_lo[:, k, tok[g]], x_in[:, k, tok[g]], h_hi[:, k, tok[g]].bitcast(F32), ALU.subtract)\
                        .then_inc(s_x_lo, 1)

            dve.wait_ge(s_kv_stored, 16)
            dve.wait_ge(s_spilled, 16)
            step(dve.memset(R[:, :], 0.0))
            for g in range(NG):
                dve.wait_ge(s_group_ready[g], 1)
                dve.tensor_scalar(gi[:, tok[g]], bank[g][0:4, 0:G], bif[:, 0:1], None, ALU.add)
                dve.tensor_scalar(gf[:, tok[g]], bank[g][32:36, 0:G], bif[:, 1:2], None, ALU.add).then_inc(s_group_free[g], 1)
            dve.wait_ge(s_group_free[2], 1)
            stt(tg[:, :], gf[:, :], -1.0, gf[:, :], ALU.mult, ALU.max).then_inc(s_gate_row, 1)
            dve.wait_ge(s_gate_act, 2)
            step(stt(lf[:, :], gf[:, :], 0.0, tg[:, :], ALU.min, ALU.subtract))
            dve.tensor_tensor_scan(mm_[:, 0:T], lf[:, 0:T], gi[:, 0:T], 0.0, ALU.add, ALU.max)
            dve.memset(gf[:, :], 1.0)
            step(dve.tensor_tensor(tg[:, T:N], lf[:, T:N], m0[:, :], ALU.add))
            dve.tensor_tensor(mm_[:, T:N], tg[:, T:N], gi[:, T:N], ALU.max)
            step(dve.memset(gf[:, 0:T].rearrange("p (c l) -> p c l", l=L)[:, :, 0:1], 0.0))
            dve.tensor_copy(bb[:, T:N], lf[:, T:N])
            step(dve.tensor_tensor_scan(bb[:, 0:T], gf[:, 0:T], lf[:, 0:T], 0.0, ALU.mult, ALU.add))
            dve.memset(mprev[:, 0:1], 0.0)
            dve.tensor_copy(mprev[:, 1:NC + 1], mm_[:, L - 1:T:L])
            dve.tensor_copy(m_out[:, :], mm_[:, T - 1:N])
            dve.tensor_tensor(A_row[:, :], bb[:, :], mm_[:, :], ALU.subtract)
            step(dve.tensor_tensor(R[0:4, :], gi[:, :], bb[:, :], ALU.subtract))

            def chunks(a):
                return a.rearrange("p (c l) -> p c l", l=L)
            dve.tensor_tensor(chunks(tg[:, 0:T]), chunks(A_row[:, 0:T]),
                              mprev[:, 0:NC].unsqueeze(2).to_broadcast([4, NC, L]), ALU.add)
            dve.tensor_tensor(tg[:, T:N], A_row[:, T:N], m0[:, :], ALU.add)
            dve.tensor_tensor(chunks(lf[:, 0:T]), chunks(R[0:4, 0:T]),
                              chunks(A_row[:, 0:T])[:, :, L - 1:L].to_broadcast([4, NC, L]), ALU.add)
            dve.tensor_tensor(lf[:, T:N], R[0:4, T:N], A_row[:, T:N], ALU.add).then_inc(s_gate_row, 1)
            dve.wait_ge(s_gate_act, 3)
            dve.tensor_copy(wsel[:, 0:NC], R[32:36, L - 1:T:L])
            dve.tensor_copy(wsel[:, NC:NC + ND], R[64:68, T:N])
            step(dve.tensor_copy(wsel[:, NC + ND:NC + 2 * ND], R[32:36, T:N]))
            dve.tensor_tensor(wi_diag[:, :, :], wsel[:, :].unsqueeze(2).to_broadcast([4, NC + 2 * ND, 4]),
                              ident[0:4, 0:4].unsqueeze(1).to_broadcast([4, NC + 2 * ND, 4]), ALU.mult)\
               .then_inc(s_rows_ready, 1)
            for i, b in enumerate((b_S, b_W, b_N)):
                dve.wait_ge(s_table_t, i + 1)
                v = b[:, :].rearrange("p (c q r) -> p c q r", c=4, q=4)
                if i < 2:
                    dve.tensor_copy(cols[:, 4 * i:4 * i + 4, :, :], v[:, :, :, 0:4])
                else:
                    dve.tensor_copy(cols[0:ND, NC:NC + 1, :, :], v[0:ND, 0:1, :, 0:4])
            dve.wait_ge(s_bcast_ready, 1)
            dve.tensor_copy(decays[:, :, :], b_U[:, 0:32].rearrange("p (c h) -> p c h", h=4))
            dve.tensor_copy(dw[:, :, :, :], b_U[:, 32:96].rearrange("p (w b h) -> p w b h", w=2, h=4))
            dve.memset(v_all[:, :, 256:257], 1.0)
            step(dve.memset(acc[:, :, :], 0.0))

            with dve.Fori(0, HEADS) as h:
                t0 = UNIT_HEAD + UNITS_PER_HEAD * h
                h1 = h + 1

                def take1(dst, k, t, scale=1.0):
                    dve.wait_ge(s_group_ready[1], t + 1)
                    dve.tensor_scalar(dst[:, k, tok[1]], bank[1][:, 0:G], scale, None, ALU.mult).then_inc(s_group_free[1], 1)
                take1(o_h, 0, t0)
                take1(o_h, 1, t0 + 1)
                take1(q_h, 0, t0 + 2)
                dve.wait_ge(s_group_free[2], t0 + 2)
                dve.tensor_tensor(wv[:, :, :], o_h[:, :, T:N],
                                  dw[:, 0:1, :, bass.ds(h, 1)].rearrange("p w b h -> p (w h) b").to_broadcast([P, 2, ND]),
                                  ALU.mult).then_inc(s_wv_ready, 1)
                take1(q_h, 1, t0 + 3)
                take1(k_h, 0, t0 + 4, K_SCALE)
                take1(k_h, 1, t0 + 5, K_SCALE)
                dve.memset(Cn[:, :, :], 0.0)
                dve.tensor_copy(dcol[:, 0:4], cols[0:ND, NC, :, bass.ds(h, 1)].rearrange("p q h -> p (q h)"))
                dve.wait_ge(s_dqk_ready, h1)
                dve.tensor_copy(qkd[:, :], b_U[0:ND, :]).then_inc(s_dqk_taken, 1)
                n_h = ns[:, bass.ds(256 * h, 256)]
                dve.wait_ge(s_dqk_taken, h1)
                dve.tensor_scalar(dtmp[0:ND, 0, :], qkd[:, 256:512], dcol[:, WE_:WE_ + 1], None, ALU.mult).then_inc(s_dwk_ready, 1)
                dve.wait_ge(s_dwk_ready, h1)
                stt(dtmp[0:ND, 1, :], n_h, dcol[:, WI_:WI_ + 1], dtmp[0:ND, 0, :], ALU.mult, ALU.add).then_inc(s_dn_new, 1)
                dve.wait_ge(s_dn_new, h1)
                dve.tensor_tensor_reduce(out=dtmp[0:ND, 0, :], in0=dtmp[0:ND, 1, :], in1=qkd[:, 0:256], scale=1.0, scalar=0.0,
                                         op0=ALU.mult, op1=ALU.add, accum_out=dcol[:, 4:5]).then_inc(s_ddot_ready, 1)
                dve.tensor_scalar(n_h, dtmp[0:ND, 1, :], 1.0, None, ALU.mult)
                dve.wait_ge(s_ddot_ready, h1)
                dve.tensor_scalar(dcol[:, 7:8], dcol[:, 4:5], dcol[:, EM_:EM_ + 1], None, ALU.max).then_inc(s_dden_ready, 1)
                dve.wait_ge(s_dden_ready, 2 * h1 - 1)
                stt(dcol[:, 5:6], dcol[:, 4:5], -1.0, dcol[:, 7:8], ALU.mult, ALU.max).then_inc(s_dden_ready, 1)
                dve.wait_ge(s_dden_ready, 2 * h1)
                dve.reciprocal(dcol[:, 6:7], dcol[:, 5:6]).then_inc(s_dinv_ready, 1)
                dve.wait_ge(s_kT_taken, 4 * h1)
                dve.wait_ge(s_group_free[2], t0 + 6)
                dve.wait_ge(s_dinv_ready, h1)
                dve.tensor_scalar(rdiag[:, :], ident[0:ND, 0:ND], dcol[:, 6:7], None, ALU.mult).then_inc(s_dinv_diag, 1)

                with dve.Fori(0, NC) as c:
                    i1 = NC * h + c + 1
                    cc = bass.ds(L * c, L)
                    dve.tensor_copy(col[:, 0:4], cols[:, bass.ds(c, 1), :, bass.ds(h, 1)].rearrange("p c q h -> p (c q h)"))
                    dve.tensor_copy(col[:, 4:5], decays[:, bass.ds(c, 1), bass.ds(h, 1)].rearrange("p c h -> p (c h)"))\
                       .then_inc(s_col_set, 1)
                    dve.tensor_scalar(A_pick[:, :], A_row[:, cc], ident[0:4, bass.ds(h, 1)], None, ALU.mult)
                    dve.tensor_copy(qs[:, :, :], q_h[:, :, cc])
                    dve.tensor_copy(ks[:, :, :], k_h[:, :, cc])
                    dve.wait_ge(s_col_set, i1)
                    dve.tensor_scalar(kw[:, :], kw_all[:, bass.ds(c, 1), :].rearrange("p c n -> p (c n)"),
                                      col[:, WE_:WE_ + 1], None, ALU.mult).then_inc(s_staged, 1)
                    dve.wait_ge(s_scores_ready, i1)
                    dve.wait_ge(s_weights_ready, i1)
                    dve.tensor_tensor(SW[:, :], b_S[:, 0:L], SW[:, :], ALU.mult).then_inc(s_weighted_ready, 1)
                    dve.wait_ge(s_dstate_loaded, 32 * i1)
                    for k in range(2):
                        last = dve.tensor_scalar(dtmp[:, k, :], qkb[:, 256:512],
                                                 wv[:, k, bass.ds(c, 1)], None, ALU.mult)
                    last.then_inc(s_dkv_ready, 1)
                    dve.wait_ge(s_dkv_ready, i1)
                    stt(dC[:, :, :], dC[:, :, :],
                        dw[:, 1:2, bass.ds(c, 1), bass.ds(h, 1)].rearrange("p w b h -> p (w b h)"),
                        dtmp[:, :, :], ALU.mult, ALU.add).then_inc(s_dstate_new, 1)
                    dve.wait_ge(s_dstate_new, i1)
                    for k in range(2):
                        last = dve.tensor_tensor_reduce(out=dtmp[:, k, :], in0=dC[:, k, :], in1=qkb[:, 0:256], scale=1.0,
                                                        scalar=0.0, op0=ALU.mult, op1=ALU.add,
                                                        accum_out=den[:, 2 + k:3 + k])
                    last.then_inc(s_dstate_used, 1)
                    dve.wait_ge(s_dstate_used, i1)
                    dve.tensor_scalar(num_d[:, :, bass.ds(c, 1)].rearrange("p k b -> p (k b)"), den[:, 2:4], 1.0, None, ALU.mult)
                    dve.wait_ge(s_update_ready, i1)
                    stt(Cn[:, :, 0:256], Cn[:, :, 0:256], col[:, 4:5], b_U[:, :].rearrange("p (k n) -> p k n", k=2),
                        ALU.mult, ALU.add)
                    stt(Cn[:, :, 256], Cn[:, :, 256], col[:, 4:5], b_N[:, 260:262], ALU.mult, ALU.add).then_inc(s_C_new, 1)
                    dve.wait_ge(s_carried_scaled, i1)
                    dve.tensor_tensor(num[:, :], num[:, :], b_N[:, 0:257], ALU.add).then_inc(s_num_ready, 1)
                    dve.wait_ge(s_num_ready, i1)
                    dve.tensor_scalar(den[:, 0:1], num[:, 256:257], col[:, EM_:EM_ + 1], None, ALU.max).then_inc(s_den_max, 1)
                    dve.wait_ge(s_den_max, 2 * i1 - 1)
                    stt(den[:, 0:1], num[:, 256:257], -1.0, den[:, 0:1], ALU.mult, ALU.max).then_inc(s_den_max, 1)
                    dve.wait_ge(s_den_max, 2 * i1)
                    dve.reciprocal(den[:, 1:2], den[:, 0:1]).then_inc(s_den_inv, 1)
                    dve.wait_ge(s_den_inv, i1)
                    dve.tensor_scalar(num[:, 0:256], num[:, 0:256], den[:, 1:2], None, ALU.mult).then_inc(s_hn_ready, 1)
                    dve.wait_ge(s_hT_ready, i1)
                    dve.tensor_tensor(dtmp[:, :, 0:L], b_S[:, P:P + 256].rearrange("p (k l) -> p k l", k=2), o_h[:, :, cc],
                                      ALU.mult).then_inc(s_yv_ready, 1)
                    dve.wait_ge(s_yv_ready, i1)
                    dve.tensor_scalar(y_hi[:, :, cc], dtmp[:, :, 0:L], 1.0, None, ALU.mult).then_inc(s_yhi_ready, 1)
                    dve.wait_ge(s_yhi_ready, i1)
                    dve.tensor_tensor(y_lo[:, :, cc], dtmp[:, :, 0:L], y_hi[:, :, cc].bitcast(F32), ALU.subtract)\
                       .then_inc(s_ylo_ready, 1)
                dve.tensor_tensor(yd[:, :, :], num_d[:, :, :], o_h[:, :, T:N], ALU.mult).then_inc(s_dy_gated, 1)
                dve.wait_ge(s_dy_gated, h1)
                dve.wait_ge(s_dinv_all, h1)
                for k in range(2):
                    last = dve.tensor_tensor(yd[:, k, :], yd[:, k, :], b_U[:, 0:ND], ALU.mult)
                last.then_inc(s_dy_scaled, 1)
                dve.wait_ge(s_dy_scaled, h1)
                dve.tensor_scalar(y_hi[:, :, T:N], yd[:, :, :], 1.0, None, ALU.mult).then_inc(s_dy_hi, 1)
                dve.wait_ge(s_dy_hi, h1)
                dve.tensor_tensor(y_lo[:, :, T:N], yd[:, :, :], y_hi[:, :, T:N].bitcast(F32), ALU.subtract)\
                   .then_inc(s_dy_ready, 1)
                for j in range(8):
                    for g in range(NG):
                        dve.wait_ge(s_group_ready[g], t0 + 17 + j)
                        dve.tensor_tensor(acc[:, j, tok[g]], acc[:, j, tok[g]], bank[g][:, 0:G], ALU.add)\
                           .then_inc(s_group_free[g], 1)
                dve.wait_ge(s_C_stored, 16 * h1)

            dve.memset(u_pad[:, :, 0:16], 0.0)
            dve.memset(win_a[:, 0:16], 0.0)
            step(dve.memset(win_b[:, 0:16], 0.0))
            for t in range(15):
                dve.memset(inv_count[:, t:t + 1], 1.0 / (t + 1))

            def pool_lo(w):
                for g in range(NG):
                    dve.wait_ge(s_pool_hi, NG * w + g + 1)
                    stt(yp_lo[:, w, tok[g]], bank[g][:, 0:G], vcol(V_POOL + w), yp_hi[:, w, tok[g]].bitcast(F32),
                        ALU.mult, ALU.subtract).then_inc(s_group_free[g], 1)

            dve.wait_ge(s_pool_in_loaded, 32)
            for w in range(4):
                win = 2 << w
                u = u_pad[:, w, :]
                dve.wait_ge(s_u_loaded, 64)
                src = u
                for i in range(w + 1):
                    dst = (win_a, win_b)[i % 2]
                    step(dve.tensor_tensor(dst[:, 16:], src[:, 16:16 + N], src[:, 16 - (1 << i):16 + N - (1 << i)], ALU.add))
                    src = dst
                d = pool_d[:, w % 2, :]
                if w >= 2:
                    dve.wait_ge(s_group_ready[2], UNIT_POOL + w - 1)
                dve.tensor_reduce(sm[:, 0:ND], bufT[:, w, :, 15 - (win - 1):15], axis=AX.X, op=ALU.add)
                step(stt(d, src[:, 16:], 1.0 / win, u[:, 16:], ALU.mult, ALU.subtract))
                dve.tensor_tensor(sm[:, 0:ND], sm[:, 0:ND], u[:, 16 + T:], ALU.add)
                step(dve.tensor_tensor(d[:, 0:win - 1], src[:, 16:16 + win - 1], inv_count[:, 0:win - 1], ALU.mult))
                dve.tensor_tensor(d[:, 0:win - 1], d[:, 0:win - 1], u[:, 16:16 + win - 1], ALU.subtract)
                stt(d[:, T:N], sm[:, 0:ND], 1.0 / win, u[:, 16 + T:], ALU.mult, ALU.subtract).then_inc(s_pool_d_ready, 1)
                if w:
                    pool_lo(w - 1)
            po = win_a[:, 0:480].rearrange("p (k b j) -> p k b j", k=4, b=ND)
            for k in range(4):
                dve.tensor_copy(po[:, k, :, 0:14], bufT[:, k, :, 1:15])
            dve.tensor_copy(po[:, :, :, 14], u_pad[:, :, 16 + T:16 + N]).then_inc(s_pool_state_ready, 1)
            dve.wait_ge(s_dkeys_used, ND)
            dve.tensor_copy(dec_scores[:, :], b_N[:, 0:64]).then_inc(s_dscores_taken, 1)
            dve.wait_ge(s_dscoresT_ready, 1)
            step(dve.tensor_reduce(sm[0:32, 8:9], b_U[0:32, 0:MEM], axis=AX.X, op=ALU.max))
            dve.tensor_scalar(sm[0:32, 9:10], sm[0:32, 8:9], -X_SCALE, None, ALU.mult).then_inc(s_xbias_ready, 1)
            dve.wait_ge(s_dexp_ready, 1)
            step(dve.reciprocal(sm[0:32, 11:12], sm[0:32, 10:11]))
            dve.tensor_scalar(dec_exp[:, :], dec_exp[:, :], sm[0:32, 11:12], None, ALU.mult).then_inc(s_dprob_ready, 1)
            pool_lo(3)
            dve.wait_ge(s_dprobT_ready, 1)
            dve.tensor_copy(dec_probs[:, :], b_N[:, 0:64]).then_inc(s_dprobT_taken, 1)
            with dve.Fori(0, NC) as c:
                cc = bass.ds(L * c, L)
                c1 = c + 1
                for i in range(2):
                    dve.wait_ge(s_xscores_ready, 2 * c + 1 + i)
                    last = dve.tensor_reduce(sm[:, 2 * i:2 * i + 2], (b_S, b_W)[i][:, :].rearrange("p (h m) -> p h m", h=2),
                                             axis=AX.X, op=ALU.max)
                last.then_inc(s_xmax_ready, 1)
                dve.wait_ge(s_xmax_ready, c1)
                dve.tensor_scalar(sm[:, 4:8], sm[:, 0:4], -X_SCALE, None, ALU.mult).then_inc(s_xbias_ready, 1)
                dve.wait_ge(s_xexp_ready, 4 * c1)
                dve.reciprocal(sm[:, 12:16], sm[:, 8:12]).then_inc(s_xinv_ready, 1)
                dve.wait_ge(s_xinv_ready, c1)
                for hh in range(4):
                    last = dve.tensor_scalar(P_sb[:, hh, :], P_sb[:, hh, :], sm[:, 12 + hh:13 + hh], None, ALU.mult)
                last.then_inc(s_xprob_ready, 1)
                dve.wait_ge(s_dvalues_used, c1)
                dve.tensor_scalar(dec_out[:, :, bass.ds(c, 1)].rearrange("p h b -> p (h b)"), b_S[:, 0:4], 1.0, None, ALU.mult)\
                   .then_inc(s_dvalues_taken, 1)

                def a(g):
                    return acc[:, bass.ds(c, 1), tok[g]].rearrange("p a t -> p (a t)")
                for g in range(NG):
                    dve.wait_ge(s_g_sig, NG * c + g + 1)
                    dve.tensor_tensor(a(g), a(g), gates[:, g, 1, :], ALU.mult).then_inc(s_acc_gated, 1)
                    dve.wait_ge(s_group_ready[g], UNIT_MERGE + c + 1)
                    dve.tensor_tensor(gates[:, g, 0, :], bank[g][:, 0:G], gates[:, g, 0, :], ALU.mult).then_inc(s_group_free[g], 1)
                for g in range(NG):
                    dve.wait_ge(s_acc_gated, NG * c + g + 1)
                    dve.wait_ge(s_group_free[g], UNIT_MERGE + c + 1)
                    dve.tensor_tensor(a(g), a(g), gates[:, g, 0, :], ALU.add).then_inc(s_pool_added, 1)
                dve.wait_ge(s_xo_hi, c1)
                dve.tensor_tensor(yx_lo[:, :, cc], b_U[:, :].rearrange("p (h t) -> p h t", h=4),
                                  yx_hi[:, :, cc].bitcast(F32), ALU.subtract).then_inc(s_xo_lo, 1)
            dve.wait_ge(s_dattn_hi, 1)
            dve.tensor_tensor(yx_lo[:, :, T:N], dec_out[:, :, :],
                              yx_hi[:, :, T:N].bitcast(F32), ALU.subtract).then_inc(s_dattn_lo, 1)
            def merged_lo(j, g):
                dve.wait_ge(s_merged_hi, NG * j + g + 1)
                at = [t[:, bass.ds(j, 1), tok[g]].rearrange("p a t -> p (a t)") for t in (h_lo, acc, h_hi)]
                dve.tensor_tensor(at[0], at[1], at[2].bitcast(F32), ALU.subtract).then_inc(s_merged_lo, 1)
            with dve.Fori(0, 4) as i:
                for e in range(2):
                    j = 2 * i + e
                    slot = (2, 0)[e]
                    dve.wait_ge(s_xg_sig, j + 1)

                    def a(g):
                        return acc[:, bass.ds(j, 1), tok[g]].rearrange("p a t -> p (a t)")
                    for g in range(NG):
                        dve.wait_ge(s_group_ready[g], UNIT_MERGE + 8 + j + 1)
                        dve.tensor_tensor(gates[:, g, slot, :], bank[g][:, 0:G], gates[:, g, slot, :], ALU.mult)\
                           .then_inc(s_group_free[g], 1)
                        dve.wait_ge(s_group_free[g], UNIT_MERGE + 8 + j + 1)
                        dve.tensor_tensor(a(g), a(g), gates[:, g, slot, :], ALU.add).then_inc(s_merged, 1)
                        if g:
                            merged_lo(j, g - 1)
                    merged_lo(j, NG - 1)
            dve.wait_ge(s_group_ready[2], UNIT_OUT)
            for g in range(NG):
                dve.memset(rstd0b[:, tok[g]], 0.0).then_inc(s_z_acc, 1)
            with dve.Fori(0, 8) as j:
                for g in range(NG):
                    dve.wait_ge(s_group_free[g], UNIT_OUT + j + 1)
                    dve.wait_ge(s_z_acc, NG * j + g + 1)
                    dve.tensor_tensor(rstd0b[:, tok[g]], rstd0b[:, tok[g]], gates[:, g, 0, :], ALU.add).then_inc(s_z_acc, 1)
            for g in range(NG):
                dve.wait_ge(s_z_std, g + 1)
                step(dve.reciprocal(rstd0[:, tok[g]], rstd0b[:, tok[g]]))
                for k in range(KD):
                    dve.wait_ge(s_x2_loaded, 16)
                    stt(acc[:, k, tok[g]], acc[:, k, tok[g]], vcol(V_POST + k), rstd0[:, tok[g]], ALU.mult, ALU.mult)\
                        .then_inc(s_z_scaled, 1)
                for k in range(KD):
                    dve.wait_ge(s_z_scaled, g * KD + k + 1)
                    dve.tensor_tensor(x_in[:, k, tok[g]], x_in[:, k, tok[g]], acc[:, k, tok[g]], ALU.add).then_inc(s_x1_ready, 1)
            for g in range(NG):
                dve.wait_ge(s_x1_std, g + 1)
                step(dve.reciprocal(rstd0[:, tok[g]], rstd0b[:, tok[g]]))
                for k in range(KD):
                    stt(acc[:, k, tok[g]], x_in[:, k, tok[g]], vcol(V_MLP + k), rstd0[:, tok[g]], ALU.mult, ALU.mult)\
                        .then_inc(s_h2_ready, 1)
                for k in range(KD):
                    dve.wait_ge(s_h2_hi, g * KD + k + 1)
                    dve.tensor_tensor(h_lo[:, k, tok[g]], acc[:, k, tok[g]], h_hi[:, k, tok[g]].bitcast(F32), ALU.subtract)\
                        .then_inc(s_h2_lo, 1)
            dve.wait_ge(s_h2_lo, NG * KD)
            step(dve.memset(acc[:, :, :], 0.0))

            def ff1(t, half, count):
                for j in range(4):
                    for g in range(NG):
                        dve.wait_ge(s_group_free[g], t + j + 1)
                        dve.tensor_tensor(sqv[:, g, :], rl[:, g, :], rl[:, g, :], ALU.mult).then_inc(s_relu_squared, 1)
                        dve.wait_ge(s_f_hi, count + NG * j + g + 1)
                        dve.tensor_tensor(f_lo[:, half, j, tok[g]], sqv[:, g, :], f_hi[:, half, j, tok[g]].bitcast(F32),
                                          ALU.subtract).then_inc(s_f_lo, 1)

            def ff2(t):
                for j in range(8):
                    for g in range(NG):
                        dve.wait_ge(s_group_ready[g], t + j + 1)
                        dve.tensor_tensor(acc[:, j, tok[g]], acc[:, j, tok[g]], bank[g][:, 0:G], ALU.add)\
                           .then_inc(s_group_free[g], 1)

            ff1(UNIT_FF, 0, 0)
            with dve.Fori(0, 3) as i:
                t0 = UNIT_FF_LOOP + UNITS_PER_FF_STEP * i
                ff1(t0, 1, 24 * i + 12)
                ff2(t0 + 4)
                ff1(t0 + 12, 0, 24 * i + 24)
                ff2(t0 + 16)
            ff1(UNIT_FF_TAIL, 1, 84)
            ff2(UNIT_FF_TAIL + 4)
            ff2(UNIT_FF_TAIL + 12)
            for g in range(NG):
                dve.wait_ge(s_group_free[g], UNIT_FF_TAIL + 20)
            dve.memset(sm[:, 0:1], 0.0).then_inc(s_f_added, 192)
            for g in range(NG):
                dve.wait_ge(s_f_std, g + 1)
                step(dve.reciprocal(rstd0[:, tok[g]], rstd0b[:, tok[g]]))
            dve.wait_ge(s_x3_loaded, 16)
            for k in range(KD):
                stt(acc[:, k, :], acc[:, k, :], vcol(V_FF + k), rstd0[:, :], ALU.mult, ALU.mult).then_inc(s_y_scaled, 1)
                if k:
                    dve.wait_ge(s_y_scaled, k)
                    dve.tensor_tensor(x_in[:, k - 1, :], x_in[:, k - 1, :], acc[:, k - 1, :], ALU.add).then_inc(s_y_ready, 1)
            dve.wait_ge(s_y_scaled, KD)
            dve.tensor_tensor(x_in[:, KD - 1, :], x_in[:, KD - 1, :], acc[:, KD - 1, :], ALU.add).then_inc(s_y_ready, 1)


def lay_out(inputs):
    import numpy as np

    def feat(a):
        return a.T.reshape(KD, P, a.shape[0]).transpose(1, 0, 2)

    def slab(w):
        return w.reshape(-1, P, w.shape[1]).transpose(1, 0, 2).reshape(P, 1024)

    def vector(v):
        return v.reshape(-1, P).T

    x = np.concatenate([inputs["x_prompt"][0], inputs["x_sample"][:, 0]], axis=0)
    w_in = inputs["w_in"][0]
    q0, k0, v0, o0 = (512 + 1024 * i for i in range(4))
    gif = np.zeros((D, P), np.float32)
    gif[:, 0:4] = w_in[:, 4608:4612]
    gif[:, 32:36] = w_in[:, 4612:4616]
    slabs = [slab(inputs["w_mem_kv"][0][:, P * j:P * (j + 1)]) for j in range(8)] + [slab(gif)]
    side = [P * j for j in range(4)] + [4616 + P * j for j in range(4)]
    side += [5128 + 1024 * b + P * j for j in range(8) for b in range(3)]
    for h in range(HEADS):
        for c0 in (v0, q0, k0, o0):
            slabs += [slab(w_in[:, c0 + 256 * h + P * i:c0 + 256 * h + P * (i + 1)]) for i in range(2)]
        slabs += [slab(w_in[:, side[8 * h + c]:side[8 * h + c] + P]) for c in range(8)]
        slabs += [slab(inputs["w_br_mlstm"][0][256 * h:256 * (h + 1), 512 * i:512 * (i + 1)]) for i in range(2)]
    for name in ("w_br_pool", "w_br_xattn"):
        slabs += [slab(inputs[name][0][:, 256 * j:256 * (j + 1)]) for j in range(4)]
    slabs += [slab(inputs["w_out"][0][:, P * j:P * (j + 1)]) for j in range(8)]

    def ff1(c):
        return [slab(inputs["w_ff1"][0][:, 512 * c + P * j:512 * c + P * (j + 1)]) for j in range(4)]

    def ff2(c):
        return [slab(inputs["w_ff2"][0][512 * c:512 * (c + 1), 256 * j:256 * (j + 1)]) for j in range(4)]
    slabs += ff1(0)
    for c in range(7):
        slabs += ff1(c + 1) + ff2(c)
    slabs += ff2(7)
    return {
        "w_stream": np.stack(slabs),
        "xT": feat(x), "memT": feat(inputs["mem_prompt"][0]),
        "vecs": np.concatenate([vector(inputs[n][0]) for n in ("g_pre_mix", "g_mem", "g_post_mix", "g_pre_mlp",
                                                                "g_post_mlp", "pool_scale")], axis=1),
        "b_if": inputs["b_if"][0].reshape(2, 4).T,
        "w_pool": inputs["w_pool"][0].transpose(1, 0, 2),
        "poolbuf": inputs["state_pool_buf"][0].transpose(2, 0, 1).reshape(4, P, ND, 15).transpose(1, 0, 2, 3),
        "stC": inputs["state_mlstm_C"][0].reshape(ND, 4, 2, P, 256).transpose(1, 0, 3, 2, 4),
        "stn": inputs["state_mlstm_n"][0].reshape(ND, 1024),
        "stm": inputs["state_mlstm_m"][0].T,
        "ckT": inputs["cache_mem_k"][0].transpose(0, 3, 2, 1),
        "cv": inputs["cache_mem_v"][0].reshape(ND, 2, P, 512).transpose(0, 2, 1, 3),
    }


def kernel(**inputs):
    import numpy as np
    import concourse.bacc as bacc
    from concourse.bass_utils import run_bass_kernel_spmd

    nc = bacc.Bacc("TRN2", target_bir_lowering=False, num_devices=1)
    arrays, args = {}, []
    for name, a in lay_out({n: np.asarray(v) for n, v in inputs.items()}).items():
        arrays[name] = np.ascontiguousarray(a)
        args.append(nc.dram_tensor(name, a.shape, F32, kind="ExternalInput").ap())
    outs = {"o_y": (P, KD, N), "o_pool": (P, 4, 15), "o_C": (4, P, 2, 257), "o_m": (4, 1 + ND), "o_kv": (P, 8, MEM),
            "o_pool_s": (P, 480), "o_C_s": (4, ND, P, 2, 256), "o_n_s": (ND, 1024)}
    for name, shape in outs.items():
        args.append(nc.dram_tensor(name, shape, F32, kind="ExternalOutput").ap())
    for name, shape in (("d_side", (FILL, P, N)), ("d_x1", (P, KD, N)), ("d_qk", (4, ND, 512)), ("d_v", (P, 2, 512))):
        args.append(nc.dram_tensor(name, shape, F32, kind="Internal").ap())
    hybrid_layer(nc, *args)
    r = run_bass_kernel_spmd(nc, [arrays], core_ids=[0]).results[0]
    y = r["o_y"].transpose(1, 0, 2).reshape(D, N).T
    pool_p = r["o_pool"].transpose(2, 1, 0).reshape(1, 1, 15, 512)
    C_p = r["o_C"][:, :, :, 0:256].transpose(0, 3, 2, 1).reshape(1, 1, 4, 256, 256)
    n_p = r["o_C"][:, :, :, 256].transpose(0, 2, 1).reshape(1, 1, 4, 256)
    kv = r["o_kv"].transpose(1, 0, 2).reshape(1024, MEM).T
    pool_s = r["o_pool_s"].reshape(P, 4, ND, 15).transpose(2, 3, 1, 0).reshape(1, ND, 15, 512)
    C_s = r["o_C_s"].transpose(1, 0, 3, 2, 4).reshape(1, ND, 4, 256, 256)
    out = (y[0:T].reshape(1, T, D), y[T:].reshape(ND, 1, D), pool_p, C_p, n_p, r["o_m"][:, 0].reshape(1, 1, 4),
           kv[:, 0:512].reshape(1, 1, MEM, 4, P), kv[:, 512:].reshape(1, 1, MEM, 4, P),
           pool_s, C_s, r["o_n_s"].reshape(1, ND, 4, 256), r["o_m"][:, 1:].T.reshape(1, ND, 4))
    return tuple(np.ascontiguousarray(a) for a in out)
```

```python
import concourse.bass as bass
from concourse import mybir
from contextlib import ExitStack

F32 = mybir.dt.float32
F32R = mybir.dt.float32r
BF16 = mybir.dt.bfloat16
ACT = mybir.ActivationFunctionType
ALU = mybir.AluOpType
AX = mybir.AxisListType

P = 128
D = 1024
T = 1024
ND = 8
N = T + ND
NG = 3
G = N // NG
KD = D // P
HEADS = 4
L = 128
NC = T // L
MEM = 256
FILL = 32
EPS = 1e-6
MASKED = -1e30
K_SCALE = 1.0 / 16.0
X_SCALE = float(128) ** -0.5

SLAB_GATE = 0
SLAB_MEM = 1
SLAB_HEAD = 9
SLABS_PER_HEAD = 18
SLAB_MERGE = SLAB_HEAD + HEADS * SLABS_PER_HEAD
SLAB_OUT = SLAB_MERGE + 8
SLAB_FF = SLAB_OUT + 8
SLABS = SLAB_FF + 64

UNIT_HEAD = 1
UNITS_PER_HEAD = 24
UNIT_POOL = UNIT_HEAD + HEADS * UNITS_PER_HEAD
UNIT_MERGE = UNIT_POOL + 4
UNIT_OUT = UNIT_MERGE + 16
UNIT_FF = UNIT_OUT + 8
UNIT_FF_LOOP = UNIT_FF + 4
UNITS_PER_FF_STEP = 24
UNIT_FF_TAIL = UNIT_FF_LOOP + 3 * UNITS_PER_FF_STEP
V_PRE, V_MEM, V_POST, V_MLP, V_FF, V_POOL = 0, 8, 16, 24, 32, 40
B_, WI_, WE_, EM_ = range(4)


def hybrid_layer(nc, w_stream, xT, memT, vecs, b_if, w_pool, poolbuf, stC, stn, stm, ckT, cv,
                 o_y, o_pool, o_C, o_m, o_kv, o_pool_s, o_C_s, o_n_s,
                 d_side, d_x1, d_qk, d_v):
    with ExitStack() as ctx:
        def sb(name, shape, dt=F32):
            return ctx.enter_context(nc.sbuf_tensor(name, shape, dt))

        def overlap(*groups):
            sizes = []
            made = []
            for group in groups:
                with ExitStack() as own:
                    made.append([own.enter_context(nc.sbuf_tensor(n, s, d)) for n, s, d in group])
                size = 0
                for _, s, d in group:
                    b = 2 if d == BF16 else 4
                    for e in s[1:]:
                        b *= e
                    size += -(-b // 32) * 32
                sizes.append(size)
            ctx.enter_context(nc.sbuf_tensor(f"room_{groups[0][0][0]}", [P, max(sizes) // 4], F32))
            return made

        (h_hi, h_lo), (u_pad, xq, kv_in, v_in, P_sb, PT_sb, cache_t, xs_t,
                          dec_scores, dec_exp, dec_probs, dec_out), (mem_sq,), (x1_back,) = overlap(
            [("h_hi", [P, KD, N], F32R), ("h_lo", [P, KD, N], F32R)],
            [("u_pad", [P, 4, 16 + N], F32), ("xq", [P, 4, N], F32), ("kv_in", [P, 4, MEM], F32),
             ("v_in", [P, 2, 512], F32), ("P_sb", [P, 4, MEM], F32), ("PT_sb", [P, 8, P], F32),
             ("cache_t", [P, 2, 4 * MEM], F32), ("xs_t", [P, 4, P], F32), ("dec_scores", [P, 64], F32),
             ("dec_exp", [32, MEM], F32), ("dec_probs", [P, 64], F32),
             ("dec_out", [P, 4, ND], F32)],
            [("mem_sq", [P, KD, MEM], F32)],
            [("x1_back", [P, KD, N], F32)])
        (acc,), (R, gf, gi, lf, bb, mm_, tg, wi_diag, mprev, wsel, mem_std) = overlap(
            [("acc", [P, KD, N], F32)],
            [("R", [P, N], F32), ("gf", [4, N], F32), ("gi", [4, N], F32), ("lf", [4, N], F32),
             ("bb", [4, N], F32), ("mm_", [4, N], F32), ("tg", [4, N], F32), ("wi_diag", [4, NC + 2 * ND, 4], F32), ("mprev", [4, NC + 1], F32),
             ("wsel", [4, NC + 2 * ND], F32), ("mem_std", [P, 2, MEM], F32)])
        ((q_h, k_h, kw_all, v_all, o_h, y_hi, y_lo, side_t, qs, ks, kw, SW, Cn, num,
          dC, qkb, dtmp, ns),
         (x_in, mem_in, rstd0, rstd0b, sq0, m_hi, m_lo),
         (yp_hi, yp_lo, yx_hi, yx_lo, gates),
         (_p0, _p1, win_a, win_b, pool_d, inv_count, bufT, wp,
          win_c, win_d, win_e, win_f),
         (f_hi, f_lo, rl, sqv)) = overlap(
            [("q_h", [P, 2, N], F32), ("k_h", [P, 2, N], F32), ("kw_all", [P, NC, 256], F32),
             ("v_all", [P, NC, 257], F32), ("o_h", [P, 2, N], F32), ("y_hi", [P, 2, N], F32R),
             ("y_lo", [P, 2, N], F32R), ("side_t", [P, N], F32), ("qs", [P, 2, L], F32),
             ("ks", [P, 2, L], F32), ("kw", [P, 256], F32), ("SW", [P, L], F32),
             ("Cn", [P, 2, 257], F32), ("num", [P, 257], F32),
             ("dC", [P, 2, 256], F32), ("qkb", [P, 512], F32), ("dtmp", [P, 2, 256], F32), ("ns", [ND, 1024], F32)],
            [("x_in", [P, KD, N], F32), ("mem_in", [P, KD, MEM], F32), ("rstd0", [P, N], F32),
             ("rstd0b", [P, N], F32), ("sq0", [P, 2, N], F32),
             ("m_hi", [P, KD, MEM], F32R), ("m_lo", [P, KD, MEM], F32R)],
            [("yp_hi", [P, 4, N], F32R), ("yp_lo", [P, 4, N], F32R), ("yx_hi", [P, 4, N], F32R),
             ("yx_lo", [P, 4, N], F32R), ("gates", [P, NG, 3, G], F32)],
            [("_p0", [P, 4, N], F32R), ("_p1", [P, 4, N], F32R), ("win_a", [P, 16 + N], F32),
             ("win_b", [P, 16 + N], F32), ("pool_d", [P, 2, N], F32), ("inv_count", [P, 16], F32),
             ("bufT", [P, 4, ND, 15], F32), ("wp", [P, 4, P], F32),
             ("win_c", [P, 16 + N], F32), ("win_d", [P, 16 + N], F32), ("win_e", [P, 16 + N], F32),
             ("win_f", [P, 16 + N], F32)],
            [("f_hi", [P, 2, 4, N], F32R), ("f_lo", [P, 2, 4, N], F32R), ("rl", [P, NG, G], F32),
             ("sqv", [P, NG, G], F32)])
        kvT = mem_in
        v_tok = sq0[:, 0, 0:1024].rearrange("p (m n) -> p m n", m=2)
        w_raw = sb("w_raw", [P, 2, 1024])
        w_hi = sb("w_hi", [P, 2, 1024], F32R)
        w_lo = sb("w_lo", [P, 2, 1024], F32R)
        vec = sb("vec", [P, 44])
        bif = sb("bif", [4, 2])
        ident = sb("ident", [P, P])
        ident_b = sb("ident_b", [P, P], BF16)
        mask_b = sb("mask_b", [P, P], BF16)
        ones = sb("ones", [P, P])
        eps = sb("eps", [P, 1])
        A_row = sb("A_row", [4, N])
        A_pick = sb("A_pick", [4, L])
        cols = sb("cols", [P, NC + 1, 4, 4])
        col = sb("col", [P, 5])
        decays = sb("decays", [P, NC, 4])
        dw = sb("dw", [P, 2, ND, 4])
        m_out = sb("m_out", [4, 1 + ND])
        m0 = sb("m0", [4, ND])
        wv = sb("wv", [P, 2, ND])
        qkd = sb("qkd", [ND, 512])
        dcol = sb("dcol", [ND, 8])
        rdiag = sb("rdiag", [ND, ND])
        num_d = sb("num_d", [P, 2, ND])
        yd = sb("yd", [P, 2, ND])
        den = sb("den", [P, 4])
        sm = sb("sm", [P, 16])

        bank = [ctx.enter_context(nc.psum_tensor(f"bank{i}", [P, 512], F32)) for i in range(8)]
        b_S, b_W, b_N, b_I, b_U = bank[3:8]

        def sem(name):
            return ctx.enter_context(nc.semaphore(name))

        s_consts = sem("consts")
        s_masks = sem("masks")
        s_const_loaded = sem("const_loaded")
        s_mem_loaded = sem("mem_loaded")
        s_slab_split = sem("slab_split")
        s_mem_sq = sem("mem_sq")
        s_mem_ssq = sem("mem_ssq")
        s_mem_std = sem("mem_std")
        s_mem_h = sem("mem_h")
        s_mem_hi = sem("mem_hi")
        s_mem_lo = sem("mem_lo")
        s_mem_ready = sem("mem_ready")
        s_mem_taken = sem("mem_taken")
        s_memv_t = sem("memv_t")
        s_memv_taken = sem("memv_taken")
        s_kv_stored = sem("kv_stored")
        s_x_sq = sem("x_sq")
        s_x_sq_used = sem("x_sq_used")
        s_x_std = sem("x_std")
        s_x_h = sem("x_h")
        s_x_hi = sem("x_hi")
        s_x_lo = sem("x_lo")
        s_x_lo_pool = sem("x_lo_pool")
        s_ns_loaded = sem("ns_loaded")
        s_gate_row = sem("gate_row")
        s_gate_act = sem("gate_act")
        s_rows_ready = sem("rows_ready")
        s_table_t = sem("table_t")
        s_bcast_ready = sem("bcast_ready")
        s_vT_ready = sem("vT_ready")
        s_vT_taken = sem("vT_taken")
        s_kT_ready = sem("kT_ready")
        s_kT_taken = sem("kT_taken")
        s_dqk_ready = sem("dqk_ready")
        s_dqk_taken = sem("dqk_taken")
        s_dqk_stored = sem("dqk_stored")
        s_col_set = sem("col_set")
        s_staged = sem("staged")
        s_scores_ready = sem("scores_ready")
        s_logw_ready = sem("logw_ready")
        s_weights_ready = sem("weights_ready")
        s_weighted_ready = sem("weighted_ready")
        s_carried_ready = sem("carried_ready")
        s_update_ready = sem("update_ready")
        s_carried_scaled = sem("carried_scaled")
        s_num_ready = sem("num_ready")
        s_den_step = sem("den_step")
        s_hn_ready = sem("hn_ready")
        s_hT_ready = sem("hT_ready")
        s_yv_ready = sem("yv_ready")
        s_yhi_ready = sem("yhi_ready")
        s_ylo_ready = sem("ylo_ready")
        s_C_new = sem("C_new")
        s_dstate_loaded = sem("dstate_loaded")
        s_dstate_used = sem("dstate_used")
        s_dstate_stored = sem("dstate_stored")
        s_dkv_ready = sem("dkv_ready")
        s_spilled = sem("spilled")
        s_dnorm_step = sem("dnorm_step")
        s_dinv_diag = sem("dinv_diag")
        s_dinv_all = sem("dinv_all")
        s_dy_gated = sem("dy_gated")
        s_dy_scaled = sem("dy_scaled")
        s_dy_hi = sem("dy_hi")
        s_dy_ready = sem("dy_ready")
        s_C_stored = sem("C_stored")
        s_wv_ready = sem("wv_ready")
        s_n_stored = sem("n_stored")
        s_dve_step = sem("dve_step")
        s_dstate_new = sem("dstate_new")
        s_u_loaded = sem("u_loaded")
        s_xq_loaded = sem("xq_loaded")
        s_pool_state_ready = sem("pool_state_ready")
        s_pool_d_ready = sem("pool_d_ready")
        s_cleared = sem("cleared")
        s_window_step = sem("window_step")
        s_pool_in_loaded = sem("pool_in_loaded")
        s_pool_hi = sem("pool_hi")
        s_pool_stored = sem("pool_stored")
        s_kv_loaded = sem("kv_loaded")
        s_xs_staged = sem("xs_staged")
        s_xscores_ready = sem("xscores_ready")
        s_xstep = sem("xstep")
        s_xbias_ready = sem("xbias_ready")
        s_xexp_ready = sem("xexp_ready")
        s_xprob_ready = sem("xprob_ready")
        s_xprobT_ready = sem("xprobT_ready")
        s_xprobT_taken = sem("xprobT_taken")
        s_xo_ready = sem("xo_ready")
        s_xo_hi = sem("xo_hi")
        s_xo_lo = sem("xo_lo")
        s_dscores_taken = sem("dscores_taken")
        s_dtransposed = sem("dtransposed")
        s_dexp_ready = sem("dexp_ready")
        s_dprob_ready = sem("dprob_ready")
        s_dprobT_taken = sem("dprobT_taken")
        s_dattn_hi = sem("dattn_hi")
        s_dattn_lo = sem("dattn_lo")
        s_dkeys_used = sem("dkeys_used")
        s_dvalues_used = sem("dvalues_used")
        s_dvalues_taken = sem("dvalues_taken")
        s_g_sig = sem("g_sig")
        s_xg_sig = sem("xg_sig")
        s_acc_gated = sem("acc_gated")
        s_pool_added = sem("pool_added")
        s_merged = sem("merged")
        s_merged_hi = sem("merged_hi")
        s_merged_lo = sem("merged_lo")
        s_z_acc = sem("z_acc")
        s_z_ssq = sem("z_ssq")
        s_z_std = sem("z_std")
        s_x2_loaded = sem("x2_loaded")
        s_z_scaled = sem("z_scaled")
        s_x1_ready = sem("x1_ready")
        s_x1_sq = sem("x1_sq")
        s_x1_ssq = sem("x1_ssq")
        s_x1_std = sem("x1_std")
        s_x1_stored = sem("x1_stored")
        s_h2_ready = sem("h2_ready")
        s_h2_hi = sem("h2_hi")
        s_h2_lo = sem("h2_lo")
        s_h2_lo_pool = sem("h2_lo_pool")
        s_relu_squared = sem("relu_squared")
        s_f_hi = sem("f_hi")
        s_f_lo = sem("f_lo")
        s_f_squared = sem("f_squared")
        s_f_ssq = sem("f_ssq")
        s_f_std = sem("f_std")
        s_x3_loaded = sem("x3_loaded")
        s_y_scaled = sem("y_scaled")
        s_y_ready = sem("y_ready")
        s_y_ready_pool = sem("y_ready_pool")
        s_y_stored = sem("y_stored")
        s_hi_made = sem("hi_made")
        s_x_loaded = [sem(f"x_loaded{i}") for i in range(3)]
        s_slab_loaded = [sem(f"slab_loaded{i}") for i in range(2)]
        s_g_loaded = [sem(f"g_loaded{i}") for i in range(3)]
        s_xg_loaded = [sem(f"xg_loaded{i}") for i in range(2)]
        s_cache_loaded = [sem(f"cache_loaded{i}") for i in range(2)]
        s_group_ready = [sem(f"group_ready{i}") for i in range(3)]
        s_group_free = [sem(f"group_free{i}") for i in range(3)]
        block = ctx.enter_context(nc.Block())
        tok = [slice(g * G, (g + 1) * G) for g in range(NG)]
        blocks = [(j, g) for j in range(4) for g in range(NG)]
        first_blocks = [(j, g) for g in range(NG) for j in range(2)] + blocks[6:]
        z_last = [(6, 0), (6, 1), (7, 0), (7, 1), (6, 2), (7, 2)]
        f_last = [(4, 0), (5, 0), (4, 1), (5, 1), (6, 0), (7, 0), (6, 1), (7, 1), (4, 2), (5, 2), (6, 2), (7, 2)]

        def sq_ring(i):
            return sq0[:, i // 3, (i % 3) * G:(i % 3 + 1) * G]

        @block.sync
        def _(sp):
            def slab(n, slot, split):
                if split is not None:
                    sp.wait_ge(s_slab_split, split)
                src = w_stream[n] if isinstance(n, int) else w_stream[bass.ds(n, 1)].rearrange("a p c -> (a p) c")
                sp.dma_start(w_raw[:, slot, :], src).then_inc(s_slab_loaded[slot], 16)

            sp.dma_start(x_in[:, :, tok[0]], xT[:, :, tok[0]]).then_inc(s_x_loaded[0], 16)
            sp.dma_start(mem_in[:, :, :], memT).then_inc(s_mem_loaded, 16)
            slab(0, 0, None)
            sp.dma_start(vec[:, :], vecs).then_inc(s_const_loaded, 16)
            sp.dma_start(bif[:, :], b_if).then_inc(s_const_loaded, 16)
            sp.dma_start(m0[:, :], stm).then_inc(s_const_loaded, 16)
            for g in (1, 2):
                sp.dma_start(x_in[:, :, tok[g]], xT[:, :, tok[g]]).then_inc(s_x_loaded[g], 16)
            slab(1, 1, None)
            for n in range(2, SLAB_HEAD + 2):
                slab(n, n % 2, n - 1)
            sp.wait_ge(s_mem_ready, 8)
            sp.dma_start(ns[:, :], stn).then_inc(s_ns_loaded, 16)
            with sp.Fori(0, HEADS) as h:
                for j in range(2, 10):
                    slab(SLAB_HEAD + SLABS_PER_HEAD * h + j, (SLAB_HEAD + j) % 2,
                         SLAB_HEAD + SLABS_PER_HEAD * h + j - 1)
                with sp.Fori(0, NC // 2) as c2:
                    for e in range(2):
                        c = 2 * c2 + e
                        sp.wait_ge(s_dqk_stored, 16 * (h + 1))
                        sp.dma_start(dC[:, :, :], stC[bass.ds(h, 1), bass.ds(c, 1)].rearrange("a b p k c -> (a b p) k c"))\
                            .then_inc(s_dstate_loaded, 16)
                        sp.dma_start(qkb[:, :], d_qk[bass.ds(h, 1), bass.ds(c, 1)].rearrange("a b n -> (a b) n")
                                     .to_broadcast([P, 512])).then_inc(s_dstate_loaded, 16)
                        sp.wait_ge(s_dstate_used, NC * h + c + 1)
                        sp.dma_start(o_C_s[bass.ds(h, 1), bass.ds(c, 1)].rearrange("a b p k c -> (a b p) k c"), dC[:, :, :])\
                            .then_inc(s_dstate_stored, 16)
                        sp.wait_ge(s_dstate_stored, 16 * (NC * h + c + 1))
                        n = SLAB_HEAD + SLABS_PER_HEAD * h + 10 + c
                        slab(n, (SLAB_HEAD + e) % 2, n - 1)
                for j in range(2):
                    n = SLAB_HEAD + SLABS_PER_HEAD * (h + 1) + j
                    slab(n, (SLAB_HEAD + j) % 2, n - 1)
            sp.wait_ge(s_spilled, 16 * (FILL + 1))
            sp.wait_ge(s_group_ready[2], UNIT_HEAD + UNITS_PER_HEAD * (HEADS - 1) + 16)
            for k in range(4):
                sp.dma_start(u_pad[:, k, 16:16 + N], d_side[k]).then_inc(s_u_loaded, 16)
            for k in range(4):
                sp.dma_start(xq[:, k, :], d_side[4 + k]).then_inc(s_xq_loaded, 16)

            def cache(b, slot, values):
                src = (cv if values else ckT)[bass.ds(b, 1)].rearrange("a p k c -> (a p) (k c)")
                sp.dma_start(cache_t[:, slot, :], src).then_inc(s_cache_loaded[slot], 16)

            def keys(b):
                dst = (cache_t[:, 0, :], cache_t[:, 1, :], P_sb[:, :, :], PT_sb[:, :, :])[b % 4]
                if b % 4 >= 2:
                    dst = dst.rearrange("p a b -> p (a b)")
                sp.dma_start(dst, ckT[b].rearrange("p k c -> p (k c)")).then_inc(s_cache_loaded[b // 2 % 2], 16)
            keys(0)
            keys(1)
            sp.wait_ge(s_group_ready[2], UNIT_POOL)
            sp.dma_start(bufT[:, :, :, :], poolbuf).then_inc(s_pool_in_loaded, 16)
            sp.dma_start(wp[:, :, :], w_pool).then_inc(s_pool_in_loaded, 16)
            keys(2)
            keys(3)
            sp.dma_start(kv_in[:, :, :], o_kv[:, 0:4, :]).then_inc(s_kv_loaded, 16)
            sp.dma_start(v_in[:, :, :], d_v).then_inc(s_kv_loaded, 16)
            for b in range(4, ND):
                sp.wait_ge(s_dkeys_used, b - 3)
                keys(b)
            sp.wait_ge(s_n_stored, 32)
            sp.wait_ge(s_C_stored, 64)

            def pool_gates(j):
                for g in range(NG):
                    if not isinstance(j, int) or j:
                        sp.wait_ge(s_pool_added, NG * (j - 1) + g + 1)
                    sp.dma_start(gates[:, g, 0:2, :], d_side[bass.ds(8 + 3 * j, 2), :, tok[g]].rearrange("b p t -> p b t"))\
                        .then_inc(s_g_loaded[g], 16)

            def attention_gates(j):
                sp.dma_start(gates[:, :, (2, 0)[j % 2], :], d_side[8 + 3 * j + 2].rearrange("p (g t) -> p g t", g=NG))\
                    .then_inc(s_xg_loaded[j % 2], 16)

            def m_slab(i):
                slab(SLAB_MERGE + i, (SLAB_MERGE + i) % 2, SLAB_MERGE + i - 1)
            for e in range(2):
                sp.wait_ge(s_dkeys_used, (5, 7)[e])
                cache(e, e, True)
            sp.wait_ge(s_group_ready[2], UNIT_MERGE)
            pool_gates(0)
            m_slab(2)
            m_slab(3)
            attention_gates(0)
            for c in range(NC):
                if c + 2 < ND:
                    sp.wait_ge(s_dvalues_used, c + 1)
                    cache(c + 2, c % 2, True)
                if c + 1 < NC:
                    pool_gates(c + 1)
                if c % 2:
                    m_slab(4 + c // 2)
            for j in range(1, 8):
                if j == 1:
                    sp.wait_ge(s_pool_added, NG * 8)
                else:
                    sp.wait_ge(s_merged, NG * (j - 1))
                attention_gates(j)
                if j % 2 == 0:
                    m_slab(7 + j // 2)
            m_slab(11)
            sp.wait_ge(s_merged_lo, 24)
            sp.wait_ge(s_group_ready[2], UNIT_OUT)
            sp.dma_start(x_in[:, :, :], xT).then_inc(s_x2_loaded, 16)
            with sp.Fori(SLAB_MERGE + 12, SLABS - 1, 2) as n:
                slab(n, (SLAB_MERGE + 12) % 2, n - 1)
                slab(n + 1, (SLAB_MERGE + 13) % 2, n)
            sp.wait_ge(s_group_ready[2], UNIT_FF_TAIL + 4)
            sp.wait_ge(s_x1_stored, 16)
            sp.dma_start(x1_back[:, :, :], d_x1).then_inc(s_x3_loaded, 16)
            for g in range(NG):
                sp.wait_ge(s_y_ready_pool, 5 * (g + 1))
                sp.dma_start(o_y[:, 0:5, tok[g]], x1_back[:, 0:5, tok[g]]).then_inc(s_y_stored, 16)
                sp.wait_ge(s_y_ready, (KD - 5) * (g + 1))
                sp.dma_start(o_y[:, 5:KD, tok[g]], x1_back[:, 5:KD, tok[g]]).then_inc(s_y_stored, 16)
            sp.wait_ge(s_y_stored, 16 * 2 * NG)

        @block.gpsimd
        def _(pool):
            for tile_, value in ((ident, 0.0), (ident_b, 0.0), (mask_b, 0.0), (ones, 1.0), (eps, EPS)):
                pool.memset(tile_[:, :], value).then_inc(s_consts, 1)
            pool.wait_ge(s_consts, 5)
            for tile_ in (ident, ident_b):
                pool.affine_select(out=tile_[:, :], in_=tile_[:, :], compare_op=ALU.not_equal, fill=1.0, base=0,
                                   pattern=[[-1, P]], channel_multiplier=1).then_inc(s_masks, 1)
            pool.affine_select(out=mask_b[:, :], in_=mask_b[:, :], compare_op=ALU.is_ge, fill=MASKED, base=0,
                               pattern=[[1, P]], channel_multiplier=-1).then_inc(s_masks, 1)

            def split(n, slot, used=None, by_scalar=False):
                pool.wait_ge(s_slab_loaded[slot], 16 * (n // 2 + 1) if isinstance(n, int) else 8 * (n - slot) + 16)
                if used is not None:
                    pool.wait_ge(*used)
                if by_scalar:
                    pool.wait_ge(s_hi_made, n + 1)
                    pool.tensor_tensor(w_lo[:, slot, :], w_raw[:, slot, :], w_hi[:, slot, :].bitcast(F32), ALU.subtract)\
                        .then_inc(s_slab_split, 1)
                    return
                pool.tensor_tensor(w_hi[:, slot, :], w_raw[:, slot, :], ones[:, 0:1].to_broadcast([P, 1024]), ALU.mult).then_inc(s_hi_made, 1)
                pool.wait_ge(s_hi_made, n + 1)
                pool.tensor_tensor(w_lo[:, slot, :], w_raw[:, slot, :], w_hi[:, slot, :].bitcast(F32), ALU.subtract)\
                    .then_inc(s_slab_split, 1)

            pool.memset(R[:, :], 0.0).then_inc(s_masks, 1)
            split(0, 0)

            def x_lo(g):
                for k in range(KD // 2):
                    pool.wait_ge(s_x_hi, g * KD + k + 1)
                    pool.tensor_tensor(h_lo[:, k, tok[g]], x_in[:, k, tok[g]], h_hi[:, k, tok[g]].bitcast(F32), ALU.subtract)\
                        .then_inc(s_x_lo_pool, 1)
            split(1, 1)
            x_lo(0)
            pool.wait_ge(s_mem_hi, 1)
            pool.tensor_tensor(m_lo[:, :, :], mem_in[:, :, :], m_hi[:, :, :].bitcast(F32), ALU.subtract).then_inc(s_mem_lo, 1)
            x_lo(1)
            x_lo(2)
            for n in range(2, SLAB_HEAD):
                split(n, n % 2, by_scalar=True)
            for n in (SLAB_HEAD, SLAB_HEAD + 1):
                split(n, n % 2, (s_mem_ready, n - 2))
            pool.wait_ge(s_bcast_ready, 1)
            pool.memset(acc[:, :, :], 0.0).then_inc(s_cleared, 1)
            with pool.Fori(0, HEADS) as h:
                for j in range(2, SLABS_PER_HEAD + 2):
                    d = j - 2
                    units = d + 1 if d < 16 else 20 + 4 * (d - 16)
                    split(SLAB_HEAD + SLABS_PER_HEAD * h + j, (SLAB_HEAD + j) % 2,
                          (s_group_ready[2], UNIT_HEAD + UNITS_PER_HEAD * h + units))

            def split_merge(j, by_scalar=False):
                d = j - 2
                units = UNIT_MERGE + 2 * (d + 1) if d < 8 else UNIT_OUT + d - 7
                split(SLAB_MERGE + j, (SLAB_MERGE + j) % 2, (s_group_ready[2], units), by_scalar)
            pool.wait_ge(s_cleared, 2)
            pool.wait_ge(s_u_loaded, 64)
            for w, wins in ((2, (win_c, win_d)), (3, (win_e, win_f))):
                src = u_pad[:, w, :]
                for i in range(w + 1):
                    dst = wins[i % 2]
                    pool.tensor_tensor(dst[:, 16:], src[:, 16:16 + N], src[:, 16 - (1 << i):16 + N - (1 << i)], ALU.add)\
                        .then_inc(s_window_step, 1)
                    steps = (0, 0, 0, 3)[w] + i + 1
                    pool.wait_ge(s_window_step, steps)
                    src = dst
            pool.wait_ge(s_xq_loaded, 64)
            for c in range(NC):
                if c:
                    pool.wait_ge(s_xbias_ready, c + 1)
                pool.tensor_copy(xs_t[:, :, :], xq[:, :, c * L:(c + 1) * L]).then_inc(s_xs_staged, 1)
                if c >= 2 and c % 2 == 0:
                    split_merge(1 + c // 2)
            for j in range(5, 16):
                split_merge(j)
            pool.wait_ge(s_x2_loaded, 16)
            for g in range(NG):
                for k in range(KD):
                    pool.wait_ge(s_z_scaled, g * KD + k + 1)
                    pool.tensor_tensor(x_in[:, k, tok[g]], x_in[:, k, tok[g]], acc[:, k, tok[g]], ALU.add).then_inc(s_x1_ready, 1)
                if g:
                    split_merge(15 + g, True)
            for g in range(NG):
                for k in range(KD // 2):
                    pool.wait_ge(s_h2_hi, g * KD + k + 1)
                    pool.tensor_tensor(h_lo[:, k, tok[g]], acc[:, k, tok[g]], h_hi[:, k, tok[g]].bitcast(F32), ALU.subtract)\
                        .then_inc(s_h2_lo_pool, 1)
            split_merge(18)
            split_merge(19)
            pool.wait_ge(s_h2_lo, NG * KD // 2)
            pool.memset(acc[:, :, :], 0.0).then_inc(s_cleared, 1)
            done = [0, 1] + [1, 2, 3, 4] + [6, 8, 10, 12] + [13, 14, 15, 16] + [18, 20]
            done[0] = -1
            done[1] = 0
            with pool.Fori(0, 3) as i:
                for j in range(16):
                    split(SLAB_FF + 4 + 16 * i + j, (SLAB_FF + j) % 2,
                          (s_group_ready[2], UNIT_FF_LOOP + UNITS_PER_FF_STEP * i + done[j]))
            tail = [-1, 0, 1, 2, 3, 4, 6, 8, 10, 12, 14, 16]
            for j in range(12):
                n = SLAB_FF + 52 + j
                split(n, n % 2, (s_group_ready[2], UNIT_FF_TAIL + tail[j]))
            pool.wait_ge(s_x3_loaded, 16)
            for g in range(NG):
                for k in range(5):
                    pool.wait_ge(s_y_scaled, g * KD + k + 1)
                    pool.tensor_tensor(x1_back[:, k, tok[g]], x1_back[:, k, tok[g]], acc[:, k, tok[g]], ALU.add)\
                        .then_inc(s_y_ready_pool, 1)

        @block.tensor
        def _(pe):
            def product(out, blocks, passes3=True):
                n = 3 * len(blocks) if passes3 else len(blocks)
                i = 0
                for b in blocks:
                    for st, mv in (((b[0], b[2]), (b[1], b[2]), (b[0], b[3])) if passes3 else (b,)):
                        last = pe.matmul(out, st, mv, start=i == 0, stop=i == n - 1)
                        i += 1
                return last

            def group(g, t, blocks, passes3=True, bank_of=None):
                if not (isinstance(t, int) and t == 0):
                    pe.wait_ge(s_group_free[g], t if bank_of is None else t - 1)
                product(bank[g + 3 * (bank_of or 0)][:, 0:G], blocks, passes3).then_inc(s_group_ready[g], 1)

            def w_blocks(slot, count, width, col0):
                return [(w_hi[:, slot, k * width + col0:k * width + col0 + P],
                         w_lo[:, slot, k * width + col0:k * width + col0 + P]) for k in range(count)]

            def h_group(slot, g, t, bank_of=None):
                group(g, t, [(a, b, h_hi[:, k, tok[g]], h_lo[:, k, tok[g]])
                             for k, (a, b) in enumerate(w_blocks(slot, KD, P, 0))], True, bank_of)

            def h_unit(n, slot, t):
                pe.wait_ge(s_slab_split, n + 1)
                for g in range(NG):
                    h_group(slot, g, t)

            pe.wait_ge(s_consts, 5)
            pe.wait_ge(s_masks, 3)
            for g in range(NG):
                if g == 1:
                    pe.wait_ge(s_mem_sq, 1)
                    for k in range(KD):
                        last = pe.matmul(b_U[:, 0:MEM], ones[:, :], mem_sq[:, k, :], start=k == 0, stop=k == 7)
                    last.then_inc(s_mem_ssq, 1)
                for k in range(KD):
                    i = g * KD + k
                    pe.wait_ge(s_x_sq, i + 1)
                    pe.matmul((b_S, b_W, b_N)[g][:, 0:G], ones[:, :], sq_ring(i % 6), start=k == 0, stop=k == 7)\
                        .then_inc(s_x_sq_used, 1)
            pe.wait_ge(s_slab_split, SLAB_GATE + 1)
            for g in range(NG):
                pe.wait_ge(s_x_lo, KD // 2 * (g + 1))
                pe.wait_ge(s_x_lo_pool, KD // 2 * (g + 1))
                h_group(SLAB_GATE % 2, g, 0)
            def gate_tables():
                pe.wait_ge(s_rows_ready, 1)
                for c in range(NC + 1):
                    w = L if c < NC else ND
                    b = (b_S, b_W, b_N)[c // 4]
                    last = pe.transpose(b[0:w, (c % 4) * P:(c % 4 + 1) * P], R[:, c * L:c * L + w], ident[:, :])
                    if c in (3, 7, 8):
                        last.then_inc(s_table_t, 1)
                pe.matmul(b_N[:, 256:352], ones[0:4, :], wi_diag[:, :, :].rearrange("p c h -> p (c h)"),
                          start=True, stop=True).then_inc(s_bcast_ready, 1)

            pe.wait_ge(s_mem_lo, 1)
            for n in range(8):
                if n == 7:
                    gate_tables()
                pe.wait_ge(s_slab_split, SLAB_MEM + n + 1)
                if n >= 2:
                    pe.wait_ge(s_mem_taken, n - 1)
                product((b_I, b_U)[n % 2][:, 0:MEM], [(a, b, m_hi[:, k, :], m_lo[:, k, :])
                        for k, (a, b) in enumerate(w_blocks((SLAB_MEM + n) % 2, KD, P, 0))]).then_inc(s_mem_ready, 1)
            pe.wait_ge(s_mem_taken, 8)
            for m in range(2):
                for j in range(4):
                    last = pe.transpose((b_I, b_U)[m][:, j * P:(j + 1) * P], kvT[:, 4 + j, m * P:(m + 1) * P], ident[:, :])
                last.then_inc(s_memv_t, 1)

            b_tr = (b_S, b_W, b_N, b_I)
            with pe.Fori(0, HEADS) as h:
                n0 = SLAB_HEAD + SLABS_PER_HEAD * h
                t0 = UNIT_HEAD + UNITS_PER_HEAD * h
                sl = [(SLAB_HEAD + j) % 2 for j in range(SLABS_PER_HEAD)]

                def transposes(src, ready, taken):
                    for r in range(4):
                        for c in (2 * r, 2 * r + 1):
                            for k in range(2):
                                last = pe.transpose(b_tr[r][:, (c % 2) * 256 + k * P:(c % 2) * 256 + (k + 1) * P],
                                                    src[:, k, c * L:(c + 1) * L], ident[:, :])
                        last.then_inc(ready, 1)

                for j in range(3):
                    h_unit(n0 + j, sl[j], t0 + j)
                for g in range(NG):
                    pe.wait_ge(s_group_free[g], t0 + 2)
                transposes(o_h, s_vT_ready, None)
                for j in range(3, 7):
                    h_unit(n0 + j, sl[j], t0 + j)
                for g in range(NG):
                    pe.wait_ge(s_group_free[g], t0 + 6)
                pe.wait_ge(s_vT_taken, 4 * h + 4)
                transposes(k_h, s_kT_ready, None)
                for i, src in enumerate((q_h, k_h)):
                    for k in range(2):
                        last = pe.transpose(b_U[0:ND, (2 * i + k) * P:(2 * i + k + 1) * P], src[:, k, T:N], ident[:, :])
                last.then_inc(s_dqk_ready, 1)
                h_unit(n0 + 7, sl[7], t0 + 7)
                with pe.Fori(0, NC // 2) as c2:
                    for e in range(2):
                        c = 2 * c2 + e
                        i1 = NC * h + c + 1
                        t = t0 + 8 + c
                        n = n0 + 8 + c
                        slot = (SLAB_HEAD + e) % 2
                        pe.wait_ge(s_staged, i1)
                        for k in range(2):
                            last = pe.matmul(b_S[:, 0:L], ks[:, k, :], qs[:, k, :], start=k == 0, stop=k == 1)
                        last.then_inc(s_scores_ready, 1)
                        pe.matmul(b_W[:, 0:L], ident_b[:, :], mask_b[:, :], start=True, stop=False)
                        pe.matmul(b_W[:, 0:L], ones[0:4, :], A_pick[:, :], start=False, stop=True).then_inc(s_logw_ready, 1)
                        pe.wait_ge(s_slab_split, n + 1)
                        h_group(slot, 0, t)
                        pe.wait_ge(s_weighted_ready, i1)
                        vc = v_all[:, bass.ds(c, 1), :].rearrange("p a n -> p (a n)")
                        pe.matmul(b_N[:, 0:257], SW[:, :], vc, start=True, stop=True)
                        for k in range(2):
                            pe.matmul(b_N[:, 260 + k:261 + k], kw[:, k * P:(k + 1) * P], ones[:, 0:1], start=True, stop=True)
                        for k in range(2):
                            last = pe.matmul(b_I[:, 0:257], qs[:, k, :], Cn[:, k, :], start=k == 0, stop=k == 1)
                        last.then_inc(s_carried_ready, 1)
                        for k in range(2):
                            last = pe.matmul(b_U[:, k * 256:(k + 1) * 256], kw[:, k * P:(k + 1) * P],
                                             v_all[:, bass.ds(c, 1), 0:256].rearrange("p a n -> p (a n)"), start=True, stop=True)
                        last.then_inc(s_update_ready, 1)
                        h_group(slot, 1, t)
                        pe.wait_ge(s_hn_ready, i1)
                        for k in range(2):
                            last = pe.transpose(b_S[:, P + k * P:P + (k + 1) * P], num[:, k * P:(k + 1) * P], ident[:, :])
                        last.then_inc(s_hT_ready, 1)
                        h_group(slot, 2, t)
                pe.wait_ge(s_dinv_diag, h + 1)
                pe.wait_ge(s_dy_gated, h + 1)
                pe.matmul(b_U[:, 0:ND], ones[0:ND, :], rdiag[:, :], start=True, stop=True).then_inc(s_dinv_all, 1)
                pe.wait_ge(s_ylo_ready, NC * h + NC)
                for j in range(8):
                    sj = 16 + j // 4
                    if j % 4 == 0:
                        pe.wait_ge(s_slab_split, n0 + sj + 1)
                    for g in range(NG):
                        if j == 0 and g == 2:
                            pe.wait_ge(s_dy_ready, h + 1)
                        group(g, t0 + 16 + j, [(a, b, y_hi[:, k, tok[g]], y_lo[:, k, tok[g]])
                                               for k, (a, b) in enumerate(w_blocks(sl[sj], 2, 512, (j % 4) * P))])

            pe.wait_ge(s_pool_in_loaded, 32)
            pe.wait_ge(s_xq_loaded, 64)
            for w in range(4):
                pe.wait_ge(s_cache_loaded[w % 2], 32 * (w // 2 + 1))
                for b in (2 * w, 2 * w + 1):
                    kb = (cache_t[:, 0, :], cache_t[:, 1, :], P_sb[:, :, :], PT_sb[:, :, :])[b % 4]
                    if b % 4 >= 2:
                        kb = kb.rearrange("p a b -> p (a b)")
                    for m in range(2):
                        for hh in range(4):
                            last = pe.matmul(b_N[:, m * 32 + hh * 8 + b:m * 32 + hh * 8 + b + 1],
                                             kb[:, hh * MEM + m * P:hh * MEM + (m + 1) * P],
                                             xq[:, hh, T + b:T + b + 1], start=True, stop=True)
                    last.then_inc(s_dkeys_used, 1)
                if w == 3:
                    pe.wait_ge(s_dscores_taken, 1)
                    for m in range(2):
                        last = pe.transpose(b_U[0:32, m * P:(m + 1) * P], dec_scores[:, m * 32:(m + 1) * 32], ident[:, :])
                    last.then_inc(s_dtransposed, 1)
                pe.wait_ge(s_pool_d_ready, w + 1)
                for g in range(NG):
                    group(g, UNIT_POOL + w, [(wp[:, w, :], pool_d[:, w % 2, tok[g]])], False)
            pe.wait_ge(s_dprob_ready, 1)
            for m in range(2):
                last = pe.transpose(b_N[:, m * 32:(m + 1) * 32], dec_exp[:, m * P:(m + 1) * P], ident[0:32, 0:32])
            last.then_inc(s_dtransposed, 1)
            pe.wait_ge(s_dprobT_taken, 1)

            def merge_group(i, e, g, branch, hi, lo):
                if g == 0 and e % 2 == 0:
                    pe.wait_ge(s_slab_split, SLAB_MERGE + 4 * branch + 2 * i + e // 2 + 1)
                wb = w_blocks((SLAB_MERGE + e // 2) % 2, 4, 256, (e % 2) * P)
                group(g, UNIT_MERGE + 8 * branch + 4 * i + e,
                      [(*wb[k], hi[:, k, tok[g]], lo[:, k, tok[g]]) for k in range(4)])
            pe.wait_ge(s_kv_loaded, 32)
            with pe.Fori(0, 2) as i:
                for e in range(4):
                    c = 4 * i + e
                    pe.wait_ge(s_xs_staged, c + 1)
                    for hh in range(4):
                        last = pe.matmul((b_S, b_W)[hh // 2][:, (hh % 2) * MEM:(hh % 2 + 1) * MEM], xs_t[:, hh, :], kv_in[:, hh, :],
                                         start=True, stop=True)
                        if hh % 2:
                            last.then_inc(s_xscores_ready, 1)
                    merge_group(i, e, 0, 0, yp_hi, yp_lo)
                    merge_group(i, e, 1, 0, yp_hi, yp_lo)
                    merge_group(i, e, 2, 0, yp_hi, yp_lo)
                    pe.wait_ge(s_xprob_ready, c + 1)
                    for q in range(8):
                        last = pe.transpose((b_N, b_I)[q // 4][:, (q % 4) * P:(q % 4 + 1) * P],
                                            P_sb[:, q // 2, (q % 2) * P:(q % 2 + 1) * P], ident[:, :])
                        if q % 4 == 3:
                            last.then_inc(s_xprobT_ready, 1)
                    pe.wait_ge(s_cache_loaded[e % 2], 64 + 16 * (2 * i + e // 2 + 1))
                    for hh in range(4):
                        for m in range(2):
                            last = pe.matmul(b_S[:, hh:hh + 1], cache_t[:, e % 2, m * 512 + hh * P:m * 512 + (hh + 1) * P],
                                             dec_probs[:, bass.ds(m * 32 + hh * 8 + c, 1)], start=m == 0, stop=m == 1)
                    last.then_inc(s_dvalues_used, 1)
                    for hh in range(4):
                        if hh % 2 == 0:
                            pe.wait_ge(s_xprobT_taken, 2 * c + 1 + hh // 2)
                        for m in range(2):
                            last = pe.matmul(b_U[:, hh * P:(hh + 1) * P], v_in[:, m, hh * P:(hh + 1) * P], PT_sb[:, 2 * hh + m, :],
                                             start=m == 0, stop=m == 1)
                    last.then_inc(s_xo_ready, 1)
                    pe.wait_ge(s_dvalues_taken, c + 1)
            pe.wait_ge(s_xo_lo, NC - 1)
            with pe.Fori(0, 2) as i:
                for e in range(4):
                    for g in range(NG):
                        if e == 0 and g == 2:
                            pe.wait_ge(s_xo_lo, NC)
                            pe.wait_ge(s_dattn_lo, 1)
                        merge_group(i, e, g, 1, yx_hi, yx_lo)
            with pe.Fori(0, 6, 2) as j2:
                for e in range(2):
                    pe.wait_ge(s_slab_split, SLAB_OUT + j2 + e + 1)
                    for g in range(NG):
                        if e == 0:
                            pe.wait_ge(s_merged_lo, 22 + g)
                        h_group((SLAB_OUT + e) % 2, g, UNIT_OUT + j2 + e)

            def z_mean(g):
                pe.wait_ge(s_z_acc, (24, 25, 27)[g])
                pe.matmul((b_I, b_U, b_S)[g][:, 0:G], ones[:, :], rstd0b[:, tok[g]], start=True, stop=True).then_inc(s_z_ssq, 1)

            for i, (j, g) in enumerate(z_last):
                if g == 0:
                    pe.wait_ge(s_slab_split, SLAB_OUT + j + 1)
                h_group((SLAB_OUT + j) % 2, g, UNIT_OUT + j, (None, 1)[j - 6])
                if i in (3, 4):
                    z_mean(i - 3)
            z_mean(2)
            for g in range(NG):
                for k in range(KD):
                    i = g * KD + k
                    pe.wait_ge(s_x1_sq, i + 1)
                    pe.matmul((b_W, b_N, b_I)[g][:, 0:G], ones[:, :], sq_ring(i % 6), start=k == 0, stop=k == 7).then_inc(s_x1_ssq, 1)
            def ff1(n, slots, t, first=0):
                for j in range(first, 4):
                    pe.wait_ge(s_slab_split, n + j + 1)
                    for g in range(NG):
                        h_group(slots[j], g, t + j)

            def ff2(n, slots, t, half, blocks_done, units=8):
                pe.wait_ge(s_f_lo, blocks_done)
                for j in range(units):
                    if j % 2 == 0:
                        pe.wait_ge(s_slab_split, n + j // 2 + 1)
                    for g in range(NG):
                        ff2_group(slots, t, half, j, g)

            def ff2_group(slots, t, half, j, g, bank_of=None):
                group(g, t + j, [(a, b, f_hi[:, half, k, tok[g]], f_lo[:, half, k, tok[g]])
                                 for k, (a, b) in enumerate(w_blocks(slots[j // 2], 4, 256, (j % 2) * P))], True, bank_of)

            def par(n0_):
                return [(n0_ + j) % 2 for j in range(4)]

            for g in range(NG):
                pe.wait_ge(s_h2_lo, KD // 2 * (g + 1))
                pe.wait_ge(s_h2_lo_pool, KD // 2 * (g + 1))
                for j in range(2):
                    if g == 0:
                        pe.wait_ge(s_slab_split, SLAB_FF + j + 1)
                    h_group((SLAB_FF + j) % 2, g, UNIT_FF + j, (None, 1)[j])
            ff1(SLAB_FF, par(SLAB_FF), UNIT_FF, 2)
            with pe.Fori(0, 3) as i:
                n0 = SLAB_FF + 4 + 16 * i
                t0 = UNIT_FF_LOOP + UNITS_PER_FF_STEP * i
                p = par(SLAB_FF)
                ff1(n0, p, t0)
                ff2(n0 + 4, p, t0 + 4, 0, 24 * i + 12)
                ff1(n0 + 8, p, t0 + 12)
                ff2(n0 + 12, p, t0 + 16, 1, 24 * i + 24)
            n0, t0, p = SLAB_FF + 52, UNIT_FF_TAIL, par(SLAB_FF)
            ff1(n0, p, t0)
            ff2(n0 + 4, p, t0 + 4, 0, 84)
            ff2(n0 + 8, p, t0 + 12, 1, 96, 4)

            def f_mean(g):
                for k in range(KD):
                    i = g * KD + k
                    pe.wait_ge(s_f_squared, i + 1)
                    pe.matmul((b_I, b_U, b_S)[g][:, 0:G], ones[:, :], (rl, sqv)[i // 3 % 2][:, i % 3, :], start=k == 0, stop=k == 7)\
                        .then_inc(s_f_ssq, 1)

            for i, (j, g) in enumerate(f_last):
                if g == 0 and j % 2 == 0:
                    pe.wait_ge(s_slab_split, n0 + 8 + j // 2 + 1)
                ff2_group(p, t0 + 12, 1, j, g, (None, 1, 0, 1)[j - 4])
                if i in (7, 9):
                    f_mean((i - 7) // 2)
            f_mean(2)

        @block.scalar
        def _(act):
            def take(g, t, out, func=ACT.Copy, scale=1.0, second=False):
                act.wait_ge(s_group_ready[g], t + 1)
                act.activation(out, bank[g + 3 * second][:, 0:G], func, scale=scale).then_inc(s_group_free[g], 1)

            act.wait_ge(s_consts, 5)

            def x_squares(g, ks):
                act.wait_ge(s_x_loaded[g], 16)
                for k in ks:
                    i = g * KD + k
                    if i >= 6:
                        act.wait_ge(s_x_sq_used, i - 5)
                    act.activation(sq_ring(i % 6), x_in[:, k, tok[g]], ACT.Square).then_inc(s_x_sq, 1)

            def x_std(g):
                act.wait_ge(s_x_sq_used, KD * (g + 1))
                act.activation(rstd0b[:, tok[g]], (b_S, b_W, b_N)[g][:, 0:G], ACT.Sqrt, scale=1.0 / D, bias=eps[:, 0:1]).then_inc(s_x_std, 1)

            def x_hi(g):
                for k in range(KD):
                    act.wait_ge(s_x_h, g * KD + k + 1)
                    act.activation(h_hi[:, k, tok[g]], x_in[:, k, tok[g]], ACT.Copy).then_inc(s_x_hi, 1)

            x_squares(0, range(KD))
            act.wait_ge(s_mem_loaded, 16)
            act.activation(mem_sq[:, :, :], mem_in[:, :, :], ACT.Square).then_inc(s_mem_sq, 1)
            x_squares(1, range(4))
            x_std(0)
            act.wait_ge(s_mem_ssq, 1)
            act.activation(mem_std[:, 0, :], b_U[:, 0:MEM], ACT.Sqrt, scale=1.0 / D, bias=eps[:, 0:1]).then_inc(s_mem_std, 1)
            x_squares(1, range(4, KD))
            x_hi(0)
            x_squares(2, range(4))
            x_std(1)
            x_squares(2, range(4, KD))
            x_std(2)
            act.wait_ge(s_mem_h, 1)
            act.activation(m_hi[:, :, :], mem_in[:, :, :], ACT.Copy).then_inc(s_mem_hi, 1)
            x_hi(1)
            x_hi(2)

            def slab_hi(n):
                act.wait_ge(s_slab_loaded[n % 2], 16 * (n // 2 + 1))
                if n == 2:
                    act.wait_ge(s_group_ready[2], 1)
                else:
                    act.wait_ge(s_mem_ready, n - 2)
                act.activation(w_hi[:, n % 2, :], w_raw[:, n % 2, :], ACT.Copy).then_inc(s_hi_made, 1)

            def mem_taken(n):
                act.wait_ge(s_mem_ready, n + 1)
                act.activation(kvT[:, n, :], (b_I, b_U)[n % 2][:, 0:MEM], ACT.Copy).then_inc(s_mem_taken, 1)

            act.wait_ge(s_mem_lo, 1)
            slab_hi(2)
            slab_hi(3)
            mem_taken(0)
            act.wait_ge(s_gate_row, 1)
            act.activation(lf[:, :], tg[:, :], ACT.Exp, scale=-1.0).then_inc(s_gate_act, 1)
            act.wait_ge(s_gate_act, 1)
            act.activation(tg[:, :], lf[:, :], ACT.Ln, bias=ones[0:4, 0:1]).then_inc(s_gate_act, 1)
            for n in range(1, 5):
                mem_taken(n)
                slab_hi(n + 3)
            act.wait_ge(s_gate_row, 2)
            act.activation(R[32:36, :], tg[:, :], ACT.Exp)
            act.activation(R[64:68, :], lf[:, :], ACT.Exp)
            act.activation(R[96:100, :], mm_[:, :], ACT.Exp, scale=-1.0).then_inc(s_gate_act, 1)
            mem_taken(5)
            slab_hi(8)
            for n in (6, 7):
                mem_taken(n)
            act.wait_ge(s_mem_taken, 8)
            act.dma_start(o_kv, kvT[:, :, :]).then_inc(s_kv_stored, 16)
            for m in range(2):
                act.wait_ge(s_memv_t, m + 1)
                act.activation(v_tok[:, m, :], (b_I, b_U)[m][:, :], ACT.Copy).then_inc(s_memv_taken, 1)
            act.wait_ge(s_memv_taken, 2)
            act.dma_start(d_v, v_tok).then_inc(s_spilled, 16)
            act.wait_ge(s_kv_stored, 16)

            with act.Fori(0, HEADS) as h:
                t0 = UNIT_HEAD + UNITS_PER_HEAD * h
                def block_of(dst, k, t, scale=1.0):
                    for g in (0, 2):
                        take(g, t, dst[:, k, tok[g]], scale=scale)
                block_of(o_h, 0, t0)
                block_of(o_h, 1, t0 + 1)
                block_of(q_h, 0, t0 + 2)
                for r in range(4):
                    act.wait_ge(s_vT_ready, 4 * h + r + 1)
                    act.activation(v_all[:, 2 * r:2 * r + 2, 0:256],
                                   (b_S, b_W, b_N, b_I)[r][:, :].rearrange("p (c n) -> p c n", c=2), ACT.Copy)\
                       .then_inc(s_vT_taken, 1)
                block_of(q_h, 1, t0 + 3)
                block_of(k_h, 0, t0 + 4, K_SCALE)
                block_of(k_h, 1, t0 + 5, K_SCALE)
                act.wait_ge(s_wv_ready, h + 1)
                for g in range(NG):
                    take(g, t0 + 6, o_h[:, 0, tok[g]], ACT.Sigmoid)
                for r in range(4):
                    act.wait_ge(s_kT_ready, 4 * h + r + 1)
                    act.activation(kw_all[:, 2 * r:2 * r + 2, :],
                                   (b_S, b_W, b_N, b_I)[r][:, :].rearrange("p (c n) -> p c n", c=2), ACT.Copy)\
                       .then_inc(s_kT_taken, 1)
                act.wait_ge(s_dqk_taken, h + 1)
                act.dma_start(d_qk[bass.ds(h, 1)].rearrange("a b n -> (a b) n"), qkd[:, :]).then_inc(s_dqk_stored, 16)
                for g in range(NG):
                    take(g, t0 + 7, o_h[:, 1, tok[g]], ACT.Sigmoid)
                with act.Fori(0, NC) as c:
                    i1 = NC * h + c + 1
                    t = t0 + 8 + c
                    act.wait_ge(s_logw_ready, i1)
                    act.activation(SW[:, :], b_W[:, 0:L], ACT.Exp, bias=col[:, B_:B_ + 1]).then_inc(s_weights_ready, 1)
                    act.wait_ge(s_spilled, 16 * i1)
                    take(0, t, side_t[:, tok[0]])
                    act.wait_ge(s_carried_ready, i1)
                    act.activation(num[:, :], b_I[:, 0:257], ACT.Copy, scale=col[:, WI_:WI_ + 1]).then_inc(s_carried_scaled, 1)
                    take(1, t, side_t[:, tok[1]])
                    take(2, t, side_t[:, tok[2]])
                    act.wait_ge(s_group_free[2], t + 1)
                    act.dma_start(d_side[bass.ds(NC * h + c, 1)].rearrange("a p n -> (a p) n"), side_t[:, :])\
                       .then_inc(s_spilled, 16)
                act.wait_ge(s_C_new, NC * (h + 1))
                act.dma_start(o_C[bass.ds(h, 1)].rearrange("a p k c -> (a p) k c"), Cn[:, :, :]).then_inc(s_C_stored, 16)
            act.dma_start(o_n_s, ns[:, :]).then_inc(s_n_stored, 16)
            act.dma_start(o_m, m_out[:, :]).then_inc(s_n_stored, 16)
            act.wait_ge(s_u_loaded, 64)
            act.dma_start(o_pool, u_pad[:, :, 16 + T - 15:16 + T]).then_inc(s_pool_stored, 16)
            def pool_hi(w):
                for g in range(NG):
                    act.wait_ge(s_group_ready[g], UNIT_POOL + w + 1)
                    act.activation(yp_hi[:, w, tok[g]], bank[g][:, 0:G], ACT.Copy, scale=vec[:, V_POOL + w:V_POOL + w + 1])\
                       .then_inc(s_pool_hi, 1)

            for w in range(3):
                pool_hi(w)
            act.wait_ge(s_xbias_ready, 1)
            act.activation(dec_exp[:, :], b_U[0:32, 0:MEM], ACT.Exp, bias=sm[0:32, 9:10], scale=X_SCALE,
                           accum_out=sm[0:32, 10:11]).then_inc(s_dexp_ready, 1)
            pool_hi(3)
            act.wait_ge(s_pool_state_ready, 1)
            act.dma_start(o_pool_s, win_a[:, 0:480]).then_inc(s_pool_stored, 16)
            act.wait_ge(s_pool_stored, 32)
            with act.Fori(0, NC) as c:
                act.wait_ge(s_xbias_ready, c + 2)
                for hh in range(4):
                    act.activation(P_sb[:, hh, :], (b_S, b_W)[hh // 2][:, (hh % 2) * MEM:(hh % 2 + 1) * MEM], ACT.Exp,
                                   bias=sm[:, 4 + hh:5 + hh], scale=X_SCALE, accum_out=sm[:, 8 + hh:9 + hh]).then_inc(s_xexp_ready, 1)
                for g in range(NG):
                    act.wait_ge(s_g_loaded[g], 16 * (c + 1))
                    act.activation(gates[:, g, 0:2, :], gates[:, g, 0:2, :], ACT.Sigmoid).then_inc(s_g_sig, 1)
                for q, b in enumerate((b_N, b_I)):
                    act.wait_ge(s_xprobT_ready, 2 * c + 1 + q)
                    act.activation(PT_sb[:, 4 * q:4 * q + 4, :], b[:, :].rearrange("p (i t) -> p i t", i=4), ACT.Copy)\
                       .then_inc(s_xprobT_taken, 1)
                act.wait_ge(s_xo_ready, c + 1)
                act.activation(yx_hi[:, :, bass.ds(L * c, L)], b_U[:, :].rearrange("p (h t) -> p h t", h=4), ACT.Copy)\
                   .then_inc(s_xo_hi, 1)
            act.wait_ge(s_dvalues_taken, ND)
            act.activation(yx_hi[:, :, T:N], dec_out[:, :, :], ACT.Copy).then_inc(s_dattn_hi, 1)
            with act.Fori(0, 4) as i:
                for e in range(2):
                    j = 2 * i + e
                    act.wait_ge(s_xg_loaded[e], 16 * (i + 1))
                    act.activation(gates[:, :, (2, 0)[e], :], gates[:, :, (2, 0)[e], :], ACT.Sigmoid).then_inc(s_xg_sig, 1)
                    for g in range(NG):
                        act.wait_ge(s_merged, NG * j + g + 1)
                        act.activation(h_hi[:, bass.ds(j, 1), tok[g]].rearrange("p a t -> p (a t)"),
                                       acc[:, bass.ds(j, 1), tok[g]].rearrange("p a t -> p (a t)"), ACT.Copy).then_inc(s_merged_hi, 1)
            def z_block(j, g, added):
                act.wait_ge(s_group_ready[g], UNIT_OUT + j + 1)
                z = bank[g + (3 if isinstance(j, int) and j == 7 else 0)][:, 0:G]
                act.activation(acc[:, bass.ds(j, 1), tok[g]].rearrange("p a t -> p (a t)"), z, ACT.Copy)
                act.wait_ge(s_z_acc, added)
                act.activation(gates[:, g, 0, :], z, ACT.Square).then_inc(s_group_free[g], 1)

            def root(dst, src, summed, count, made):
                act.wait_ge(summed, count)
                act.activation(dst, src, ACT.Sqrt, scale=1.0 / D, bias=eps[:, 0:1]).then_inc(made, 1)

            def z_root(g):
                root(rstd0b[:, tok[g]], (b_I, b_U, b_S)[g][:, 0:G], s_z_ssq, g + 1, s_z_std)

            with act.Fori(0, 6) as j:
                for g in range(NG):
                    z_block(j, g, NG * j + g + 1)
            for i, (j, g) in enumerate(z_last):
                z_block(j, g, 19 + g if j == 6 else 22 + z_last.index((6, g)))
                if i in (3, 4):
                    z_root(i - 3)
            z_root(2)
            for j in range(2):
                n = SLAB_FF + j
                act.wait_ge(s_slab_loaded[n % 2], 16 * (n // 2 + 1))
                act.wait_ge(s_group_ready[2], UNIT_OUT + 7 + j)
                act.activation(w_hi[:, n % 2, :], w_raw[:, n % 2, :], ACT.Copy).then_inc(s_hi_made, 1)

            def x1_root(g):
                root(rstd0b[:, tok[g]], (b_W, b_N, b_I)[g][:, 0:G], s_x1_ssq, KD * (g + 1), s_x1_std)

            def h2_hi(g):
                for k in range(KD):
                    act.wait_ge(s_h2_ready, g * KD + k + 1)
                    act.activation(h_hi[:, k, tok[g]], acc[:, k, tok[g]], ACT.Copy).then_inc(s_h2_hi, 1)

            for g in range(NG):
                if g == 2:
                    x1_root(1)
                    h2_hi(0)
                for k in range(KD):
                    i = g * KD + k
                    act.wait_ge(s_x1_ready, i + 1)
                    if i >= 6:
                        act.wait_ge(s_x1_ssq, i - 5)
                    act.activation(sq_ring(i % 6), x_in[:, k, tok[g]], ACT.Square).then_inc(s_x1_sq, 1)
                    if g == 1 and k == 3:
                        x1_root(0)
            act.dma_start(d_x1, x_in[:, :, :]).then_inc(s_x1_stored, 16)
            h2_hi(1)
            x1_root(2)
            h2_hi(2)
            act.wait_ge(s_x1_stored, 16)

            def ff1(t, half, count, order):
                for i, (j, g) in enumerate(order):
                    take(g, t + j, rl[:, g, :], ACT.Relu, second=order is first_blocks and j == 1)
                    act.wait_ge(s_relu_squared, count + i + 1)
                    act.activation(f_hi[:, half, j, tok[g]], sqv[:, g, :], ACT.Copy).then_inc(s_f_hi, 1)

            ff1(UNIT_FF, 0, 0, first_blocks)
            with act.Fori(0, 3) as i:
                t0 = UNIT_FF_LOOP + UNITS_PER_FF_STEP * i
                ff1(t0, 1, 24 * i + 12, blocks)
                ff1(t0 + 12, 0, 24 * i + 24, blocks)
            ff1(UNIT_FF_TAIL, 1, 84, blocks)

            def f_root(g):
                root(rstd0b[:, tok[g]], (b_I, b_U, b_S)[g][:, 0:G], s_f_ssq, KD * (g + 1), s_f_std)

            act.wait_ge(s_f_lo, 96)
            for g in range(NG):
                for k in range(KD):
                    i = g * KD + k
                    act.wait_ge(s_group_free[g], UNIT_FF_TAIL + 12 + k + 1)
                    if i >= 6:
                        act.wait_ge(s_f_ssq, i - 5)
                    act.activation((rl, sqv)[i // 3 % 2][:, i % 3, :], acc[:, k, tok[g]], ACT.Square).then_inc(s_f_squared, 1)
                    if g and k == 3:
                        f_root(g - 1)
            f_root(2)
            for q, n in ((s_kv_stored, 16), (s_C_stored, 64), (s_n_stored, 32), (s_pool_stored, 32),
                         (s_spilled, 16 * (FILL + 1))):
                act.wait_ge(q, n)

        @block.vector
        def _(dve):
            chain = [0]

            def step(ins):
                chain[0] += 1
                ins.then_inc(s_dve_step, 1)
                dve.wait_ge(s_dve_step, chain[0])

            def stt(out, in0, scalar, in1, op0, op1):
                return dve.scalar_tensor_tensor(out=out, in0=in0, scalar=scalar, in1=in1, op0=op0, op1=op1)

            def vcol(c):
                return vec[:, c:c + 1]

            dve.wait_ge(s_const_loaded, 48)
            dve.wait_ge(s_masks, 4)
            for g in range(NG):
                dve.wait_ge(s_x_std, g + 1)
                step(dve.reciprocal(rstd0[:, tok[g]], rstd0b[:, tok[g]]))
                for k in range(KD):
                    stt(x_in[:, k, tok[g]], x_in[:, k, tok[g]], vcol(V_PRE + k), rstd0[:, tok[g]], ALU.mult, ALU.mult)\
                        .then_inc(s_x_h, 1)
                for k in range(KD // 2, KD):
                    dve.wait_ge(s_x_hi, g * KD + k + 1)
                    dve.tensor_tensor(h_lo[:, k, tok[g]], x_in[:, k, tok[g]], h_hi[:, k, tok[g]].bitcast(F32), ALU.subtract)\
                        .then_inc(s_x_lo, 1)
                if g == 0:
                    dve.wait_ge(s_mem_std, 1)
                    step(dve.reciprocal(mem_std[:, 1, :], mem_std[:, 0, :]))
                    for k in range(KD):
                        last = stt(mem_in[:, k, :], mem_in[:, k, :], vcol(V_MEM + k), mem_std[:, 1, :], ALU.mult, ALU.mult)
                    last.then_inc(s_mem_h, 1)

            for g in range(NG):
                dve.wait_ge(s_group_ready[g], 1)
                dve.tensor_scalar(gi[:, tok[g]], bank[g][0:4, 0:G], bif[:, 0:1], None, ALU.add)
                dve.tensor_scalar(gf[:, tok[g]], bank[g][32:36, 0:G], bif[:, 1:2], None, ALU.add).then_inc(s_group_free[g], 1)
            dve.wait_ge(s_group_free[2], 1)
            stt(tg[:, :], gf[:, :], -1.0, gf[:, :], ALU.mult, ALU.max).then_inc(s_gate_row, 1)
            dve.wait_ge(s_gate_act, 2)
            step(stt(lf[:, :], gf[:, :], 0.0, tg[:, :], ALU.min, ALU.subtract))
            dve.tensor_tensor_scan(mm_[:, 0:T], lf[:, 0:T], gi[:, 0:T], 0.0, ALU.add, ALU.max)
            dve.memset(gf[:, :], 1.0)
            step(dve.tensor_tensor(tg[:, T:N], lf[:, T:N], m0[:, :], ALU.add))
            dve.tensor_tensor(mm_[:, T:N], tg[:, T:N], gi[:, T:N], ALU.max)
            step(dve.memset(gf[:, 0:T].rearrange("p (c l) -> p c l", l=L)[:, :, 0:1], 0.0))
            dve.tensor_copy(bb[:, T:N], lf[:, T:N])
            step(dve.tensor_tensor_scan(bb[:, 0:T], gf[:, 0:T], lf[:, 0:T], 0.0, ALU.mult, ALU.add))
            dve.memset(mprev[:, 0:1], 0.0)
            dve.tensor_copy(mprev[:, 1:NC + 1], mm_[:, L - 1:T:L])
            dve.tensor_copy(m_out[:, :], mm_[:, T - 1:N])
            dve.tensor_tensor(A_row[:, :], bb[:, :], mm_[:, :], ALU.subtract)
            step(dve.tensor_tensor(R[0:4, :], gi[:, :], bb[:, :], ALU.subtract))

            def chunks(a):
                return a.rearrange("p (c l) -> p c l", l=L)
            dve.tensor_tensor(chunks(tg[:, 0:T]), chunks(A_row[:, 0:T]),
                              mprev[:, 0:NC].unsqueeze(2).to_broadcast([4, NC, L]), ALU.add)
            dve.tensor_tensor(tg[:, T:N], A_row[:, T:N], m0[:, :], ALU.add)
            dve.tensor_tensor(chunks(lf[:, 0:T]), chunks(R[0:4, 0:T]),
                              chunks(A_row[:, 0:T])[:, :, L - 1:L].to_broadcast([4, NC, L]), ALU.add)
            dve.tensor_tensor(lf[:, T:N], R[0:4, T:N], A_row[:, T:N], ALU.add).then_inc(s_gate_row, 1)
            dve.wait_ge(s_gate_act, 3)
            dve.tensor_copy(wsel[:, 0:NC], R[32:36, L - 1:T:L])
            dve.tensor_copy(wsel[:, NC:NC + ND], R[64:68, T:N])
            step(dve.tensor_copy(wsel[:, NC + ND:NC + 2 * ND], R[32:36, T:N]))
            dve.tensor_tensor(wi_diag[:, :, :], wsel[:, :].unsqueeze(2).to_broadcast([4, NC + 2 * ND, 4]),
                              ident[0:4, 0:4].unsqueeze(1).to_broadcast([4, NC + 2 * ND, 4]), ALU.mult)\
               .then_inc(s_rows_ready, 1)
            for i, b in enumerate((b_S, b_W, b_N)):
                dve.wait_ge(s_table_t, i + 1)
                if i == 2:
                    dve.wait_ge(s_bcast_ready, 1)
                v = b[:, :].rearrange("p (c q r) -> p c q r", c=4, q=4)
                if i < 2:
                    dve.tensor_copy(cols[:, 4 * i:4 * i + 4, :, :], v[:, :, :, 0:4])
                else:
                    dve.tensor_copy(cols[0:ND, NC:NC + 1, :, :], v[0:ND, 0:1, :, 0:4])
            dve.tensor_copy(decays[:, :, :], b_N[:, 256:288].rearrange("p (c h) -> p c h", h=4))
            dve.tensor_copy(dw[:, :, :, :], b_N[:, 288:352].rearrange("p (w b h) -> p w b h", w=2, h=4))
            dve.wait_ge(s_kv_stored, 16)
            step(dve.memset(v_all[:, :, 256:257], 1.0))

            with dve.Fori(0, HEADS) as h:
                t0 = UNIT_HEAD + UNITS_PER_HEAD * h
                h1 = h + 1

                def take1(dst, k, t, scale=1.0):
                    dve.wait_ge(s_group_ready[1], t + 1)
                    dve.tensor_scalar(dst[:, k, tok[1]], bank[1][:, 0:G], scale, None, ALU.mult).then_inc(s_group_free[1], 1)
                take1(o_h, 0, t0)
                take1(o_h, 1, t0 + 1)
                take1(q_h, 0, t0 + 2)
                dve.wait_ge(s_group_free[2], t0 + 2)
                dve.tensor_tensor(wv[:, :, :], o_h[:, :, T:N],
                                  dw[:, 0:1, :, bass.ds(h, 1)].rearrange("p w b h -> p (w h) b").to_broadcast([P, 2, ND]),
                                  ALU.mult).then_inc(s_wv_ready, 1)
                take1(q_h, 1, t0 + 3)
                take1(k_h, 0, t0 + 4, K_SCALE)
                take1(k_h, 1, t0 + 5, K_SCALE)
                dve.memset(Cn[:, :, :], 0.0)
                dve.tensor_copy(dcol[:, 0:4], cols[0:ND, NC, :, bass.ds(h, 1)].rearrange("p q h -> p (q h)"))
                dve.wait_ge(s_dqk_ready, h1)
                dve.tensor_copy(qkd[:, :], b_U[0:ND, :]).then_inc(s_dqk_taken, 1)
                n_h = ns[:, bass.ds(256 * h, 256)]
                dve.wait_ge(s_ns_loaded, 16)
                dve.wait_ge(s_dqk_taken, h1)
                dve.tensor_scalar(dtmp[0:ND, 0, :], qkd[:, 256:512], dcol[:, WE_:WE_ + 1], None, ALU.mult).then_inc(s_dnorm_step, 1)
                dve.wait_ge(s_dnorm_step, 6 * h + 1)
                stt(dtmp[0:ND, 1, :], n_h, dcol[:, WI_:WI_ + 1], dtmp[0:ND, 0, :], ALU.mult, ALU.add).then_inc(s_dnorm_step, 1)
                dve.wait_ge(s_dnorm_step, 6 * h + 2)
                dve.tensor_tensor_reduce(out=dtmp[0:ND, 0, :], in0=dtmp[0:ND, 1, :], in1=qkd[:, 0:256], scale=1.0, scalar=0.0,
                                         op0=ALU.mult, op1=ALU.add, accum_out=dcol[:, 4:5]).then_inc(s_dnorm_step, 1)
                dve.tensor_scalar(n_h, dtmp[0:ND, 1, :], 1.0, None, ALU.mult)
                dve.wait_ge(s_dnorm_step, 6 * h + 3)
                dve.tensor_scalar(dcol[:, 7:8], dcol[:, 4:5], dcol[:, EM_:EM_ + 1], None, ALU.max).then_inc(s_dnorm_step, 1)
                dve.wait_ge(s_dnorm_step, 6 * h + 4)
                stt(dcol[:, 5:6], dcol[:, 4:5], -1.0, dcol[:, 7:8], ALU.mult, ALU.max).then_inc(s_dnorm_step, 1)
                dve.wait_ge(s_dnorm_step, 6 * h + 5)
                dve.reciprocal(dcol[:, 6:7], dcol[:, 5:6]).then_inc(s_dnorm_step, 1)
                dve.wait_ge(s_kT_taken, 4 * h1)
                dve.wait_ge(s_group_free[2], t0 + 6)
                dve.wait_ge(s_dnorm_step, 6 * h + 6)
                dve.tensor_scalar(rdiag[:, :], ident[0:ND, 0:ND], dcol[:, 6:7], None, ALU.mult).then_inc(s_dinv_diag, 1)

                dve.wait_ge(s_spilled, 16)
                with dve.Fori(0, NC) as c:
                    i1 = NC * h + c + 1
                    cc = bass.ds(L * c, L)
                    dve.tensor_copy(col[:, 0:4], cols[:, bass.ds(c, 1), :, bass.ds(h, 1)].rearrange("p c q h -> p (c q h)"))
                    dve.tensor_copy(col[:, 4:5], decays[:, bass.ds(c, 1), bass.ds(h, 1)].rearrange("p c h -> p (c h)"))\
                       .then_inc(s_col_set, 1)
                    dve.tensor_scalar(A_pick[:, :], A_row[:, cc], ident[0:4, bass.ds(h, 1)], None, ALU.mult)
                    dve.tensor_copy(qs[:, :, :], q_h[:, :, cc])
                    dve.tensor_copy(ks[:, :, :], k_h[:, :, cc])
                    dve.wait_ge(s_col_set, i1)
                    dve.tensor_scalar(kw[:, :], kw_all[:, bass.ds(c, 1), :].rearrange("p c n -> p (c n)"),
                                      col[:, WE_:WE_ + 1], None, ALU.mult).then_inc(s_staged, 1)
                    dve.wait_ge(s_scores_ready, i1)
                    dve.wait_ge(s_weights_ready, i1)
                    dve.tensor_tensor(SW[:, :], b_S[:, 0:L], SW[:, :], ALU.mult).then_inc(s_weighted_ready, 1)
                    dve.wait_ge(s_dstate_loaded, 32 * i1)
                    for k in range(2):
                        last = dve.tensor_scalar(dtmp[:, k, :], qkb[:, 256:512],
                                                 wv[:, k, bass.ds(c, 1)], None, ALU.mult)
                    last.then_inc(s_dkv_ready, 1)
                    dve.wait_ge(s_dkv_ready, i1)
                    stt(dC[:, :, :], dC[:, :, :],
                        dw[:, 1:2, bass.ds(c, 1), bass.ds(h, 1)].rearrange("p w b h -> p (w b h)"),
                        dtmp[:, :, :], ALU.mult, ALU.add).then_inc(s_dstate_new, 1)
                    dve.wait_ge(s_dstate_new, i1)
                    for k in range(2):
                        last = dve.tensor_tensor_reduce(out=dtmp[:, k, :], in0=dC[:, k, :], in1=qkb[:, 0:256], scale=1.0,
                                                        scalar=0.0, op0=ALU.mult, op1=ALU.add,
                                                        accum_out=den[:, 2 + k:3 + k])
                    last.then_inc(s_dstate_used, 1)
                    dve.wait_ge(s_dstate_used, i1)
                    dve.tensor_scalar(num_d[:, :, bass.ds(c, 1)].rearrange("p k b -> p (k b)"), den[:, 2:4], 1.0, None, ALU.mult)
                    dve.wait_ge(s_update_ready, i1)
                    stt(Cn[:, :, 0:256], Cn[:, :, 0:256], col[:, 4:5], b_U[:, :].rearrange("p (k n) -> p k n", k=2),
                        ALU.mult, ALU.add)
                    stt(Cn[:, :, 256], Cn[:, :, 256], col[:, 4:5], b_N[:, 260:262], ALU.mult, ALU.add).then_inc(s_C_new, 1)
                    dve.wait_ge(s_carried_scaled, i1)
                    dve.tensor_tensor(num[:, :], num[:, :], b_N[:, 0:257], ALU.add).then_inc(s_num_ready, 1)
                    dve.wait_ge(s_num_ready, i1)
                    dve.tensor_scalar(den[:, 0:1], num[:, 256:257], col[:, EM_:EM_ + 1], None, ALU.max).then_inc(s_den_step, 1)
                    dve.wait_ge(s_den_step, 3 * i1 - 2)
                    stt(den[:, 0:1], num[:, 256:257], -1.0, den[:, 0:1], ALU.mult, ALU.max).then_inc(s_den_step, 1)
                    dve.wait_ge(s_den_step, 3 * i1 - 1)
                    dve.reciprocal(den[:, 1:2], den[:, 0:1]).then_inc(s_den_step, 1)
                    dve.wait_ge(s_den_step, 3 * i1)
                    dve.tensor_scalar(num[:, 0:256], num[:, 0:256], den[:, 1:2], None, ALU.mult).then_inc(s_hn_ready, 1)
                    dve.wait_ge(s_hT_ready, i1)
                    dve.tensor_tensor(dtmp[:, :, 0:L], b_S[:, P:P + 256].rearrange("p (k l) -> p k l", k=2), o_h[:, :, cc],
                                      ALU.mult).then_inc(s_yv_ready, 1)
                    dve.wait_ge(s_yv_ready, i1)
                    dve.tensor_scalar(y_hi[:, :, cc], dtmp[:, :, 0:L], 1.0, None, ALU.mult).then_inc(s_yhi_ready, 1)
                    dve.wait_ge(s_yhi_ready, i1)
                    dve.tensor_tensor(y_lo[:, :, cc], dtmp[:, :, 0:L], y_hi[:, :, cc].bitcast(F32), ALU.subtract)\
                       .then_inc(s_ylo_ready, 1)
                dve.tensor_tensor(yd[:, :, :], num_d[:, :, :], o_h[:, :, T:N], ALU.mult).then_inc(s_dy_gated, 1)
                dve.wait_ge(s_dy_gated, h1)
                dve.wait_ge(s_dinv_all, h1)
                for k in range(2):
                    last = dve.tensor_tensor(yd[:, k, :], yd[:, k, :], b_U[:, 0:ND], ALU.mult)
                last.then_inc(s_dy_scaled, 1)
                dve.wait_ge(s_dy_scaled, h1)
                dve.tensor_scalar(y_hi[:, :, T:N], yd[:, :, :], 1.0, None, ALU.mult).then_inc(s_dy_hi, 1)
                dve.wait_ge(s_dy_hi, h1)
                dve.tensor_tensor(y_lo[:, :, T:N], yd[:, :, :], y_hi[:, :, T:N].bitcast(F32), ALU.subtract)\
                   .then_inc(s_dy_ready, 1)
                dve.wait_ge(s_cleared, 1)
                for j in range(8):
                    for g in range(NG):
                        dve.wait_ge(s_group_ready[g], t0 + 17 + j)
                        dve.tensor_tensor(acc[:, j, tok[g]], acc[:, j, tok[g]], bank[g][:, 0:G], ALU.add)\
                           .then_inc(s_group_free[g], 1)
                dve.wait_ge(s_C_stored, 16 * h1)

            dve.memset(u_pad[:, :, 0:16], 0.0)
            for win in (win_a, win_b, win_c, win_d, win_e, win_f):
                last = dve.memset(win[:, 0:16], 0.0)
            last.then_inc(s_cleared, 1)
            dve.wait_ge(s_cleared, 2)
            for t in range(15):
                dve.memset(inv_count[:, t:t + 1], 1.0 / (t + 1))

            def pool_lo(w):
                for g in range(NG):
                    dve.wait_ge(s_pool_hi, NG * w + g + 1)
                    stt(yp_lo[:, w, tok[g]], bank[g][:, 0:G], vcol(V_POOL + w), yp_hi[:, w, tok[g]].bitcast(F32),
                        ALU.mult, ALU.subtract).then_inc(s_group_free[g], 1)

            dve.wait_ge(s_pool_in_loaded, 32)
            for w in range(4):
                win = 2 << w
                u = u_pad[:, w, :]
                dve.wait_ge(s_u_loaded, 64)
                src = u
                if w >= 2:
                    src = (win_c, win_f)[w - 2]
                    dve.wait_ge(s_window_step, (3, 7)[w - 2])
                for i in range(w + 1 if w < 2 else 0):
                    dst = (win_a, win_b)[i % 2]
                    step(dve.tensor_tensor(dst[:, 16:], src[:, 16:16 + N], src[:, 16 - (1 << i):16 + N - (1 << i)], ALU.add))
                    src = dst
                d = pool_d[:, w % 2, :]
                if w >= 2:
                    dve.wait_ge(s_group_ready[2], UNIT_POOL + w - 1)
                held = sm[:, ND * (w % 2):ND * (w % 2 + 1)]
                dve.tensor_reduce(held, bufT[:, w, :, 15 - (win - 1):15], axis=AX.X, op=ALU.add)
                step(stt(d, src[:, 16:], 1.0 / win, u[:, 16:], ALU.mult, ALU.subtract))
                dve.tensor_tensor(held, held, u[:, 16 + T:], ALU.add)
                step(dve.tensor_tensor(d[:, 0:win - 1], src[:, 16:16 + win - 1], inv_count[:, 0:win - 1], ALU.mult))
                dve.tensor_tensor(d[:, 0:win - 1], d[:, 0:win - 1], u[:, 16:16 + win - 1], ALU.subtract)
                stt(d[:, T:N], held, 1.0 / win, u[:, 16 + T:], ALU.mult, ALU.subtract).then_inc(s_pool_d_ready, 1)
                if w:
                    pool_lo(w - 1)
            po = win_a[:, 0:480].rearrange("p (k b j) -> p k b j", k=4, b=ND)
            for k in range(4):
                dve.tensor_copy(po[:, k, :, 0:14], bufT[:, k, :, 1:15])
            dve.tensor_copy(po[:, :, :, 14], u_pad[:, :, 16 + T:16 + N]).then_inc(s_pool_state_ready, 1)
            dve.wait_ge(s_dkeys_used, ND)
            dve.tensor_copy(dec_scores[:, :], b_N[:, 0:64]).then_inc(s_dscores_taken, 1)
            dve.wait_ge(s_dtransposed, 1)
            step(dve.tensor_reduce(sm[0:32, 8:9], b_U[0:32, 0:MEM], axis=AX.X, op=ALU.max))
            dve.tensor_scalar(sm[0:32, 9:10], sm[0:32, 8:9], -X_SCALE, None, ALU.mult).then_inc(s_xbias_ready, 1)
            dve.wait_ge(s_dexp_ready, 1)
            step(dve.reciprocal(sm[0:32, 11:12], sm[0:32, 10:11]))
            dve.tensor_scalar(dec_exp[:, :], dec_exp[:, :], sm[0:32, 11:12], None, ALU.mult).then_inc(s_dprob_ready, 1)
            pool_lo(3)
            dve.wait_ge(s_dtransposed, 2)
            dve.tensor_copy(dec_probs[:, :], b_N[:, 0:64]).then_inc(s_dprobT_taken, 1)
            with dve.Fori(0, NC) as c:
                cc = bass.ds(L * c, L)
                c1 = c + 1
                for i in range(2):
                    dve.wait_ge(s_xscores_ready, 2 * c + 1 + i)
                    last = dve.tensor_reduce(sm[:, 2 * i:2 * i + 2], (b_S, b_W)[i][:, :].rearrange("p (h m) -> p h m", h=2),
                                             axis=AX.X, op=ALU.max)
                last.then_inc(s_xstep, 1)
                dve.wait_ge(s_xstep, 2 * c + 1)
                dve.tensor_scalar(sm[:, 4:8], sm[:, 0:4], -X_SCALE, None, ALU.mult).then_inc(s_xbias_ready, 1)
                dve.wait_ge(s_xexp_ready, 4 * c1)
                dve.reciprocal(sm[:, 12:16], sm[:, 8:12]).then_inc(s_xstep, 1)
                dve.wait_ge(s_xstep, 2 * c + 2)
                for hh in range(4):
                    last = dve.tensor_scalar(P_sb[:, hh, :], P_sb[:, hh, :], sm[:, 12 + hh:13 + hh], None, ALU.mult)
                last.then_inc(s_xprob_ready, 1)

                def a(g):
                    return acc[:, bass.ds(c, 1), tok[g]].rearrange("p a t -> p (a t)")
                for g in range(NG):
                    dve.wait_ge(s_g_sig, NG * c + g + 1)
                    dve.tensor_tensor(a(g), a(g), gates[:, g, 1, :], ALU.mult).then_inc(s_acc_gated, 1)
                    dve.wait_ge(s_group_ready[g], UNIT_MERGE + c + 1)
                    dve.tensor_tensor(gates[:, g, 0, :], bank[g][:, 0:G], gates[:, g, 0, :], ALU.mult).then_inc(s_group_free[g], 1)
                dve.wait_ge(s_dvalues_used, c1)
                dve.tensor_scalar(dec_out[:, :, bass.ds(c, 1)].rearrange("p h b -> p (h b)"), b_S[:, 0:4], 1.0, None, ALU.mult)\
                   .then_inc(s_dvalues_taken, 1)
                for g in range(NG):
                    dve.wait_ge(s_acc_gated, NG * c + g + 1)
                    dve.wait_ge(s_group_free[g], UNIT_MERGE + c + 1)
                    dve.tensor_tensor(a(g), a(g), gates[:, g, 0, :], ALU.add).then_inc(s_pool_added, 1)
                dve.wait_ge(s_xo_hi, c1)
                dve.tensor_tensor(yx_lo[:, :, cc], b_U[:, :].rearrange("p (h t) -> p h t", h=4),
                                  yx_hi[:, :, cc].bitcast(F32), ALU.subtract).then_inc(s_xo_lo, 1)
            dve.wait_ge(s_dattn_hi, 1)
            dve.tensor_tensor(yx_lo[:, :, T:N], dec_out[:, :, :],
                              yx_hi[:, :, T:N].bitcast(F32), ALU.subtract).then_inc(s_dattn_lo, 1)
            def merged_lo(j, g):
                dve.wait_ge(s_merged_hi, NG * j + g + 1)
                at = [t[:, bass.ds(j, 1), tok[g]].rearrange("p a t -> p (a t)") for t in (h_lo, acc, h_hi)]
                dve.tensor_tensor(at[0], at[1], at[2].bitcast(F32), ALU.subtract).then_inc(s_merged_lo, 1)
            with dve.Fori(0, 4) as i:
                for e in range(2):
                    j = 2 * i + e
                    slot = (2, 0)[e]
                    dve.wait_ge(s_xg_sig, j + 1)

                    def a(g):
                        return acc[:, bass.ds(j, 1), tok[g]].rearrange("p a t -> p (a t)")
                    for g in range(NG):
                        dve.wait_ge(s_group_ready[g], UNIT_MERGE + 8 + j + 1)
                        dve.tensor_tensor(gates[:, g, slot, :], bank[g][:, 0:G], gates[:, g, slot, :], ALU.mult)\
                           .then_inc(s_group_free[g], 1)
                        dve.wait_ge(s_group_free[g], UNIT_MERGE + 8 + j + 1)
                        dve.tensor_tensor(a(g), a(g), gates[:, g, slot, :], ALU.add).then_inc(s_merged, 1)
                        if g:
                            merged_lo(j, g - 1)
                    merged_lo(j, NG - 1)
            dve.wait_ge(s_group_ready[2], UNIT_OUT)
            for g in range(NG):
                dve.memset(rstd0b[:, tok[g]], 0.0).then_inc(s_z_acc, 1)
            def z_add(j, g, added):
                dve.wait_ge(s_group_free[g], UNIT_OUT + j + 1)
                dve.wait_ge(s_z_acc, added)
                dve.tensor_tensor(rstd0b[:, tok[g]], rstd0b[:, tok[g]], gates[:, g, 0, :], ALU.add).then_inc(s_z_acc, 1)

            def z_scale(g, ks):
                for k in ks:
                    stt(acc[:, k, tok[g]], acc[:, k, tok[g]], vcol(V_POST + k), rstd0[:, tok[g]], ALU.mult, ALU.mult)\
                        .then_inc(s_z_scaled, 1)

            def z_inverse(g):
                dve.wait_ge(s_z_std, g + 1)
                step(dve.reciprocal(rstd0[:, tok[g]], rstd0b[:, tok[g]]))

            with dve.Fori(0, 6) as j:
                for g in range(NG):
                    z_add(j, g, NG * j + g + 1)
            for j, g in z_last[:4]:
                z_add(j, g, 19 + g if j == 6 else 22 + g)
            z_inverse(0)
            z_scale(0, range(4))
            z_add(6, 2, 21)
            z_scale(0, range(4, 6))
            z_add(7, 2, 26)
            z_scale(0, range(6, 8))
            for g in (1, 2):
                z_inverse(g)
                z_scale(g, range(KD))
            for g in range(NG):
                dve.wait_ge(s_x1_std, g + 1)
                step(dve.reciprocal(rstd0[:, tok[g]], rstd0b[:, tok[g]]))
                for k in range(KD):
                    stt(acc[:, k, tok[g]], x_in[:, k, tok[g]], vcol(V_MLP + k), rstd0[:, tok[g]], ALU.mult, ALU.mult)\
                        .then_inc(s_h2_ready, 1)
                for k in range(KD // 2, KD):
                    dve.wait_ge(s_h2_hi, g * KD + k + 1)
                    dve.tensor_tensor(h_lo[:, k, tok[g]], acc[:, k, tok[g]], h_hi[:, k, tok[g]].bitcast(F32), ALU.subtract)\
                        .then_inc(s_h2_lo, 1)

            def ff1(t, half, count, order):
                for i, (j, g) in enumerate(order):
                    dve.wait_ge(s_group_free[g], t + j + 1)
                    if order is first_blocks and i % 2:
                        dve.wait_ge(s_f_lo, i)
                    dve.tensor_tensor(sqv[:, g, :], rl[:, g, :], rl[:, g, :], ALU.mult).then_inc(s_relu_squared, 1)
                    dve.wait_ge(s_f_hi, count + i + 1)
                    dve.tensor_tensor(f_lo[:, half, j, tok[g]], sqv[:, g, :], f_hi[:, half, j, tok[g]].bitcast(F32),
                                      ALU.subtract).then_inc(s_f_lo, 1)

            def ff2(t, units=8):
                for j in range(units):
                    for g in range(NG):
                        ff2_add(t, j, g)

            def ff2_add(t, j, g, second=False):
                dve.wait_ge(s_group_ready[g], t + j + 1)
                dve.tensor_tensor(acc[:, j, tok[g]], acc[:, j, tok[g]], bank[g + 3 * second][:, 0:G], ALU.add).then_inc(s_group_free[g], 1)

            ff1(UNIT_FF, 0, 0, first_blocks)
            dve.wait_ge(s_cleared, 3)
            with dve.Fori(0, 3) as i:
                t0 = UNIT_FF_LOOP + UNITS_PER_FF_STEP * i
                ff1(t0, 1, 24 * i + 12, blocks)
                ff2(t0 + 4)
                ff1(t0 + 12, 0, 24 * i + 24, blocks)
                ff2(t0 + 16)
            ff1(UNIT_FF_TAIL, 1, 84, blocks)
            ff2(UNIT_FF_TAIL + 4)
            ff2(UNIT_FF_TAIL + 12, 4)
            for j, g in f_last[:8]:
                ff2_add(UNIT_FF_TAIL + 12, j, g, j % 2 == 1)

            def y_inverse(g):
                dve.wait_ge(s_f_std, g + 1)
                step(dve.reciprocal(rstd0[:, tok[g]], rstd0b[:, tok[g]]))

            def y_scale(g, ks):
                for k in ks:
                    stt(acc[:, k, tok[g]], acc[:, k, tok[g]], vcol(V_FF + k), rstd0[:, tok[g]], ALU.mult, ALU.mult)\
                        .then_inc(s_y_scaled, 1)

            def y_add(g):
                for k in range(5, KD):
                    dve.wait_ge(s_y_scaled, g * KD + k + 1)
                    dve.tensor_tensor(x1_back[:, k, tok[g]], x1_back[:, k, tok[g]], acc[:, k, tok[g]], ALU.add).then_inc(s_y_ready, 1)

            dve.wait_ge(s_x3_loaded, 16)
            y_inverse(0)
            ff2_add(UNIT_FF_TAIL + 12, 4, 2)
            y_scale(0, range(3))
            ff2_add(UNIT_FF_TAIL + 12, 5, 2, True)
            y_scale(0, range(3, KD))
            y_add(0)
            y_inverse(1)
            ff2_add(UNIT_FF_TAIL + 12, 6, 2)
            y_scale(1, range(2))
            ff2_add(UNIT_FF_TAIL + 12, 7, 2, True)
            y_scale(1, range(2, KD))
            y_add(1)
            y_inverse(2)
            y_scale(2, range(KD))
            y_add(2)


def lay_out(inputs):
    import numpy as np

    def feat(a):
        return a.T.reshape(KD, P, a.shape[0]).transpose(1, 0, 2)

    def slab(w):
        return w.reshape(-1, P, w.shape[1]).transpose(1, 0, 2).reshape(P, 1024)

    def vector(v):
        return v.reshape(-1, P).T

    x = np.concatenate([inputs["x_prompt"][0], inputs["x_sample"][:, 0]], axis=0)
    w_in = inputs["w_in"][0]
    q0, k0, v0, o0 = (512 + 1024 * i for i in range(4))
    gif = np.zeros((D, P), np.float32)
    gif[:, 0:4] = w_in[:, 4608:4612]
    gif[:, 32:36] = w_in[:, 4612:4616]
    slabs = [slab(gif)] + [slab(inputs["w_mem_kv"][0][:, P * j:P * (j + 1)]) for j in range(8)]
    side = [P * j for j in range(4)] + [4616 + P * j for j in range(4)]
    side += [5128 + 1024 * b + P * j for j in range(8) for b in range(3)]
    for h in range(HEADS):
        for c0 in (v0, q0, k0, o0):
            slabs += [slab(w_in[:, c0 + 256 * h + P * i:c0 + 256 * h + P * (i + 1)]) for i in range(2)]
        slabs += [slab(w_in[:, side[8 * h + c]:side[8 * h + c] + P]) for c in range(8)]
        slabs += [slab(inputs["w_br_mlstm"][0][256 * h:256 * (h + 1), 512 * i:512 * (i + 1)]) for i in range(2)]
    for name in ("w_br_pool", "w_br_xattn"):
        slabs += [slab(inputs[name][0][:, 256 * j:256 * (j + 1)]) for j in range(4)]
    slabs += [slab(inputs["w_out"][0][:, P * j:P * (j + 1)]) for j in range(8)]

    def ff1(c):
        return [slab(inputs["w_ff1"][0][:, 512 * c + P * j:512 * c + P * (j + 1)]) for j in range(4)]

    def ff2(c):
        return [slab(inputs["w_ff2"][0][512 * c:512 * (c + 1), 256 * j:256 * (j + 1)]) for j in range(4)]
    slabs += ff1(0)
    for c in range(7):
        slabs += ff1(c + 1) + ff2(c)
    slabs += ff2(7)
    return {
        "w_stream": np.stack(slabs),
        "xT": feat(x), "memT": feat(inputs["mem_prompt"][0]),
        "vecs": np.concatenate([vector(inputs[n][0]) for n in ("g_pre_mix", "g_mem", "g_post_mix", "g_pre_mlp",
                                                                "g_post_mlp", "pool_scale")], axis=1),
        "b_if": inputs["b_if"][0].reshape(2, 4).T,
        "w_pool": inputs["w_pool"][0].transpose(1, 0, 2),
        "poolbuf": inputs["state_pool_buf"][0].transpose(2, 0, 1).reshape(4, P, ND, 15).transpose(1, 0, 2, 3),
        "stC": inputs["state_mlstm_C"][0].reshape(ND, 4, 2, P, 256).transpose(1, 0, 3, 2, 4),
        "stn": inputs["state_mlstm_n"][0].reshape(ND, 1024),
        "stm": inputs["state_mlstm_m"][0].T,
        "ckT": inputs["cache_mem_k"][0].transpose(0, 3, 2, 1),
        "cv": inputs["cache_mem_v"][0].reshape(ND, 2, P, 512).transpose(0, 2, 1, 3),
    }


def kernel(**inputs):
    import numpy as np
    import concourse.bacc as bacc
    from concourse.bass_utils import run_bass_kernel_spmd

    nc = bacc.Bacc("TRN2", target_bir_lowering=False, num_devices=1)
    arrays, args = {}, []
    for name, a in lay_out({n: np.asarray(v) for n, v in inputs.items()}).items():
        arrays[name] = np.ascontiguousarray(a)
        args.append(nc.dram_tensor(name, a.shape, F32, kind="ExternalInput").ap())
    outs = {"o_y": (P, KD, N), "o_pool": (P, 4, 15), "o_C": (4, P, 2, 257), "o_m": (4, 1 + ND), "o_kv": (P, 8, MEM),
            "o_pool_s": (P, 480), "o_C_s": (4, ND, P, 2, 256), "o_n_s": (ND, 1024)}
    for name, shape in outs.items():
        args.append(nc.dram_tensor(name, shape, F32, kind="ExternalOutput").ap())
    for name, shape in (("d_side", (FILL, P, N)), ("d_x1", (P, KD, N)), ("d_qk", (4, ND, 512)), ("d_v", (P, 2, 512))):
        args.append(nc.dram_tensor(name, shape, F32, kind="Internal").ap())
    hybrid_layer(nc, *args)
    r = run_bass_kernel_spmd(nc, [arrays], core_ids=[0]).results[0]
    y = r["o_y"].transpose(1, 0, 2).reshape(D, N).T
    pool_p = r["o_pool"].transpose(2, 1, 0).reshape(1, 1, 15, 512)
    C_p = r["o_C"][:, :, :, 0:256].transpose(0, 3, 2, 1).reshape(1, 1, 4, 256, 256)
    n_p = r["o_C"][:, :, :, 256].transpose(0, 2, 1).reshape(1, 1, 4, 256)
    kv = r["o_kv"].transpose(1, 0, 2).reshape(1024, MEM).T
    pool_s = r["o_pool_s"].reshape(P, 4, ND, 15).transpose(2, 3, 1, 0).reshape(1, ND, 15, 512)
    C_s = r["o_C_s"].transpose(1, 0, 3, 2, 4).reshape(1, ND, 4, 256, 256)
    out = (y[0:T].reshape(1, T, D), y[T:].reshape(ND, 1, D), pool_p, C_p, n_p, r["o_m"][:, 0].reshape(1, 1, 4),
           kv[:, 0:512].reshape(1, 1, MEM, 4, P), kv[:, 512:].reshape(1, 1, MEM, 4, P),
           pool_s, C_s, r["o_n_s"].reshape(1, ND, 4, 256), r["o_m"][:, 1:].T.reshape(1, ND, 4))
    return tuple(np.ascontiguousarray(a) for a in out)
```
